# Optimizing a Trainium2 kernel written in Bass

```python
import jax, jax.numpy as jnp
from jax import lax
import numpy as np
import math
import jax
import jax.numpy as jnp

D_MODEL = 1024
BATCH = 1
SEQ = 256
DEPTH = 1

EPS = 1e-6
CONV_WIDTH = D_MODEL
CONV_K = 3
GDN_HEADS = 8
GDN_DK = 128
GDN_DV = 128
GDN_CONV_K = 4
GDN_CHUNK = 64
GDN_QK = GDN_HEADS * GDN_DK
GDN_VW = GDN_HEADS * GDN_DV
D_FF = 256 * ((8 * D_MODEL // 3 + 255) // 256)
FFN_CONV_K = 3
IN_SPLITS = (CONV_WIDTH, CONV_WIDTH, CONV_WIDTH, GDN_QK, GDN_QK, GDN_VW, GDN_VW, GDN_HEADS, GDN_HEADS, D_MODEL, D_MODEL)
IN_WIDTH = sum(IN_SPLITS)


def _split_points():
    pts, acc = [], 0
    for w in IN_SPLITS[:-1]:
        acc += w
        pts.append(acc)
    return pts

def rmsnorm(x, g):
    xf = x.astype(jnp.float32)
    y = xf * lax.rsqrt(jnp.mean(xf * xf, axis=-1, keepdims=True) + EPS)
    return (y * g.astype(jnp.float32)).astype(x.dtype)

def l2norm(x):
    return x * lax.rsqrt(jnp.sum(x * x, axis=-1, keepdims=True) + EPS)

def causal_dwconv(x, w):
    K = w.shape[0]
    S = x.shape[1]
    xp = jnp.pad(x, ((0, 0), (K - 1, 0), (0, 0)))
    return sum(xp[:, j:j + S] * w[j] for j in range(K))

def short_conv_branch(bg, cg, xv, conv_w):
    return bg * causal_dwconv(cg * xv, conv_w)

def gated_delta_rule_chunked(q, k, v, g, beta):
    Bsz, S, H, dk = q.shape
    dv = v.shape[-1]
    C = GDN_CHUNK
    N = S // C

    def chunks(t):
        return t.reshape(Bsz, N, C, H, *t.shape[3:]).swapaxes(2, 3)

    q, k, v, g, beta = (chunks(t) for t in (q, k, v, g, beta))
    G = jnp.cumsum(g, axis=-1)
    tril = jnp.tril(jnp.ones((C, C), dtype=bool))
    strict = jnp.tril(jnp.ones((C, C), dtype=bool), -1)
    decay = jnp.exp(jnp.where(tril, G[..., :, None] - G[..., None, :], -jnp.inf))
    k_beta = k * beta[..., None]
    v_beta = v * beta[..., None]
    L = jnp.where(strict, jnp.einsum('bnhid,bnhjd->bnhij', k_beta, k) * decay, 0.0)
    eye = jnp.eye(C, dtype=q.dtype)
    rhs = jnp.concatenate([v_beta, k_beta * jnp.exp(G)[..., None]], axis=-1)
    sol = lax.linalg.triangular_solve(eye + L, rhs, left_side=True, lower=True)
    u, w = sol[..., :dv], sol[..., dv:]
    A_qk = jnp.einsum('bnhid,bnhjd->bnhij', q, k) * decay
    q_dec = q * jnp.exp(G)[..., None]
    G_last = G[..., -1:]
    k_dec = k * jnp.exp(G_last - G)[..., None]

    def step(state, inp):
        q_c, k_c, u_c, w_c, A_c, gl = inp
        v_new = u_c - jnp.einsum('bhcd,bhde->bhce', w_c, state)
        o = jnp.einsum('bhcd,bhde->bhce', q_c, state) + jnp.einsum('bhij,bhje->bhie', A_c, v_new)
        state = state * jnp.exp(gl)[..., None] + jnp.einsum('bhcd,bhce->bhde', k_c, v_new)
        return state, o

    xs = tuple(jnp.moveaxis(t, 1, 0) for t in (q_dec, k_dec, u, w, A_qk, G_last))
    state0 = jnp.zeros((Bsz, H, dk, dv), dtype=q.dtype)
    _, o = lax.scan(step, state0, xs)
    return o.transpose(1, 0, 3, 2, 4).reshape(Bsz, S, H, dv)

def gdn_branch(q, k, v, z, a, b, conv_w, A_log, dt_bias, norm_g):
    Bsz, S, _ = q.shape
    dtype = q.dtype
    f32 = jnp.float32
    qkv = jax.nn.silu(causal_dwconv(jnp.concatenate([q, k, v], axis=-1), conv_w))
    q, k, v = jnp.split(qkv, [GDN_QK, 2 * GDN_QK], axis=-1)
    q = l2norm(q.reshape(Bsz, S, GDN_HEADS, GDN_DK).astype(f32)) * (GDN_DK ** -0.5)
    k = l2norm(k.reshape(Bsz, S, GDN_HEADS, GDN_DK).astype(f32))
    v = v.reshape(Bsz, S, GDN_HEADS, GDN_DV).astype(f32)
    beta = jax.nn.sigmoid(b.astype(f32))
    g = -jnp.exp(A_log.astype(f32)) * jax.nn.softplus(a.astype(f32) + dt_bias.astype(f32))
    o = gated_delta_rule_chunked(q, k, v, g, beta)
    o = o * lax.rsqrt(jnp.mean(o * o, axis=-1, keepdims=True) + EPS) * norm_g.astype(f32)
    o = o * jax.nn.silu(z.reshape(Bsz, S, GDN_HEADS, GDN_DV).astype(f32))
    return o.reshape(Bsz, S, GDN_VW).astype(dtype)

def conv_ffn(h, w_up, conv_w, w_down):
    up = causal_dwconv(h @ w_up, conv_w)
    gate, val = jnp.split(up, [D_FF], axis=-1)
    return (jax.nn.silu(gate) * val) @ w_down

def first_inputs(seed: int = 0) -> dict:
    key = jax.random.key(seed)
    ks = jax.random.split(key, 16)
    f32 = jnp.float32
    nrm = lambda k, shape, scale: jax.random.normal(k, shape, f32) * scale
    x = jax.random.normal(ks[0], (BATCH, SEQ, D_MODEL), f32)
    norm_mix_g = 1.0 + nrm(ks[1], (DEPTH, D_MODEL), 0.02)
    w_in = nrm(ks[2], (DEPTH, D_MODEL, IN_WIDTH), D_MODEL ** -0.5)
    conv_a_w = nrm(ks[3], (DEPTH, CONV_K, CONV_WIDTH), CONV_K ** -0.5)
    gdn_conv_w = nrm(ks[4], (DEPTH, GDN_CONV_K, 2 * GDN_QK + GDN_VW), GDN_CONV_K ** -0.5)
    gdn_A_log = jnp.log(jax.random.uniform(ks[5], (DEPTH, GDN_HEADS), f32, 1.0, 16.0))
    dt = jnp.exp(jax.random.uniform(ks[6], (DEPTH, GDN_HEADS), f32, np.log(1e-3), np.log(1e-1)))
    gdn_dt_bias = dt + jnp.log(-jnp.expm1(-dt))
    gdn_norm_g = 1.0 + nrm(ks[7], (DEPTH, GDN_DV), 0.02)
    w_a_out = nrm(ks[8], (DEPTH, CONV_WIDTH, D_MODEL), CONV_WIDTH ** -0.5)
    w_b_out = nrm(ks[9], (DEPTH, GDN_VW, D_MODEL), GDN_VW ** -0.5)
    w_o = nrm(ks[10], (DEPTH, D_MODEL, D_MODEL), D_MODEL ** -0.5)
    norm_ffn_g = 1.0 + nrm(ks[11], (DEPTH, D_MODEL), 0.02)
    w_up = nrm(ks[12], (DEPTH, D_MODEL, 2 * D_FF), D_MODEL ** -0.5)
    ffn_conv_w = nrm(ks[13], (DEPTH, FFN_CONV_K, 2 * D_FF), FFN_CONV_K ** -0.5)
    w_down = nrm(ks[14], (DEPTH, D_FF, D_MODEL), D_FF ** -0.5)
    norm_final_g = 1.0 + nrm(ks[15], (D_MODEL,), 0.02)
    return {"x": x, "norm_mix_g": norm_mix_g, "w_in": w_in, "conv_a_w": conv_a_w,
            "gdn_conv_w": gdn_conv_w, "gdn_A_log": gdn_A_log, "gdn_dt_bias": gdn_dt_bias,
            "gdn_norm_g": gdn_norm_g, "w_a_out": w_a_out, "w_b_out": w_b_out, "w_o": w_o,
            "norm_ffn_g": norm_ffn_g, "w_up": w_up, "ffn_conv_w": ffn_conv_w, "w_down": w_down,
            "norm_final_g": norm_final_g}

def first_block(x, norm_mix_g, w_in, conv_a_w, gdn_conv_w, gdn_A_log, gdn_dt_bias, gdn_norm_g,
              w_a_out, w_b_out, w_o, norm_ffn_g, w_up, ffn_conv_w, w_down, norm_final_g):
    pts = _split_points()
    for l in range(DEPTH):
        h = rmsnorm(x, norm_mix_g[l])
        proj = h @ w_in[l]
        bg, cg, xv, q, k, v, z, a, b, ga, gb = jnp.split(proj, pts, axis=-1)
        y_a = short_conv_branch(bg, cg, xv, conv_a_w[l]) @ w_a_out[l]
        y_b = gdn_branch(q, k, v, z, a, b, gdn_conv_w[l], gdn_A_log[l], gdn_dt_bias[l],
                         gdn_norm_g[l]) @ w_b_out[l]
        mix = jax.nn.sigmoid(ga) * y_a + jax.nn.sigmoid(gb) * y_b
        x = x + mix @ w_o[l]
        h = rmsnorm(x, norm_ffn_g[l])
        x = x + conv_ffn(h, w_up[l], ffn_conv_w[l], w_down[l])
    return rmsnorm(x, norm_final_g)


N_HEADS_A = 8
HEAD_DIM_A = 64
ROPE_DIM_A = HEAD_DIM_A // 4
NOPE_DIM_A = HEAD_DIM_A - ROPE_DIM_A
KV_RANK = 128
IDX_HEADS = 8
IDX_DIM = 32
IDX_ROPE_DIM = IDX_DIM // 4
TOPK_MAX = 256
N_HEADS_B = 8
HEAD_DIM_B = 64
WIDTH_A = N_HEADS_A * HEAD_DIM_A
WIDTH_B = N_HEADS_B * HEAD_DIM_B
MIX_WIDTH = WIDTH_A + WIDTH_B
Q_BLOCK = 128
ROPE_THETA = 500000.0
PEER_HEADS = 8
N_KEYS = 128
N_EXPERTS = N_KEYS * N_KEYS
PEER_KEY_DIM = 128
PEER_TOPK = 16
PEER_CHUNK = 128
IN_SIZES = (WIDTH_A, KV_RANK, ROPE_DIM_A, IDX_HEADS * IDX_DIM, IDX_DIM, IDX_HEADS,
            WIDTH_B, WIDTH_B, WIDTH_B, N_HEADS_B)
IN_COLS = sum(IN_SIZES)


def rms_norm(x, g):
    xf = x.astype(jnp.float32)
    y = xf * lax.rsqrt(jnp.mean(xf * xf, axis=-1, keepdims=True) + EPS)
    return (y * g.astype(jnp.float32)).astype(x.dtype)

def rope_tables(pos, rot_dim):
    inv = ROPE_THETA ** (-jnp.arange(0, rot_dim, 2, dtype=jnp.float32) / rot_dim)
    ang = pos.astype(jnp.float32)[..., None] * inv
    return jnp.cos(ang), jnp.sin(ang)

def apply_partial_rope(x, cos, sin):
    half = cos.shape[-1]
    cos = cos.astype(x.dtype)
    sin = sin.astype(x.dtype)
    x1 = x[..., :half]
    x2 = x[..., half:2 * half]
    return jnp.concatenate([x1 * cos - x2 * sin, x2 * cos + x1 * sin, x[..., 2 * half:]], axis=-1)

def to_blocks(a):
    b, s = a.shape[:2]
    return a.reshape(b, s // Q_BLOCK, Q_BLOCK, *a.shape[2:]).swapaxes(0, 1)

def from_blocks(a):
    nb, b, q = a.shape[:3]
    return a.swapaxes(0, 1).reshape(b, nb * q, *a.shape[3:])

def dsa_attention(q, latent, k_rope, iq, ik, iw, cos_a, sin_a, cos_i, sin_i, w_uk, w_uv):
    b, s = q.shape[:2]
    topk = min(TOPK_MAX, s // 4)
    q = apply_partial_rope(q, cos_a[:, :, None], sin_a[:, :, None])
    q_rope, q_nope = q[..., :ROPE_DIM_A], q[..., ROPE_DIM_A:]
    k_rope = apply_partial_rope(k_rope, cos_a, sin_a)
    q_lat = jnp.einsum('bshn,rhn->bshr', q_nope, w_uk)
    iq = apply_partial_rope(iq, cos_i[:, :, None], sin_i[:, :, None])
    ik = apply_partial_rope(ik, cos_i, sin_i)
    key_pos = jnp.arange(s)
    t_blocks = key_pos.reshape(s // Q_BLOCK, Q_BLOCK)
    gather_rows = jax.vmap(lambda table, ids: table[ids])
    scale = HEAD_DIM_A ** -0.5

    def block(args):
        q_lat_b, q_rope_b, iq_b, iw_b, t_b = args
        dots = jnp.einsum('bqhd,bsd->bqhs', iq_b, ik,
                          preferred_element_type=jnp.float32) * (IDX_DIM ** -0.5)
        w_h = iw_b.astype(jnp.float32) * (IDX_HEADS ** -0.5)
        score = jnp.einsum('bqhs,bqh->bqs', jax.nn.relu(dots), w_h)
        causal = key_pos[None, :] <= t_b[:, None]
        score = jnp.where(causal[None], score, -jnp.inf)
        _, sel = lax.top_k(score, topk)
        valid = sel <= t_b[None, :, None]
        lat_s = gather_rows(latent, sel)
        kr_s = gather_rows(k_rope, sel)
        logits = (jnp.einsum('bqhr,bqkr->bqhk', q_lat_b, lat_s, preferred_element_type=jnp.float32)
                  + jnp.einsum('bqhd,bqkd->bqhk', q_rope_b, kr_s, preferred_element_type=jnp.float32)) * scale
        logits = jnp.where(valid[:, :, None, :], logits, -jnp.inf)
        p = jax.nn.softmax(logits, axis=-1).astype(lat_s.dtype)
        return jnp.einsum('bqhk,bqkr->bqhr', p, lat_s)

    o = lax.map(block, (to_blocks(q_lat), to_blocks(q_rope), to_blocks(iq), to_blocks(iw), t_blocks))
    o = from_blocks(o)
    return jnp.einsum('bshr,rhd->bshd', o, w_uv).reshape(b, s, WIDTH_A)

def forgetting_attention(q, k, v, f_logit):
    b, s = q.shape[:2]
    cum = jnp.cumsum(jax.nn.log_sigmoid(f_logit.astype(jnp.float32)), axis=1)
    cum_k = cum.transpose(0, 2, 1)
    key_pos = jnp.arange(s)
    t_blocks = key_pos.reshape(s // Q_BLOCK, Q_BLOCK)
    scale = HEAD_DIM_B ** -0.5

    def block(args):
        q_b, cum_b, t_b = args
        logits = jnp.einsum('bqhd,bshd->bhqs', q_b, k, preferred_element_type=jnp.float32) * scale
        logits = logits + cum_b.transpose(0, 2, 1)[..., None] - cum_k[:, :, None, :]
        causal = key_pos[None, :] <= t_b[:, None]
        logits = jnp.where(causal, logits, -jnp.inf)
        p = jax.nn.softmax(logits, axis=-1).astype(v.dtype)
        return jnp.einsum('bhqs,bshd->bqhd', p, v)

    o = from_blocks(lax.map(block, (to_blocks(q), to_blocks(cum), t_blocks)))
    return o.reshape(b, s, WIDTH_B)

def peer_ffn(h, w_q, keys1, keys2, u, v):
    b, s, d = h.shape
    half = PEER_KEY_DIM // 2
    k1 = keys1.astype(jnp.float32)
    k2 = keys2.astype(jnp.float32)

    def chunk(hc):
        q = (hc @ w_q).reshape(-1, PEER_HEADS, PEER_KEY_DIM).astype(jnp.float32)
        s1 = jnp.einsum('chd,nd->chn', q[..., :half], k1)
        s2 = jnp.einsum('chd,nd->chn', q[..., half:], k2)
        v1, i1 = lax.top_k(s1, PEER_TOPK)
        v2, i2 = lax.top_k(s2, PEER_TOPK)
        cand_s = (v1[..., :, None] + v2[..., None, :]).reshape(*v1.shape[:-1], PEER_TOPK * PEER_TOPK)
        cand_i = (i1[..., :, None] * N_KEYS + i2[..., None, :]).reshape(*i1.shape[:-1], PEER_TOPK * PEER_TOPK)
        best_s, best_pos = lax.top_k(cand_s, PEER_TOPK)
        expert = jnp.take_along_axis(cand_i, best_pos, axis=-1)
        g = jax.nn.softmax(best_s, axis=-1)
        act = jax.nn.gelu(jnp.einsum('cd,chkd->chk', hc, u[expert],
                                     preferred_element_type=jnp.float32), approximate=False)
        wgt = (g * act).astype(hc.dtype)
        return jnp.einsum('chk,chkd->cd', wgt, v[expert])

    out = lax.map(chunk, h.reshape(-1, PEER_CHUNK, d))
    return out.reshape(b, s, d)

def second_inputs(seed: int = 0) -> dict:
    key = jax.random.key(seed)
    ks = jax.random.split(key, 21)
    f32 = jnp.float32
    L, D = DEPTH, D_MODEL

    def nrm(k, shape, sc):
        return jax.random.normal(k, shape, f32) * sc

    def gain(k, shape):
        return 1.0 + 0.05 * jax.random.normal(k, shape, f32)

    x = nrm(ks[0], (BATCH, SEQ, D), 1.0)
    c = nrm(ks[1], (BATCH, D), 1.0)
    positions = (jnp.arange(SEQ, dtype=jnp.int32)[None, :]
                 + jax.random.randint(ks[2], (BATCH, 1), 0, 1024, dtype=jnp.int32))
    w_ada = nrm(ks[3], (L, D, 6 * D), 0.2 * D ** -0.5)
    b_ada = nrm(ks[4], (L, 6 * D), 0.1)
    g_mix = gain(ks[5], (L, D))
    w_in = nrm(ks[6], (L, D, IN_COLS), D ** -0.5)
    g_kv = gain(ks[7], (L, KV_RANK))
    w_uk = nrm(ks[8], (L, KV_RANK, N_HEADS_A, NOPE_DIM_A), KV_RANK ** -0.5)
    w_uv = nrm(ks[9], (L, KV_RANK, N_HEADS_A, HEAD_DIM_A), KV_RANK ** -0.5)
    b_forget = jax.random.uniform(ks[10], (L, N_HEADS_B), f32, 2.0, 6.0)
    g_out_a = gain(ks[11], (L, WIDTH_A))
    g_out_b = gain(ks[12], (L, WIDTH_B))
    w_out = nrm(ks[13], (L, MIX_WIDTH, D), MIX_WIDTH ** -0.5)
    g_ffn = gain(ks[14], (L, D))
    w_peer_q = nrm(ks[15], (L, D, PEER_HEADS * PEER_KEY_DIM), D ** -0.5)
    peer_keys1 = nrm(ks[16], (L, N_KEYS, PEER_KEY_DIM // 2), (PEER_KEY_DIM // 2) ** -0.5)
    peer_keys2 = nrm(ks[17], (L, N_KEYS, PEER_KEY_DIM // 2), (PEER_KEY_DIM // 2) ** -0.5)
    peer_u = nrm(ks[18], (L, N_EXPERTS, D), D ** -0.5)
    peer_v = nrm(ks[19], (L, N_EXPERTS, D), 0.5)
    g_final = gain(ks[20], (D,))
    return {'x': x, 'c': c, 'positions': positions, 'w_ada': w_ada, 'b_ada': b_ada,
            'g_mix': g_mix, 'w_in': w_in, 'g_kv': g_kv, 'w_uk': w_uk, 'w_uv': w_uv,
            'b_forget': b_forget, 'g_out_a': g_out_a, 'g_out_b': g_out_b, 'w_out': w_out,
            'g_ffn': g_ffn, 'w_peer_q': w_peer_q, 'peer_keys1': peer_keys1,
            'peer_keys2': peer_keys2, 'peer_u': peer_u, 'peer_v': peer_v, 'g_final': g_final}

def second_block(x, c, positions, w_ada, b_ada, g_mix, w_in, g_kv, w_uk, w_uv, b_forget,
              g_out_a, g_out_b, w_out, g_ffn, w_peer_q, peer_keys1, peer_keys2, peer_u,
              peer_v, g_final):
    b, s, d = x.shape
    cos_a, sin_a = rope_tables(positions, ROPE_DIM_A)
    cos_i, sin_i = rope_tables(positions, IDX_ROPE_DIM)
    c_act = jax.nn.silu(c)
    split_at = []
    acc = 0
    for n in IN_SIZES[:-1]:
        acc += n
        split_at.append(acc)
    for l in range(DEPTH):
        mod = (c_act @ w_ada[l] + b_ada[l])[:, None, :]
        shift1, scale1, gate1, shift2, scale2, gate2 = jnp.split(mod, 6, axis=-1)
        h = rms_norm(x, g_mix[l]) * (1.0 + scale1) + shift1
        proj = h @ w_in[l]
        q_a, lat, k_r, iq, ik, iw, q_b, k_b, v_b, f_b = jnp.split(proj, split_at, axis=-1)
        o_a = dsa_attention(q_a.reshape(b, s, N_HEADS_A, HEAD_DIM_A), rms_norm(lat, g_kv[l]), k_r,
                            iq.reshape(b, s, IDX_HEADS, IDX_DIM), ik, iw,
                            cos_a, sin_a, cos_i, sin_i, w_uk[l], w_uv[l])
        o_b = forgetting_attention(q_b.reshape(b, s, N_HEADS_B, HEAD_DIM_B),
                                   k_b.reshape(b, s, N_HEADS_B, HEAD_DIM_B),
                                   v_b.reshape(b, s, N_HEADS_B, HEAD_DIM_B),
                                   f_b + b_forget[l])
        mixed = jnp.concatenate([rms_norm(o_a, g_out_a[l]), rms_norm(o_b, g_out_b[l])], axis=-1)
        x = x + gate1 * (mixed @ w_out[l])
        h2 = rms_norm(x, g_ffn[l]) * (1.0 + scale2) + shift2
        x = x + gate2 * peer_ffn(h2, w_peer_q[l], peer_keys1[l], peer_keys2[l], peer_u[l], peer_v[l])
    return rms_norm(x, g_final)


def setup_inputs(seed=0):
    out = dict(first_inputs(seed))
    for name, value in second_inputs(seed + 1).items():
        if name != "x":
            out[name + "_2"] = value
    return out


def reference(
    x, norm_mix_g, w_in, conv_a_w, gdn_conv_w, gdn_A_log, gdn_dt_bias, gdn_norm_g, w_a_out,
    w_b_out, w_o, norm_ffn_g, w_up, ffn_conv_w, w_down, norm_final_g, c_2, positions_2, w_ada_2,
    b_ada_2, g_mix_2, w_in_2, g_kv_2, w_uk_2, w_uv_2, b_forget_2, g_out_a_2, g_out_b_2, w_out_2,
    g_ffn_2, w_peer_q_2, peer_keys1_2, peer_keys2_2, peer_u_2, peer_v_2, g_final_2,
):
    x = first_block(
        x, norm_mix_g, w_in, conv_a_w, gdn_conv_w, gdn_A_log, gdn_dt_bias, gdn_norm_g, w_a_out,
        w_b_out, w_o, norm_ffn_g, w_up, ffn_conv_w, w_down, norm_final_g,
    )
    return second_block(
        x, c_2, positions_2, w_ada_2, b_ada_2, g_mix_2, w_in_2, g_kv_2, w_uk_2, w_uv_2,
        b_forget_2, g_out_a_2, g_out_b_2, w_out_2, g_ffn_2, w_peer_q_2, peer_keys1_2,
        peer_keys2_2, peer_u_2, peer_v_2, g_final_2,
    )


_drawn_inputs = setup_inputs


def setup_inputs(seed=0):
    import zlib

    import numpy as np

    out = dict(_drawn_inputs(seed))
    spreads = {}
    factors = {'gdn_norm_g': 5.913,
     'norm_ffn_g': 3.335,
     'g_mix_2': 2.732,
     'g_kv_2': 7.882,
     'g_out_a_2': 8.0,
     'g_out_b_2': 8.0,
     'g_ffn_2': 5.813}
    for name, (base, spread) in spreads.items():
        noise = np.random.default_rng([zlib.crc32(name.encode()), seed]).standard_normal(out[name].shape)
        drawn = base * np.exp(spread * noise) if base else spread * noise
        out[name] = jnp.asarray(drawn.astype(out[name].dtype))
    for name, factor in factors.items():
        out[name] = (out[name] * factor).astype(out[name].dtype)
    return out
```

```python
from contextlib import ExitStack

import numpy as np

import concourse.bass as bass
from concourse import mybir

F32 = mybir.dt.float32
U32 = mybir.dt.uint32
I32 = mybir.dt.int32
ALU = mybir.AluOpType
ACT = mybir.ActivationFunctionType
AX = mybir.AxisListType

P = 128
S = 256
NT = S // P
D = 1024
KT = D // P
H = 8
EPS = 1e-6
FAR = -3e38
NOPE, ROPE, IDX, IROPE = 48, 16, 32, 8
TAKE, PK = 64, 16
THETA = 500000.0
TWO_PI = (6.28125, 0.0019350051879882812, 3.019915981956753e-07)
RING, ON_DVE = 16, 4
FF = 2816
FT = FF // P
BANK = 512
LEVELS = 7
BIG = 1e30

C_ID, C_ONE = 0, P
C_OFF = 2 * P
C_STRICT = C_OFF + LEVELS * P
C_INCL = C_STRICT + P
C_CAUS = C_INCL + P
C_NEG = C_CAUS + NT * S
C_SEL = C_NEG + NT * S
C_IOTA = C_SEL + H * P
C_END = C_IOTA + 16


def constant_table():
    j = np.arange(P)[:, None]
    i = np.arange(P)[None, :]
    t = np.zeros((P, C_END), np.float32)
    t[:, C_ID:C_ID + P] = i == j
    t[:, C_ONE:C_ONE + P] = 1.0
    for s in range(LEVELS):
        w = 1 << s
        t[:, C_OFF + s * P:C_OFF + (s + 1) * P] = (j // (2 * w) == i // (2 * w)) & (j // w != i // w)
    t[:, C_STRICT:C_STRICT + P] = i > j
    t[:, C_INCL:C_INCL + P] = i >= j
    key = np.arange(S)[None, :]
    for n in range(NT):
        seen = key <= n * P + j
        t[:, C_CAUS + n * S:C_CAUS + (n + 1) * S] = seen
        t[:, C_NEG + n * S:C_NEG + (n + 1) * S] = np.where(seen, 0.0, -BIG)
    for h in range(H):
        t[h, C_SEL + h * P:C_SEL + (h + 1) * P] = 1.0
    t[:, C_IOTA:C_IOTA + 16] = np.arange(16)
    return t


VEC = {}
_rows = 0
for _name, _n in (("norm_mix_g", 8), ("conv_a_w", 24), ("gdn_conv_w", 96), ("ffn_conv_w", 132), ("norm_ffn_g", 8),
                  ("g_mix_2", 8), ("g_kv_2", 1), ("g_out_a_2", 4), ("g_out_b_2", 4), ("gdn_norm_g", 1), ("c_2", 8)):
    VEC[_name] = (_rows, _n)
    _rows += _n
VROWS = _rows
VT = -(-VROWS // P)
VEC_PIECES = []
for _name, (_row, _n) in VEC.items():
    _done = 0
    while _done < _n:
        _m = min(_n - _done, P - (_row + _done) % P)
        VEC_PIECES.append((_name, _row + _done, _m, _done))
        _done += _m
VEC_DMAS = len(VEC_PIECES) + 4

TURNS = P // 2 // RING
PARTS = 2 * NT
NS = 3
UPS = FT // 2

INPUTS = """x norm_mix_g w_in conv_a_w gdn_conv_w gdn_A_log gdn_dt_bias gdn_norm_g w_a_out w_b_out w_o norm_ffn_g
w_up ffn_conv_w w_down norm_final_g c_2 positions_2 w_ada_2 b_ada_2 g_mix_2 w_in_2 g_kv_2 w_uk_2 w_uv_2 b_forget_2
g_out_a_2 g_out_b_2 w_out_2 g_ffn_2 w_peer_q_2 peer_keys1_2 peer_keys2_2 peer_u_2 peer_v_2 g_final_2""".split()

SEMAPHORES = """const_in vec_in x_in row_in eps_done vt_ready vt_done rt_done xn_done tr_done hTa hTd pair_ready silu_done
ab_ready ab_dve ab_act gates_done gt_ready gt_done sq_done sum_ready sqrt_done qk_done row_ready row_done qd_done
dexp_done eg_done tok_ready tok_done kk_ready kk_done loff_done lq_ready lq_used ld_ready x_done u_ready u_done w_ready
w_done s1_ready s1_done ws_ready vn_done o_ready o_done osq_done osum_ready osqrt_done y_done mix_done wo_ready x1_done
up_silu act_done down_ready x2_done fin_done out_done dve_chain act_chain pool_chain
c_done acc_zero acc_in ada_used mod_done small_in ffg_in fin_row_in angle_done sin_done tok_done2 qr_done iw_done lat_rt lat_done rope_done
idx_done rl_done score_used fb_dve fb_act cum_done rows_done sel_done lg_done exp_done pT_done pv_ready orow_done oss_done
wout_ready x3_done qp_done sc_done routed best_done soft_done eid_done gelu_done weight_done slot_free
ids_ready score_out diag_done pe_used dve_used peer_ready x_final key_ready key_done final_done zero_done""".split()


class Chain:

    def __init__(self, eng, sem):
        self.eng, self.sem, self.n = eng, sem, 0

    def __call__(self, ins):
        ins.then_inc(self.sem, 1)
        self.n += 1

    def wait(self):
        self.eng.wait_ge(self.sem, self.n)



XN_PEER = 14

PAIR0 = 75
P_IDX = PAIR0 + 14
P_QR = P_IDX + 2
P_KN = P_QR + 5
P_VA = P_KN + 4
P_SC = P_VA + 2
P_ROW = P_SC + 8
P_ATT = P_ROW + 4
ATT_UNITS = [(br, t, pr) for br in (1, 0) for t in range(NT) for pr in range(4)]
ATT_PAIRS = P_ATT + 2 * len(ATT_UNITS) - P_IDX
P_PQ = P_ATT + 2 * len(ATT_UNITS)
P_PS = P_PQ + 4
P_END = P_PS + 8


def att_pair(kind, n):
    if kind == 0:
        return P_ATT + (0 if n == 0 else 2 * n - 1)
    return P_ATT + (2 * n + 2 if n < len(ATT_UNITS) - 1 else 2 * n + 1)


def att_heads(br, pr):
    return (2 * pr, 2 * pr + 1) if not br else (4 * (pr % 2) + pr // 2, 4 * (pr % 2) + pr // 2 + 2)


MOD0 = 44 + 2 * (UPS - 1)


def up_pair(m, g):
    return 44 + 2 * m + g + (9 if m == UPS - 1 else 0)


ADA_AT = {1: [0], 2: [1, 2], 3: [3], 4: [4, 5], 5: [6], 6: [7, 8], 7: [9], 8: [10, 11]}


def weight_blocks(A):
    w_in = A["w_in"][0].rearrange("(k p) n -> p k n", p=P)
    at = {"bg": 0, "cg": 1024, "xv": 2048, "q": 3072, "k": 4096, "v": 5120, "z": 6144, "ga": 7184, "gb": 8208}
    out = []
    count = {}

    def add(name, src, k, n, signal, by):
        count[signal] = count.get(signal, 0) + by
        out.append((name, src, k, n, signal, count[signal]))

    def inp(name, half):
        c = at[name] + half * BANK
        add(name, w_in[:, :, c:c + BANK], KT, BANK, "pair_ready", 2)

    for name in ("q", "k", "v"):
        inp(name, 0), inp(name, 1)
    add("ab", w_in[:, :, 7168:7184], KT, 16, "ab_ready", 1)
    inp("z", 0), inp("z", 1)
    for half in range(2):
        for name in ("cg", "xv", "bg"):
            inp(name, half)
    for name in ("ga", "gb"):
        inp(name, 0), inp(name, 1)
    for name, w in (("wa", "w_a_out"), ("wb", "w_b_out"), ("wo", "w_o")):
        for half in range(2):
            src = A[w][0].rearrange("(k p) n -> p k n", p=P)[:, :, half * BANK:(half + 1) * BANK]
            add(name, src, KT, BANK, *(("wo_ready", 2) if name == "wo" else ("pair_ready", 2)))
    up = A["w_up"][0].rearrange("(k p) (g n) -> p k g n", p=P, g=2)
    down = A["w_down"][0].rearrange("(k p) n -> p k n", p=P)
    for m in range(UPS):
        if m == UPS - 1:
            count["pair_ready"] += 9
        add("up", up[:, :, :, 2 * P * m:2 * P * (m + 1)], KT, 4 * P, "pair_ready", 2)
        if m % 2 == 0 and m >= 2:
            add("down", down[:, 2 * m - 4:2 * m, :], 4, D, "down_ready", 2)
    add("down", down[:, FT - 2:FT, :], 2, D, "down_ready", 1)
    w2 = A["w_in_2"][0].rearrange("(k p) n -> p k n", p=P)
    add("tok", w2[:, :, 512:952], KT, 440, "pair_ready", 2)
    add("qa", w2[:, :, 0:512], KT, 512, "pair_ready", 5)
    add("qb", w2[:, :, 952:1464], KT, BANK, "pair_ready", 2)
    add("kb", w2[:, :, 1464:1976], KT, BANK, "pair_ready", 2)
    add("vb", w2[:, :, 1976:2488], KT, BANK, "pair_ready", 2)
    add("fb", w2[:, :, 2488:2496], KT, H, "pair_ready", 1)
    count["pair_ready"] += ATT_PAIRS
    for name, w in (("wout", "w_out_2"), ("wpq", "w_peer_q_2")):
        for half in range(2):
            src = A[w][0].rearrange("(k p) n -> p k n", p=P)[:, :, half * BANK:(half + 1) * BANK]
            add(name, src, KT, BANK, *(("wout_ready", 2) if name == "wout" else ("pair_ready", 2)))
    return out


def program(nc, A, out):
    ctx = ExitStack()
    with ctx:
        def sb(name, shape, dt=F32):
            return ctx.enter_context(nc.sbuf_tensor(name, shape, dt))

        def sem(name):
            return ctx.enter_context(nc.semaphore(name))

        cst = sb("cst", [P, C_END])
        vec = sb("vec", [P, VT * P])
        x = sb("x", [P, NT, D])
        xn = sb("xn", [P, NT, D])
        hT = sb("hT", [P, KT, S])
        wr = [sb(f"wr{i}", [P, KT * BANK]) for i in range(NS)]
        small = sb("small", [H, 8, S])
        gate_par = sb("gate_par", [H, 4])
        stat = sb("stat", [P, 48])
        ssum = sb("ssum", [P, 64])
        Gtok = sb("Gtok", [P, NT, 2 * H])
        kbs = sb("kbs", [P, H])
        egt = sb("egt", [P, H])
        eps = sb("eps", [P, 2])
        arena = sb("arena", [P, 110 * 256])
        bank = [ctx.enter_context(nc.psum_tensor(f"bank{i}", [P, BANK], F32)) for i in range(8)]

        ident = cst[:, C_ID:C_ID + P]
        ones = cst[:, C_ONE:C_ONE + P]

        def region(kb, n):
            return arena[:, kb * 256:kb * 256 + n]

        def tiles(kb):
            return region(kb, 2048).rearrange("p (f s) -> p f s", f=KT)

        def heads16(kb):
            return region(kb, 2048).rearrange("p (e c) -> p e c", e=NT * H)

        def heads8(kb):
            return region(kb, 1024).rearrange("p (h c) -> p h c", h=H)

        vrow = region(0, VT * P).rearrange("p (t c) -> p t c", t=VT)
        qT, kT, vT, zT, sga, sgb, ya = (tiles(8 * i) for i in range(7))
        raw = region(56, 1024).rearrange("p (r u s) -> p r u s", r=2, u=2)
        t1 = region(60, 512).rearrange("p (u s) -> p u s", u=2)
        qd = heads8(56)
        DT, LT, X, XT, Vb = (heads16(62 + 8 * i) for i in range(5))
        Kb, Kd = heads8(102), heads8(106)
        sq, rn = region(70, 2048), region(78, 2048)
        Qs = xn[:, :, :].rearrange("p t (h c) -> p (t h) c", c=P)
        Loff = hT[:, :, :].rearrange("p k (a c) -> p (k a) c", a=2)
        u = heads16(0)
        wT, S1 = heads8(8), heads8(12)
        oT = vT
        act_ffn = region(0, FT * S).rearrange("p (f s) -> p f s", f=FT)
        raw2 = region(22, 2048).rearrange("p (r u s) -> p r u s", r=4, u=2)
        sg = region(30, 1024).rearrange("p (r u s) -> p r u s", r=2, u=2)
        nfg = region(90, D)
        ada = [region(34 + 16 * i, 4096).rearrange("p (k n) -> p k n", k=KT) for i in range(2)]
        acc = region(66, 6 * D)
        csil = sb("csil", [P, KT])
        modc = sb("modc", [P, 2, KT])
        modb = region(34, 4 * D).rearrange("p (m n) -> p m n", m=4)
        qn = region(0, 2048).rearrange("p (h s) -> p h s", h=H)
        kn = region(8, 2048).rearrange("p (h s) -> p h s", h=H)
        qrT = region(16, 9 * S).rearrange("p (h s) -> p h s", h=H + 1)
        tokp = region(25, NT * 440).rearrange("p (t n) -> p t n", t=NT)
        rp = region(29, NT * 9 * ROPE).rearrange("p (t h n) -> p t h n", t=NT, h=H + 1)
        rtmp = region(31, 4 * 144).rearrange("p (m n) -> p m n", m=4)
        iqT = region(50, 2 * S).rearrange("p (b s) -> p b s", b=2)
        ikT, latT = region(52, S), region(53, S)
        va = region(54, NT * BANK).rearrange("p (t n) -> p t n", t=NT)
        qb = region(58, 4 * S).rearrange("p (f s) -> p f s", f=4)
        kb = region(62, 4 * S).rearrange("p (f s) -> p f s", f=4)
        lg = region(66, 4 * BANK).rearrange("p (r u s) -> p r u s", r=4, u=2)
        pT = region(74, 4 * BANK).rearrange("p (r c) -> p r c", r=4)
        rl = region(82, 4 * BANK).rearrange("p (r u s) -> p r u s", r=4, u=2)
        latn = region(90, NT * P).rearrange("p (t c) -> p t c", t=NT)
        ikrep = region(91, NT * P).rearrange("p (t c) -> p t c", t=NT)
        work = region(92, NT * S).rearrange("p (t s) -> p t s", t=NT)
        vb = region(94, NT * BANK).rearrange("p (t n) -> p t n", t=NT)
        score = region(98, NT * S).rearrange("p (t s) -> p t s", t=NT)
        negA = region(100, NT * S).rearrange("p (t s) -> p t s", t=NT)
        wuk, wuv = region(106, H * NOPE), region(108, BANK)
        rows = xn[:, :, :].rearrange("p t (h s) -> p (t h) s", s=S)
        posi = sb("posi", [P, NT], I32)
        trig = sb("trig", [P, 4, NT * 24])
        amax = sb("amax", [P, 32])
        iws = sb("iws", [P, NT, H])
        top8 = sb("top8", [P, NT, 8])
        qpT = tiles(0)
        scr = region(8, NT * 2 * H * P).rearrange("p (t g c) -> p t g c", t=NT, g=2 * H)
        cand = region(24, H * S).rearrange("p (h c) -> p h c", h=H)
        hot = region(66, 8 * S)
        keys = region(106, P)
        keysT = sb("keysT", [P, P])
        top = region(74, NT * 256).rearrange("p (t g c) -> p t g c", t=NT, g=2 * H)
        topi = arena[:, 76 * 256:76 * 256 + NT * 256].bitcast(U32).rearrange("p (t g c) -> p t g c", t=NT, g=2 * H)
        topf = region(78, NT * 256).rearrange("p (t g c) -> p t g c", t=NT, g=2 * H)
        best = region(80, NT * P).rearrange("p (t c) -> p t c", t=NT)
        bpos = arena[:, 81 * 256:82 * 256].bitcast(U32).rearrange("p (t c) -> p t c", t=NT)
        babu = arena[:, 82 * 256:84 * 256].bitcast(U32).rearrange("p (m t c) -> p m t c", m=2, t=NT)
        babf = region(84, 512).rearrange("p (m t c) -> p m t c", m=2, t=NT)
        pick = region(86, 512).rearrange("p (m t c) -> p m t c", m=2, t=NT)
        eid = arena[:, 88 * 256:89 * 256].bitcast(U32).rearrange("p (t c) -> p t c", t=NT)
        gsoft = region(89, NT * P).rearrange("p (t c) -> p t c", t=NT)
        dots = region(98, NT * P).rearrange("p (t c) -> p t c", t=NT)
        wgt = region(99, NT * P).rearrange("p (t c) -> p t c", t=NT)
        diag = region(16, 12 * P).rearrange("p (r c) -> p r c", r=12)
        zero = region(22, P)
        vacc = region(0, NT * D).rearrange("p (t n) -> p t n", t=NT)
        dotst = sb("dotst", [P, RING])
        tick = sb("tick", [P, 4])
        eidst = sb("eidst", [P, RING], U32)
        gring = [wr[i // 4][:, (i % 4) * D:(i % 4 + 1) * D] for i in range(12)] + [region(50 + 4 * i, D) for i in range(4)]
        ffg = region(90, D)
        junk = region(102, D)

        s = {n: sem(n) for n in SEMAPHORES}
        ada_in = [sem(f"ada_in{i}") for i in range(2)]
        w_in = [sem(f"w_in{i}") for i in range(NS)]
        g_in = [sem(f"g_in{i}") for i in range(RING)]
        bank_free = [sem(f"bank_free{i}") for i in range(4)]
        blocks = weight_blocks(A)
        landed = [16 * sum(2 if b[0] == "up" else 1 for b in blocks[i % NS:i + 1:NS]) for i in range(len(blocks))]

        def slot(i):
            k, n = blocks[i][2:4]
            return wr[i % NS][:, 0:k * n].rearrange("p (k n) -> p k n", k=k)

        def vcol(name, i):
            c = VEC[name][0] + i
            return vec[:, c:c + 1]

        block = ctx.enter_context(nc.Block())

        @block.sync
        def _(sp):
            sp.dma_start(x[:, :, :], A["x"][0].rearrange("(t p) d -> p t d", p=P)).then_inc(s["x_in"], 16)
            sp.dma_start(cst[:, :], A["consts"][:, :]).then_inc(s["const_in"], 16)
            for name, row, m, r0 in VEC_PIECES:
                flat = A[name]
                while len(flat.shape) > 2:
                    flat = flat.rearrange("a b c -> (a b) c")
                if len(flat.shape) == 1:
                    flat = flat.unsqueeze(0)
                src = flat.rearrange("a (r c) -> (a r) c", c=P)
                t, r = divmod(row, P)
                sp.dma_start(vrow[r:r + m, t, :], src[r0:r0 + m, :]).then_inc(s["vec_in"], 16)
            for i, name in enumerate(("gdn_A_log", "gdn_dt_bias")):
                sp.dma_start(gate_par[:, i:i + 1], A[name].rearrange("a h -> h a")).then_inc(s["vec_in"], 16)
            sp.dma_start(gate_par[:, 3:4], A["b_forget_2"].rearrange("a h -> h a")).then_inc(s["vec_in"], 16)
            sp.dma_start(posi[:, :], A["positions_2"][0].rearrange("(t p) -> p t", p=P),
                         allow_slow_non_contiguous=True).then_inc(s["vec_in"], 16)
            ups = 0
            w_ada = A["w_ada_2"][0].rearrange("(k p) n -> p k n", p=P)
            for i, (name, src, k, cols, _, _) in enumerate(blocks):
                if i >= NS:
                    sp.wait_ge(s[blocks[i - NS][4]], blocks[i - NS][5])
                if name == "up":
                    for g in range(2):
                        half = slot(i)[:, :, g * 2 * P:(g + 1) * 2 * P]
                        sp.dma_start(half, src[:, :, g, :]).then_inc(w_in[i % NS], 16)
                else:
                    sp.dma_start(slot(i), src).then_inc(w_in[i % NS], 16)
                if name == "up":
                    ups += 1
                    for j in ADA_AT.get(ups - 2, ()):
                        if j >= 2:
                            sp.wait_ge(s["ada_used"], j - 1)
                        sp.dma_start(ada[j % 2], w_ada[:, :, j * BANK:(j + 1) * BANK]).then_inc(ada_in[j % 2], 16)
                if name == "fb":
                    sp.dma_start(wuk, A["w_uk_2"][0].rearrange("r h n -> r (h n)")).then_inc(s["small_in"], 16)
                    sp.dma_start(wuv, A["w_uv_2"][0].rearrange("r h n -> r (h n)")).then_inc(s["small_in"], 16)
                if name == "wpq" and blocks[i - 1][0] == "wpq":
                    sp.wait_ge(s["x3_done"], 4)
                    sp.dma_start(ffg, A["g_ffn_2"][0].partition_broadcast(P)).then_inc(s["ffg_in"], 16)
                    for n, key in enumerate(("peer_keys1_2", "peer_keys2_2")):
                        sp.dma_start(keys[:, n * 64:(n + 1) * 64], A[key][0]).then_inc(s["ffg_in"], 16)
                if name == "wo" and blocks[i - 1][0] == "wo":
                    sp.wait_ge(s["mix_done"], 4)
                    sp.dma_start(nfg, A["norm_final_g"].partition_broadcast(P)).then_inc(s["row_in"], 16)
            sp.wait_ge(s["xn_done"], XN_PEER)
            sp.dma_start(ffg, A["g_final_2"].partition_broadcast(P)).then_inc(s["fin_row_in"], 16)
            sp.wait_ge(s["final_done"], NT)
            sp.dma_start(out[0].rearrange("(t p) d -> p t d", p=P), x[:, :, :]).then_inc(s["out_done"], 16)
            sp.wait_ge(s["out_done"], 16)

        @block.tensor
        def _(pe):
            pairs = [0]

            def weights(i):
                pe.wait_ge(w_in[i % NS], landed[i])

            def wide(i, act):
                weights(i)
                for half in range(2):
                    p = pairs[0]
                    if p >= 4:
                        pe.wait_ge(bank_free[p % 4], p // 4)
                    for f in range(2):
                        for k in range(KT):
                            c = (2 * half + f) * P
                            mm = nc.tensor.matmul(bank[p % 4][:, f * S:(f + 1) * S], slot(i)[:, k, c:c + P],
                                                  act[:, k, :], start=k == 0, stop=k == KT - 1)
                    mm.then_inc(s["pair_ready"], 1)
                    pairs[0] += 1

            def claim():
                p = pairs[0]
                if p >= 4:
                    pe.wait_ge(bank_free[p % 4], p // 4)
                pairs[0] += 1
                return p

            def modulation():
                for r in range(8):
                    p = claim()
                    c = 2 * D + r * BANK
                    nc.tensor.matmul(bank[p % 4][:, :], ones, acc[:, c:c + BANK], start=True,
                                     stop=True).then_inc(s["pair_ready"], 1)
                p = claim()
                for f in range(2 * KT):
                    mm = nc.tensor.matmul(bank[p % 4][:, f:f + 1], acc[:, f * P:(f + 1) * P], ones[:, 0:1],
                                          start=True, stop=True)
                mm.then_inc(s["pair_ready"], 1)

            def norm_turn(n):
                pe.wait_ge(s["xn_done"], (2, 4, 8, 12, 14)[n])
                for b in range(4):
                    for i in range(4):
                        k, t = 2 * b + i // 2, i % 2
                        mm = nc.tensor.transpose(bank[4 + b][:, i * P:(i + 1) * P], xn[:, t, k * P:(k + 1) * P], ident)
                    mm.then_inc(s["tr_done"], 1)
                pe.wait_ge(s["hTa"], 4 * (n + 1))
                pe.wait_ge(s["hTd"], 4 * (n + 1))

            pe.wait_ge(s["const_in"], 16)
            pe.wait_ge(s["vec_in"], 16 * VEC_DMAS)
            for t in range(VT):
                r = min(P, VROWS - t * P)
                mm = nc.tensor.transpose(bank[0][:, t * P:t * P + r], vrow[0:r, t, :], cst[0:r, C_ID:C_ID + r])
            mm.then_inc(s["vt_ready"], 1)
            pe.wait_ge(s["vt_done"], 1)
            norm_turn(0)
            for i in range(6):
                wide(i, hT)
            weights(6)
            for g in range(2):
                for k in range(KT):
                    mm = nc.tensor.matmul(bank[4][0:H, g * S:(g + 1) * S], slot(6)[:, k, g * H:(g + 1) * H], hT[:, k, :],
                                          start=k == 0, stop=k == KT - 1)
            mm.then_inc(s["ab_ready"], 1)
            wide(7, hT)
            wide(8, hT)
            pe.wait_ge(s["gates_done"], 1)
            for g in range(2):
                for t in range(NT):
                    mm = nc.tensor.transpose(bank[4][:, t * 16 + g * H:t * 16 + (g + 1) * H],
                                             small[:, 6 + g, t * P:(t + 1) * P], cst[0:H, C_ID:C_ID + H])
            mm.then_inc(s["gt_ready"], 1)
            pe.wait_ge(s["gt_done"], 1)
            for n in range(2):
                pe.wait_ge(s["sq_done"], n + 1)
                for b in range(4):
                    if n:
                        pe.wait_ge(s["sqrt_done"], b + 1)
                    nc.tensor.matmul(bank[4 + b][:, :], ones, sq[:, b * BANK:(b + 1) * BANK],
                                     start=True, stop=True).then_inc(s["sum_ready"], 1)
            for i in range(9, 12):
                wide(i, hT)
            for g in range(2):
                for b in range(4):
                    pe.wait_ge(s["sqrt_done"], 5 + b)
                    if g:
                        pe.wait_ge(s["row_done"], b + 1)
                        pe.wait_ge(s["qd_done"], b + 1)
                    for f in range(2):
                        h = 2 * b + f
                        mm = nc.tensor.matmul(bank[4 + b][:, f * S:(f + 1) * S],
                                              cst[0:H, C_SEL + h * P:C_SEL + (h + 1) * P], small[:, 6 + g, :],
                                              start=True, stop=True)
                    mm.then_inc(s["row_ready"], 1)
            for i in range(12, 19):
                wide(i, hT)
            pe.wait_ge(s["row_done"], 8)
            pe.wait_ge(s["qk_done"], 8)
            for n in range(8):
                src, g = (vT, n) if n < 4 else (kT, n - 4)
                t, h0 = g // 2, 4 * (g % 2)
                if n >= 4:
                    pe.wait_ge(s["tok_done"], n - 3)
                for j in range(4):
                    mm = nc.tensor.transpose(bank[4 + g][:, j * P:(j + 1) * P], src[:, h0 + j, t * P:(t + 1) * P], ident)
                mm.then_inc(s["tok_ready"], 1)
            for n in range(8):
                g = n % 4
                t, h0 = g // 2, 4 * (g % 2)
                if n < 4:
                    pe.wait_ge(s["tok_done"], 5 + g)
                else:
                    pe.wait_ge(s["kk_done"], n - 3)
                other = kT if n < 4 else qT
                for j in range(4):
                    mm = nc.tensor.matmul(bank[4 + g][:, j * P:(j + 1) * P], kT[:, h0 + j, t * P:(t + 1) * P],
                                          other[:, h0 + j, t * P:(t + 1) * P], start=True, stop=True)
                mm.then_inc(s["kk_ready"], 1)
            for b in range(4):
                pe.wait_ge(bank_free[b], 9)
            for lv in range(LEVELS):
                for g in range(4):
                    pe.wait_ge(s["loff_done"], 4 * lv + g + 1)
                    if lv == 0:
                        pe.wait_ge(s["kk_done"], 5 + g)
                    else:
                        pe.wait_ge(s["x_done"], 4 * (lv - 1) + g + 1)
                    for e in range(4 * g, 4 * g + 4):
                        o = bank[4 + g][:, (e % 4) * P:(e % 4 + 1) * P]
                        if lv == 0:
                            mm = nc.tensor.transpose(o, Loff[:, e, :], ident)
                        else:
                            mm = nc.tensor.matmul(o, Loff[:, e, :], X[:, e, :], start=True, stop=True)
                    mm.then_inc(s["lq_ready"], 1)
                if lv == 0:
                    continue
                for g in range(4):
                    pe.wait_ge(s["lq_used"], 4 * (lv - 1) + g + 1)
                    for e in range(4 * g, 4 * g + 4):
                        if lv < LEVELS - 1:
                            nc.tensor.matmul(bank[4 + g][:, (e % 4) * P:(e % 4 + 1) * P], XT[:, e, :], Qs[:, e, :],
                                             start=True, stop=True)
                        mm = nc.tensor.matmul(bank[g][:, (e % 4) * P:(e % 4 + 1) * P], Qs[:, e, :], XT[:, e, :],
                                              start=True, stop=True)
                    mm.then_inc(s["ld_ready"], 1)
            for g in range(4):
                pe.wait_ge(s["x_done"], 4 * (LEVELS - 1) + g + 1)
                for e in range(4 * g, 4 * g + 4):
                    mm = nc.tensor.matmul(bank[4 + g][:, (e % 4) * P:(e % 4 + 1) * P], XT[:, e, :], Vb[:, e, :],
                                          start=True, stop=True)
                mm.then_inc(s["u_ready"], 1)

            def by_head(b, lhs, rhs, g):
                for h in range(4 * g, 4 * g + 4):
                    mm = nc.tensor.matmul(bank[b][:, (h % 4) * P:(h % 4 + 1) * P], lhs[:, h, :], rhs[:, h, :],
                                          start=True, stop=True)
                return mm

            for g in range(2):
                by_head(g, Kb, XT[:, H:, :], g).then_inc(s["w_ready"], 1)
            for g in range(2):
                pe.wait_ge(s["u_done"], g + 1)
                by_head(2 + g, Kd, u, g).then_inc(s["s1_ready"], 1)
            for g in range(2):
                by_head(4 + g, u, DT, g).then_inc(s["o_ready"], 1)
            for g in range(2):
                pe.wait_ge(s["s1_done"], g + 1)
                pe.wait_ge(s["w_done"], g + 1)
                by_head(g, wT, S1, g).then_inc(s["ws_ready"], 1)
            for g in range(2):
                pe.wait_ge(s["vn_done"], g + 1)
                for h in range(4 * g, 4 * g + 4):
                    o = bank[6 + g][:, (h % 4) * P:(h % 4 + 1) * P]
                    nc.tensor.matmul(o, S1[:, h, :], qd[:, h, :], start=True, stop=False)
                    mm = nc.tensor.matmul(o, u[:, H + h, :], DT[:, H + h, :], start=False, stop=True)
                mm.then_inc(s["o_ready"], 1)
            wide(19, ya)
            wide(20, ya)
            pe.wait_ge(s["osq_done"], 4)
            for b in range(4):
                nc.tensor.matmul(bank[4 + b][:, :], ones, sq[:, b * BANK:(b + 1) * BANK],
                                 start=True, stop=True).then_inc(s["osum_ready"], 1)
            pe.wait_ge(s["y_done"], 4)
            wide(21, oT)
            wide(22, oT)
            pe.wait_ge(s["mix_done"], 4)
            for n in range(2):
                weights(23 + n)
                for t in range(NT):
                    for k in range(KT):
                        mm = nc.tensor.matmul(bank[4 + 2 * n + t][:, :], sgb[:, k, t * P:(t + 1) * P],
                                              slot(23 + n)[:, k, :], start=k == 0, stop=k == KT - 1)
                    mm.then_inc(s["wo_ready"], 1)
            norm_turn(1)
            i = 25
            for m in range(UPS):
                assert blocks[i][0] == "up"
                wide(i, hT)
                i += 1
                downs = [m - 2, m - 1] if m % 2 == 0 and m >= 2 else []
                for step in downs + ([m] if m == UPS - 1 else []):
                    if step != m - 1:
                        weights(i)
                    pe.wait_ge(s["act_done"], step + 1)
                    for r in range(2):
                        f = 2 * step + r
                        for t in range(NT):
                            for n in range(2):
                                row = 2 * (step % 2) + r
                                mm = nc.tensor.matmul(bank[4 + 2 * n + t][:, :], act_ffn[:, f, t * P:(t + 1) * P],
                                                      slot(i)[:, row, n * BANK:(n + 1) * BANK],
                                                      start=f == 0, stop=f == FT - 1)
                    mm.then_inc(s["down_ready"], 1)
                    if step != m - 2:
                        i += 1
                if m == UPS - 2:
                    pe.wait_ge(s["ada_used"], 12)
                    modulation()
            norm_turn(2)

            def by_token(i, cols, t0=None):
                weights(i)
                for t in range(NT):
                    p = claim()
                    for k in range(KT):
                        mm = nc.tensor.matmul(bank[p % 4][:, 0:cols], hT[:, k, t * P:(t + 1) * P], slot(i)[:, k, :],
                                              start=k == 0, stop=k == KT - 1)
                    mm.then_inc(s["pair_ready"], 1)

            assert blocks[i][0] == "tok" and pairs[0] == PAIR0
            by_token(i, 440)
            i += 1
            weights(i)
            heads = slot(i).rearrange("p k (h n) -> p k h n", h=H)
            p = claim()
            for t in range(NT):
                for k in range(KT):
                    mm = nc.tensor.matmul(bank[p % 4][:, t * P:(t + 1) * P].rearrange("p (h n) -> p h n", h=H),
                                          hT[:, k, t * P:(t + 1) * P], heads[:, k, :, 0:ROPE], start=k == 0, stop=k == KT - 1)
            mm.then_inc(s["pair_ready"], 1)
            for pr in range(4):
                p = claim()
                for f in range(2):
                    for k in range(KT):
                        mm = nc.tensor.matmul(bank[p % 4][0:NOPE, f * S:(f + 1) * S], heads[:, k, 2 * pr + f, ROPE:],
                                              hT[:, k, :], start=k == 0, stop=k == KT - 1)
                mm.then_inc(s["pair_ready"], 1)
            wide(i + 1, hT)
            wide(i + 2, hT)
            by_token(i + 3, BANK)
            i += 4
            weights(i)
            p = claim()
            for k in range(KT):
                mm = nc.tensor.matmul(bank[p % 4][0:H, 0:S], slot(i)[:, k, :], hT[:, k, :], start=k == 0, stop=k == KT - 1)
            mm.then_inc(s["pair_ready"], 1)
            i += 1
            assert pairs[0] == P_IDX
            pe.wait_ge(s["rope_done"], 2)
            p = claim()
            for b in range(2):
                for t in range(NT):
                    mm = nc.tensor.transpose(bank[p % 4][:, b * S + t * P:b * S + (t + 1) * P],
                                             tokp[:, t, 144 + b * P:144 + (b + 1) * P], ident)
            mm.then_inc(s["pair_ready"], 1)
            p = claim()
            pe.wait_ge(s["lat_done"], 1)
            for b, src in enumerate((ikrep, latn)):
                for t in range(NT):
                    mm = nc.tensor.transpose(bank[p % 4][:, b * S + t * P:b * S + (t + 1) * P], src[:, t, :], ident)
            mm.then_inc(s["pair_ready"], 1)
            for pr in range(5):
                p = claim()
                for f in range(2 if pr < 4 else 1):
                    for t in range(NT):
                        mm = nc.tensor.transpose(bank[p % 4][0:ROPE, f * S + t * P:f * S + (t + 1) * P],
                                                 rp[:, t, 2 * pr + f, :], ident)
                mm.then_inc(s["pair_ready"], 1)
            pe.wait_ge(s["small_in"], 32)
            pe.wait_ge(bank_free[(P_IDX + 1) % 4], (P_IDX + 1) // 4 + 1)
            for pr in range(4):
                p = claim()
                for f in range(2):
                    h = 2 * pr + f
                    mm = nc.tensor.matmul(bank[p % 4][0:NOPE, f * S:(f + 1) * S], wuk[:, h * NOPE:(h + 1) * NOPE], latT,
                                          start=True, stop=True)
                mm.then_inc(s["pair_ready"], 1)
            for t in range(NT):
                p = claim()
                nc.tensor.matmul(bank[p % 4][:, :], latT[:, t * P:(t + 1) * P], wuv, start=True,
                                 stop=True).then_inc(s["pair_ready"], 1)
            for t in range(NT):
                for j in range(4):
                    p = claim()
                    n = (t + 1) * P
                    for b in range(2):
                        mm = nc.tensor.matmul(bank[p % 4][:, b * S:b * S + n], iqT[IDX * j:IDX * (j + 1), b, t * P:(t + 1) * P],
                                              ikT[IDX * j:IDX * (j + 1), 0:n], start=True, stop=True)
                    mm.then_inc(s["pair_ready"], 1)
            pe.wait_ge(s["cum_done"], 1)
            for pr in range(4):
                p = claim()
                for f in range(2):
                    h = 2 * pr + f
                    mm = nc.tensor.matmul(bank[p % 4][:, f * S:(f + 1) * S], cst[0:H, C_SEL + h * P:C_SEL + (h + 1) * P],
                                          small[:, 6, :], start=True, stop=True)
                mm.then_inc(s["pair_ready"], 1)
            assert pairs[0] == P_ATT
            pe.wait_ge(bank_free[(P_VA + 1) % 4], (P_VA + 1) // 4 + 1)
            U = len(ATT_UNITS)
            for step in range(U + 2):
                if step < U:
                    br, t, pr = ATT_UNITS[step]
                    p = claim()
                    assert p == att_pair(0, step)
                    n = (t + 1) * P
                    for f, h in enumerate(att_heads(br, pr)):
                        o = bank[p % 4][:, f * S:f * S + n]
                        if br:
                            r = 64 * (h % 2)
                            mm = nc.tensor.matmul(o, qb[r:r + 64, h // 2, t * P:(t + 1) * P], kb[r:r + 64, h // 2, 0:n],
                                                  start=True, stop=True)
                        else:
                            nc.tensor.matmul(o, qn[0:NOPE, h, t * P:(t + 1) * P], kn[0:NOPE, h, 0:n], start=True, stop=False)
                            mm = nc.tensor.matmul(o, qrT[0:ROPE, h, t * P:(t + 1) * P], qrT[0:ROPE, H, 0:n],
                                                  start=False, stop=True)
                    mm.then_inc(s["pair_ready"], 1)
                if 1 <= step <= U:
                    br, t, pr = ATT_UNITS[step - 1]
                    p = claim()
                    pe.wait_ge(s["exp_done"], 2 * step)
                    assert p == att_pair(1, step - 1)
                    for f in range(2):
                        for b in range(t + 1):
                            mm = nc.tensor.transpose(bank[p % 4][:, (f * 2 + b) * P:(f * 2 + b + 1) * P],
                                                     lg[:, (step - 1) % 4, f, b * P:(b + 1) * P], ident)
                    mm.then_inc(s["pair_ready"], 1)
                if step >= 2:
                    br, t, pr = ATT_UNITS[step - 2]
                    turned = att_pair(1, step - 2)
                    pe.wait_ge(bank_free[turned % 4], turned // 4 + 1)
                    src = vb if br else va
                    for f, h in enumerate(att_heads(br, pr)):
                        for b in range(t + 1):
                            mm = nc.tensor.matmul(bank[4 + 2 * br + t][:, h * 64:(h + 1) * 64],
                                                  pT[:, (step - 2) % 4, (f * 2 + b) * P:(f * 2 + b + 1) * P],
                                                  src[:, b, h * 64:(h + 1) * 64], start=b == 0, stop=b == t)
                    mm.then_inc(s["pv_ready"], 1)
            norm_turn(3)
            for n in range(2):
                weights(i + n)
                for t in range(NT):
                    for k in range(KT):
                        mm = nc.tensor.matmul(bank[4 + 2 * n + t][:, :], hT[:, k, t * P:(t + 1) * P], slot(i + n)[:, k, :],
                                              start=k == 0, stop=k == KT - 1)
                    mm.then_inc(s["wout_ready"], 1)
            pe.wait_ge(s["ffg_in"], 48)
            pe.wait_ge(s["x3_done"], 4)
            nc.tensor.transpose(bank[4][:, 0:P], keys, ident).then_inc(s["key_ready"], 1)
            pe.wait_ge(s["key_done"], 1)
            norm_turn(4)
            wide(i + 2, hT)
            wide(i + 3, hT)
            pe.wait_ge(bank_free[(P_PQ + 3) % 4], (P_PQ + 3) // 4 + 1)
            for b in range(1, 4):
                pe.wait_ge(bank_free[(P_PQ + 3 - b) % 4], (P_PQ + 3 - b) // 4 + 1)
            for t in range(NT):
                for q in range(2):
                    for half in range(2):
                        p = claim()
                        r = slice(64 * half, 64 * half + 64)
                        for h in range(4 * q, 4 * q + 4):
                            mm = nc.tensor.matmul(bank[p % 4][:, (h % 4) * P:(h % 4 + 1) * P], qpT[r, h, t * P:(t + 1) * P],
                                                  keysT[r, :], start=True, stop=True)
                        mm.then_inc(s["pair_ready"], 1)
            assert pairs[0] == P_END and i + 4 == len(blocks)
            pe.wait_ge(s["zero_done"], 1)
            per = RING - RING // ON_DVE
            for t in range(NT):
                for n in range(2):
                    mm = nc.tensor.matmul(bank[4 + 2 * n + t][:, :], zero, xn[:, 0, 0:BANK], start=True, stop=False,
                                          skip_group_check=True)
                if t == 0:
                    mm.then_inc(s["pe_used"], per)
                with pe.Fori(0, P // RING) as it:
                    for c in range(RING):
                        if c % ON_DVE == ON_DVE - 1:
                            continue
                        q = c - c // ON_DVE
                        pe.wait_ge(g_in[c], (it + (NT * P // RING + t * P // RING + 1)) * 16)
                        pe.wait_ge(s["diag_done"], it * per + (t * P // RING * per + q + 1))
                        for n in range(2):
                            mm = nc.tensor.matmul(bank[4 + 2 * n + t][:, :], diag[:, q, :], gring[c][:, n * BANK:(n + 1) * BANK],
                                                  start=False, stop=False, skip_group_check=True)
                        mm.then_inc(s["pe_used"], 1)
                for n in range(2):
                    mm = nc.tensor.matmul(bank[4 + 2 * n + t][:, :], zero, xn[:, 0, 0:BANK], start=False, stop=True,
                                          skip_group_check=True)
                mm.then_inc(s["peer_ready"], 1)

        @block.scalar
        def _(act):
            chain = Chain(act, s["act_chain"])
            A_ = nc.scalar.activation

            def norm_stats(n, ready, count):
                act.wait_ge(s[ready], count)
                for t in range(NT):
                    if t:
                        chain.wait()
                    chain(A_(junk[:, :], x[:, t, :], ACT.Square, accum_out=stat[:, t:t + 1]))
                chain.wait()
                A_(stat[:, 4:6], stat[:, 0:2], ACT.Sqrt, scale=1.0 / D, bias=eps[:, 0:1]).then_inc(s["rt_done"], 1)

            def norm_evac(n, scale, bias=None):
                for b in range(2):
                    act.wait_ge(s["tr_done"], 4 * n + b + 1)
                    for f in range(2):
                        k = 2 * b + f
                        src = bank[4 + b][:, f * S:(f + 1) * S]
                        if bias is None:
                            A_(hT[:, k, :], src, ACT.Copy, scale=scale(k)).then_inc(s["hTa"], 1)
                        else:
                            A_(hT[:, k, :], src, ACT.Identity, scale=scale(k), bias=bias(k)).then_inc(s["hTa"], 1)

            act.wait_ge(s["eps_done"], 1)
            norm_stats(0, "x_in", 16)
            act.wait_ge(s["vt_done"], 1)
            norm_evac(0, lambda k: vcol("norm_mix_g", k))
            act.wait_ge(s["angle_done"], 1)
            A_(trig[:, 3, :], trig[:, 0, :], ACT.Sin).then_inc(s["sin_done"], 1)
            for p in range(12):
                act.wait_ge(bank_free[p % 4], p // 4 + 1)
                dst = (qT, kT, vT)[p // 4]
                f = 2 * (p % 4)
                A_(dst[:, f:f + 2, :], raw[:, p % 2, :, :], ACT.Silu).then_inc(s["silu_done"], 1)

            def pair(p):
                act.wait_ge(s["pair_ready"], p + 1)
                return bank[p % 4][:, :].rearrange("p (u s) -> p u s", u=2)

            def evac(p, dst, f, func):
                A_(dst[:, f:f + 2, :], pair(p), func).then_inc(bank_free[p % 4], 1)

            for p in range(12, 16):
                evac(p, zT, 2 * (p - 12), ACT.Silu)
            act.wait_ge(s["ab_dve"], 1)
            chain(A_(gate_par[:, 2:3], gate_par[:, 0:1], ACT.Exp))
            chain(A_(small[:, 7, :], bank[4][0:H, S:2 * S], ACT.Exp, scale=-1.0))
            chain(A_(small[:, 2, :], small[:, 1, :], ACT.Exp))
            chain.wait()
            A_(small[:, 3, :], small[:, 2, :], ACT.Ln, bias=1.0).then_inc(s["ab_act"], 1)
            act.wait_ge(s["gt_done"], 1)
            A_(egt[:, :], Gtok[:, 1, 0:H], ACT.Exp).then_inc(s["eg_done"], 1)
            for n in range(2):
                for b in range(4):
                    act.wait_ge(s["sum_ready"], 4 * n + b + 1)
                    if n:
                        act.wait_ge(s["qk_done"], b + 1)
                    A_(rn[:, b * BANK:(b + 1) * BANK], bank[4 + b][:, :], ACT.Sqrt, scale=float(P) if n == 0 else 1.0,
                       bias=eps[:, 1:2] if n == 0 else eps[:, 0:1]).then_inc(s["sqrt_done"], 1)
            for p in range(16, 18):
                evac(p, ya, 2 * (p - 16), ACT.Copy)
            for b in range(4):
                act.wait_ge(s["row_ready"], b + 1)
                src = bank[4 + b][:, :].rearrange("p (h s) -> p h s", h=2)[:, :, P:S]
                A_(qd[:, 2 * b:2 * b + 2, :], src, ACT.Exp).then_inc(s["qd_done"], 1)
            for b in range(4):
                act.wait_ge(s["row_done"], b + 1)
                part = DT.rearrange("p (t h) c -> p t h c", t=NT)[:, :, 2 * b:2 * b + 2, :]
                A_(part, part, ACT.Exp).then_inc(s["dexp_done"], 1)
            for p in range(22, 24):
                evac(p, ya, 4 + 2 * (p - 22), ACT.Copy)
            for p in range(28, 36):
                evac(p, sga if p < 32 else sgb, 2 * ((p - 28) % 4), ACT.Sigmoid)
            for lv in range(1, LEVELS):
                for g in range(4):
                    act.wait_ge(s["lq_ready"], 4 * lv + g + 1)
                    A_(Qs[:, 4 * g:4 * g + 4, :], bank[4 + g][:, :], ACT.Copy).then_inc(s["lq_used"], 1)
            for g in range(4):
                act.wait_ge(s["u_ready"], g + 1)
                A_(u[:, 4 * g:4 * g + 4, :], bank[4 + g][:, :], ACT.Copy).then_inc(s["u_done"], 1)
            for g in range(2):
                act.wait_ge(s["w_ready"], g + 1)
                A_(wT[:, 4 * g:4 * g + 4, :], bank[g][:, :], ACT.Copy).then_inc(s["w_done"], 1)
            for g in range(2):
                act.wait_ge(s["s1_ready"], g + 1)
                A_(S1[:, 4 * g:4 * g + 4, :], bank[2 + g][:, :], ACT.Copy).then_inc(s["s1_done"], 1)
            for n in range(4):
                t, g = divmod(n, 2)
                act.wait_ge(s["o_ready"], n + 1)
                src = bank[4 + n][:, :].rearrange("p (h c) -> p h c", h=4)
                A_(oT[:, 4 * g:4 * g + 4, t * P:(t + 1) * P], src, ACT.Copy).then_inc(s["o_done"], 1)
                A_(sq.rearrange("p (h s) -> p h s", h=H)[:, 4 * g:4 * g + 4, t * P:(t + 1) * P], src,
                   ACT.Square).then_inc(s["osq_done"], 1)
            for b in range(4):
                act.wait_ge(s["osum_ready"], b + 1)
                A_(rn[:, b * BANK:(b + 1) * BANK], bank[4 + b][:, :], ACT.Sqrt, scale=1.0 / P,
                   bias=eps[:, 0:1]).then_inc(s["osqrt_done"], 1)
            norm_stats(1, "x1_done", 4)
            norm_evac(1, lambda k: vcol("norm_ffn_g", k))
            A_(csil[:, :], vec[:, VEC["c_2"][0]:VEC["c_2"][0] + KT], ACT.Silu).then_inc(s["c_done"], 1)
            for m in range(UPS):
                if m == UPS - 1:
                    for r in range(8):
                        src = bank[(MOD0 + r) % 4][:, :]
                        act.wait_ge(s["pair_ready"], MOD0 + r + 1)
                        A_(modb[:, r // 2, (r % 2) * BANK:(r % 2 + 1) * BANK], src, ACT.Copy).then_inc(bank_free[(MOD0 + r) % 4], 1)
                act.wait_ge(bank_free[up_pair(m, 0) % 4], up_pair(m, 0) // 4 + 1)
                if m >= 2:
                    act.wait_ge(s["act_done"], m - 1)
                A_(sg[:, m % 2, :, :], raw2[:, (2 * m) % 4, :, :], ACT.Silu).then_inc(s["up_silu"], 1)
            norm_stats(2, "x2_done", 4)
            norm_stats(3, "fin_done", NT)
            norm_evac(2, lambda k: modc[:, 1, k:k + 1], lambda k: modc[:, 0, k:k + 1])

            def copy_bank(p, dst, src, scale=1.0, func=ACT.Copy, free=True):
                act.wait_ge(s["pair_ready"], p + 1)
                ins = A_(dst, src, func, scale=scale)
                if free:
                    ins.then_inc(bank_free[p % 4], 1)
                else:
                    chain(ins)

            def by_head_pair(b, rows, width=S):
                return bank[b % 4][0:rows, :].rearrange("p (u s) -> p u s", u=2)

            for t in range(NT):
                copy_bank(PAIR0 + t, tokp[:, t, :], bank[(PAIR0 + t) % 4][:, 0:440])
            for t in range(NT):
                act.wait_ge(bank_free[(PAIR0 + t) % 4], (PAIR0 + t) // 4 + 1)
                chain.wait()
                chain(A_(junk[:, 0:P], tokp[:, t, 0:P], ACT.Square, accum_out=stat[:, 8 + t:9 + t]))
            chain.wait()
            A_(stat[:, 10:12], stat[:, 8:10], ACT.Sqrt, scale=1.0 / P, bias=eps[:, 0:1]).then_inc(s["lat_rt"], 1)
            for pr in range(4):
                p = PAIR0 + 3 + pr
                copy_bank(p, qn[0:NOPE, 2 * pr:2 * pr + 2, :], by_head_pair(p, NOPE), scale=0.125)
            for pr in range(4):
                p = PAIR0 + 7 + pr
                copy_bank(p, (qb, kb)[pr // 2][:, 2 * (pr % 2):2 * (pr % 2) + 2, :], by_head_pair(p, P),
                          scale=0.125 if pr < 2 else 1.0)
            for t in range(NT):
                p = PAIR0 + 11 + t
                copy_bank(p, vb[:, t, :], bank[p % 4][:, :])
            act.wait_ge(s["fb_dve"], 1)
            chain(A_(small[:, 2, :], small[:, 1, :], ACT.Exp))
            chain.wait()
            A_(small[:, 3, :], small[:, 2, :], ACT.Ln, bias=1.0).then_inc(s["fb_act"], 1)
            copy_bank(P_IDX, iqT, bank[P_IDX % 4][:, :].rearrange("p (b s) -> p b s", b=2))
            p = P_IDX + 1
            copy_bank(p, ikT, bank[p % 4][:, 0:S], free=False)
            copy_bank(p, latT, bank[p % 4][:, S:2 * S], scale=vcol("g_kv_2", 0))
            for pr in range(5):
                p = P_QR + pr
                n = 2 if pr < 4 else 1
                copy_bank(p, qrT[0:ROPE, 2 * pr:2 * pr + n, :], by_head_pair(p, ROPE)[:, 0:n, :])
            for pr in range(4):
                copy_bank(P_KN + pr, kn[0:NOPE, 2 * pr:2 * pr + 2, :], by_head_pair(P_KN + pr, NOPE))
            for t in range(NT):
                copy_bank(P_VA + t, va[:, t, :], bank[(P_VA + t) % 4][:, :])
            for n in range(8):
                if n >= 4:
                    act.wait_ge(s["score_used"], n - 3)
                c = (n // 4 + 1) * P
                copy_bank(P_SC + n, rl[:, n % 4, :, 0:c], by_head_pair(P_SC + n, P)[:, :, 0:c], scale=IDX ** -0.5, func=ACT.Relu)
            for pr in range(4):
                copy_bank(P_ROW + pr, rows[:, 2 * pr:2 * pr + 2, :], by_head_pair(P_ROW + pr, P))
            for step in range(len(ATT_UNITS) + 1):
                if step < len(ATT_UNITS):
                    br, t, pr = ATT_UNITS[step]
                    act.wait_ge(s["lg_done"], step + 1)
                    for f, h in enumerate(att_heads(br, pr)):
                        part = lg[:, step % 4, f, 0:(t + 1) * P]
                        c = (2 * br + t) * H + h
                        A_(part, part, ACT.Exp, bias=amax[:, 2 * step + f:2 * step + f + 1],
                           accum_out=ssum[:, c:c + 1]).then_inc(s["exp_done"], 1)
                if step >= 1:
                    br, t, pr = ATT_UNITS[step - 1]
                    p = att_pair(1, step - 1)
                    act.wait_ge(s["pair_ready"], p + 1)
                    if step - 1 >= 4:
                        act.wait_ge(s["pv_ready"], step - 4)
                    src = bank[p % 4][:, :].rearrange("p (f b c) -> p f b c", f=2, b=2)[:, :, 0:t + 1, :]
                    dst = pT[:, (step - 1) % 4, :].rearrange("p (f b c) -> p f b c", f=2, b=2)[:, :, 0:t + 1, :]
                    A_(dst, src, ACT.Copy).then_inc(bank_free[p % 4], 1)
            for c in range(4):
                br, t = 1 - c // 2, c % 2
                act.wait_ge(s["orow_done"], c + 1)
                chain.wait()
                chain(A_(junk[:, 0:BANK], xn[:, t, br * BANK:(br + 1) * BANK], ACT.Square, accum_out=stat[:, 16 + c:17 + c]))
            chain.wait()
            A_(stat[:, 20:24], stat[:, 16:20], ACT.Sqrt, scale=1.0 / BANK, bias=eps[:, 0:1]).then_inc(s["oss_done"], 1)
            norm_evac(3, lambda k: vcol("g_out_a_2" if k < 4 else "g_out_b_2", k % 4))
            norm_stats(4, "x3_done", 4)
            norm_evac(4, lambda k: 1.0)
            for pr in range(4):
                copy_bank(P_PQ + pr, qpT[:, 2 * pr:2 * pr + 2, :], by_head_pair(P_PQ + pr, P))
            for n in range(8):
                t, q, half = n // 4, n // 2 % 2, n % 2
                g = half * H + 4 * q
                copy_bank(P_PS + n, scr[:, t, g:g + 4, :], bank[(P_PS + n) % 4][:, :].rearrange("p (h c) -> p h c", h=4))
            for part in range(PARTS):
                act.wait_ge(s["best_done"], part + 1)
                mine = gsoft[:, part // 2, part % 2 * P // 2:(part % 2 + 1) * P // 2]
                A_(mine, mine, ACT.Exp).then_inc(s["soft_done"], 1)
            for t in range(NT):
                act.wait_ge(s["score_out"], 1 + (t + 1) * P // RING)
                A_(wgt[:, t, :], dots[:, t, :], ACT.Gelu).then_inc(s["gelu_done"], 1)
            per = RING - RING // ON_DVE
            act.wait_ge(s["weight_done"], NT)
            for t in range(NT):
                with act.Fori(0, P // RING) as it:
                    for c in range(RING):
                        if c % ON_DVE == ON_DVE - 1:
                            continue
                        q = c - c // ON_DVE
                        act.wait_ge(s["pe_used"], it * per + (t * P // RING * per + q + 1))
                        A_(diag[:, q, :], ident, ACT.Copy,
                           scale=wgt[:, t, bass.ds(it * RING + c, 1)]).then_inc(s["diag_done"], 1)
            norm_stats(5, "x_final", 4)

        @block.vector
        def _(dve):
            chain = Chain(dve, s["dve_chain"])
            V = nc.vector

            def norm_rows(n):
                dve.wait_ge(s["rt_done"], n + 1)
                chain(V.reciprocal(stat[:, 6:8], stat[:, 4:6]))
                chain.wait()
                for t in range(NT):
                    V.tensor_scalar(xn[:, t, :], x[:, t, :], stat[:, 6 + t:7 + t], None, ALU.mult).then_inc(s["xn_done"], 1)

            def norm_evac(n, scale, bias=None):
                for b in range(2, 4):
                    dve.wait_ge(s["tr_done"], 4 * n + b + 1)
                    for f in range(2):
                        k = 2 * b + f
                        V.tensor_scalar(hT[:, k, :], bank[4 + b][:, f * S:(f + 1) * S], scale(k),
                                        bias(k) if bias else None, ALU.mult,
                                        ALU.add if bias else ALU.bypass).then_inc(s["hTd"], 1)

            def conv(dst, src, taps, name, f0, tiles, done):
                for j in range(taps - 1, -1, -1):
                    back = taps - 1 - j
                    if back:
                        chain.wait()
                    for n in range(2):
                        w = vcol(name, j * tiles + f0[n])
                        if back == 0:
                            ins = V.tensor_scalar(dst[:, n, :], src[:, n, :], w, None, ALU.mult)
                        else:
                            ins = V.scalar_tensor_tensor(out=dst[:, n, back:S], in0=src[:, n, 0:S - back], scalar=w,
                                                         in1=dst[:, n, back:S], op0=ALU.mult, op1=ALU.add)
                        if back == taps - 1 and n == 1 and done is not None:
                            ins.then_inc(done, 1)
                        else:
                            chain(ins)

            def pair(p):
                dve.wait_ge(s["pair_ready"], p + 1)
                return bank[p % 4][:, :].rearrange("p (u s) -> p u s", u=2)

            def route(part):
                t, q = divmod(part, 2)
                h0, HP = 4 * q, H // 2
                cols = slice(h0 * PK, (h0 + HP) * PK)
                groups = [half * H + h0 + i for half in range(2) for i in range(HP)]

                def sixteen(rows_of, top_v, top_i, each):
                    for at in range(2):
                        for g in each:
                            chain(V.max(top_v(g)[:, 8 * at:8 * at + 8], rows_of(g)))
                        chain.wait()
                        for g in each:
                            chain(V.max_index(top_i(g)[:, 8 * at:8 * at + 8], top_v(g)[:, 8 * at:8 * at + 8], rows_of(g)))
                        if at == 0:
                            chain.wait()
                            for g in each:
                                chain(V.match_replace(rows_of(g), top_v(g)[:, 0:8], rows_of(g), FAR))
                        chain.wait()

                for half in range(2):
                    p = P_PS + 2 * part + half
                    dve.wait_ge(bank_free[p % 4], p // 4 + 1)
                sixteen(lambda g: scr[:, t, g, :], lambda g: top[:, t, g, :], lambda g: topi[:, t, g, :], groups)
                for half in range(2):
                    g = half * H + h0
                    chain(V.tensor_copy(topf[:, t, g:g + HP, :], topi[:, t, g:g + HP, :]))
                sums = cand[:, h0:h0 + HP, :].rearrange("p h (a b) -> p h a b", a=PK)
                chain(V.tensor_tensor(sums, top[:, t, h0:h0 + HP, :].unsqueeze(3).to_broadcast([P, HP, PK, PK]),
                                      top[:, t, H + h0:H + h0 + HP, :].unsqueeze(2).to_broadcast([P, HP, PK, PK]), ALU.add))
                chain.wait()
                b3 = best[:, t, :].rearrange("p (h k) -> p h k", h=H)
                p3 = bpos[:, t, :].rearrange("p (h k) -> p h k", h=H)
                sixteen(lambda h: cand[:, h, :], lambda h: b3[:, h, :], lambda h: p3[:, h, :], range(h0, h0 + HP))
                g3 = gsoft[:, t, cols].rearrange("p (h k) -> p h k", h=HP)
                b4 = best[:, t, cols].rearrange("p (h k) -> p h k", h=HP)
                V.tensor_tensor(g3, b4, b4[:, :, 0:1].to_broadcast([P, HP, PK]), ALU.subtract).then_inc(s["best_done"], 1)
                chain(V.tensor_scalar(babu[:, 0, t, cols], bpos[:, t, cols], 4, None, ALU.logical_shift_right))
                chain(V.tensor_scalar(babu[:, 1, t, cols], bpos[:, t, cols], 15, None, ALU.bitwise_and))
                chain.wait()
                chain(V.tensor_copy(babf[:, :, t, cols], babu[:, :, t, cols]))
                chain.wait()
                iota = cst[:, C_IOTA:C_IOTA + PK]
                flats = [hot[:, half * P // 2 * PK:(half + 1) * P // 2 * PK] for half in range(2)]
                for half in range(2):
                    chain(V.tensor_tensor(flats[half].rearrange("p (j a) -> p j a", a=PK),
                                          babf[:, half, t, cols].unsqueeze(2).to_broadcast([P, P // 2, PK]),
                                          iota.unsqueeze(1).to_broadcast([P, P // 2, PK]), ALU.is_equal))
                chain.wait()
                for half in range(2):
                    four = flats[half].rearrange("p (h k a) -> p h k a", h=HP, k=PK)
                    g = half * H + h0
                    chain(V.tensor_tensor(four, four, topf[:, t, g:g + HP, :].unsqueeze(2)
                                          .to_broadcast([P, HP, PK, PK]), ALU.mult))
                chain.wait()
                for half in range(2):
                    chain(V.tensor_reduce(pick[:, half, t, cols], flats[half].rearrange("p (j a) -> p j a", a=PK), AX.X, ALU.add))
                chain.wait()
                chain(V.scalar_tensor_tensor(out=pick[:, 0, t, cols], in0=pick[:, 0, t, cols], scalar=float(P),
                                             in1=pick[:, 1, t, cols], op0=ALU.mult, op1=ALU.add))
                chain.wait()
                V.tensor_copy(eid[:, t, cols], pick[:, 0, t, cols]).then_inc(s["eid_done"], 1)
                dve.wait_ge(s["soft_done"], part + 1)
                chain(V.tensor_reduce(stat[:, 32:32 + HP], g3, AX.X, ALU.add))
                chain.wait()
                chain(V.reciprocal(stat[:, 40:40 + HP], stat[:, 32:32 + HP]))
                chain.wait()
                ins = V.tensor_tensor(g3, g3, stat[:, 40:40 + HP].unsqueeze(2).to_broadcast([P, HP, PK]), ALU.mult)
                if part == 0:
                    ins.then_inc(s["slot_free"], RING)
                else:
                    chain(ins)
                    chain.wait()

            V.memset(eps[:, 0:1], EPS).then_inc(s["dve_chain"], 1)
            chain.n += 1
            V.memset(eps[:, 1:2], EPS * P).then_inc(s["eps_done"], 1)
            ang, turns = trig[:, 0, :].rearrange("p (t n) -> p t n", t=NT), trig[:, 1, :].rearrange("p (t n) -> p t n", t=NT)
            dve.wait_ge(s["vec_in"], 16 * VEC_DMAS)
            chain(V.tensor_copy(trig[:, 2, 0:NT], posi[:, :]))
            chain.wait()
            for n in range(12):
                width, i = (ROPE, n) if n < 8 else (IROPE, n - 8)
                inv = float(np.float32(THETA) ** np.float32(-2.0 * i / width))
                chain(V.tensor_scalar(ang[:, :, n], trig[:, 2, 0:NT], inv, None, ALU.mult))
            chain.wait()
            magic = 1.5 * 2.0 ** 23
            first, last = slice(0, 12), slice(12, 24)
            chain(V.tensor_scalar(turns[:, :, first], ang[:, :, first], 1.0 / sum(TWO_PI), magic, ALU.mult, ALU.add))
            chain.wait()
            chain(V.tensor_scalar(turns[:, :, first], turns[:, :, first], magic, None, ALU.subtract))
            chain.wait()
            for part in TWO_PI:
                chain(V.scalar_tensor_tensor(out=ang[:, :, first], in0=turns[:, :, first], scalar=-part, in1=ang[:, :, first],
                                             op0=ALU.mult, op1=ALU.add))
                chain.wait()
            chain(V.tensor_scalar(ang[:, :, last], ang[:, :, first], np.pi / 2, None, ALU.add))
            chain.wait()
            chain(V.tensor_scalar(turns[:, :, first], ang[:, :, last], np.pi, -2 * np.pi, ALU.is_gt, ALU.mult))
            chain.wait()
            chain(V.tensor_tensor(ang[:, :, last], ang[:, :, last], turns[:, :, first], ALU.add))
            chain.wait()
            V.tensor_scalar(trig[:, 0, :], trig[:, 0, :], 3.1415925, -3.1415925, ALU.min, ALU.max).then_inc(s["angle_done"], 1)
            norm_rows(0)
            dve.wait_ge(s["vt_ready"], 1)
            V.tensor_copy(vec[:, 0:VROWS], bank[0][:, 0:VROWS]).then_inc(s["vt_done"], 1)
            dve.wait_ge(s["vt_done"], 1)
            norm_evac(0, lambda k: vcol("norm_mix_g", k))
            for p in range(12):
                src = pair(p)
                if p >= 2:
                    dve.wait_ge(s["silu_done"], p - 1)
                conv(raw[:, p % 2, :, :], src, 4, "gdn_conv_w", (2 * p, 2 * p + 1), 24, bank_free[p % 4])
            dve.wait_ge(s["ab_ready"], 1)
            chain(V.tensor_scalar(small[:, 0, :], bank[4][0:H, 0:S], gate_par[:, 1:2], None, ALU.add))
            chain.wait()
            chain(V.tensor_scalar(small[:, 4, :], small[:, 0, :], -1.0, None, ALU.mult))
            chain.wait()
            V.tensor_tensor(small[:, 1, :], small[:, 0, :], small[:, 4, :], ALU.min).then_inc(s["ab_dve"], 1)
            dve.wait_ge(s["ab_act"], 1)
            chain(V.scalar_tensor_tensor(out=small[:, 5, :], in0=small[:, 0, :], scalar=0.0, in1=small[:, 3, :],
                                         op0=ALU.max, op1=ALU.add))
            chain(V.tensor_scalar(small[:, 7, :], small[:, 7, :], 1.0, None, ALU.add))
            chain.wait()
            chain(V.tensor_scalar(small[:, 5, :], small[:, 5, :], gate_par[:, 2:3], -1.0, ALU.mult, ALU.mult))
            chain(V.reciprocal(small[:, 7, :], small[:, 7, :]))
            chain.wait()
            for t in range(NT):
                ins = V.tensor_tensor_scan(small[:, 6, t * P:(t + 1) * P], ones[0:H, :], small[:, 5, t * P:(t + 1) * P],
                                           0.0, ALU.mult, ALU.add)
                if t == NT - 1:
                    ins.then_inc(s["gates_done"], 1)
                else:
                    chain(ins)
            dve.wait_ge(s["gt_ready"], 1)
            V.tensor_copy(Gtok[:, :, :], bank[4][:, 0:32].rearrange("p (t c) -> p t c", t=NT)).then_inc(s["gt_done"], 1)
            for n, buf in ((0, qT), (1, kT)):
                flat = buf.rearrange("p f s -> p (f s)")
                for b in range(4):
                    dve.wait_ge(s["sqrt_done"], 4 * n + b + 1)
                    c = slice(b * BANK, (b + 1) * BANK)
                    chain(V.reciprocal(rn[:, c], rn[:, c]))
                    chain.wait()
                    V.tensor_tensor(flat[:, c], flat[:, c], rn[:, c], ALU.mult).then_inc(s["qk_done"], 1)

            def convolved(p, half):
                for i in range(2):
                    src = pair(p + i)
                    part = ya[:, 4 * half + 2 * i:4 * half + 2 * i + 2, :]
                    dve.wait_ge(bank_free[(p + i - 2) % 4], (p + i - 2) // 4 + 1)
                    chain.wait()
                    V.tensor_tensor(t1, src, part, ALU.mult).then_inc(bank_free[(p + i) % 4], 1)
                    dve.wait_ge(bank_free[(p + i) % 4], (p + i) // 4 + 1)
                    f = 4 * half + 2 * i
                    conv(part, t1, 3, "conv_a_w", (f, f + 1), 8, None)
                chain.wait()
                for i in range(2):
                    src = pair(p + 2 + i)
                    part = ya[:, 4 * half + 2 * i:4 * half + 2 * i + 2, :]
                    V.tensor_tensor(part, src, part, ALU.mult).then_inc(bank_free[(p + 2 + i) % 4], 1)

            convolved(18, 0)
            for b in range(4):
                dve.wait_ge(s["qd_done"], b + 1)
                for f in range(2):
                    for t in range(NT):
                        ins = V.tensor_scalar(DT[:, t * H + 2 * b + f, :], bank[4 + b][:, f * S + t * P:f * S + (t + 1) * P],
                                              Gtok[:, t, 2 * b + f:2 * b + f + 1], 0.0, ALU.subtract, ALU.min)
                        if f == 1 and t == NT - 1:
                            ins.then_inc(s["row_done"], 1)
                        else:
                            chain(ins)
            mask = cst[:, C_STRICT:C_STRICT + P].unsqueeze(1).to_broadcast([P, NT * H, P])
            for b in range(4):
                dve.wait_ge(s["dexp_done"], b + 1)
                dve.wait_ge(s["row_ready"], 4 + b + 1)
                for t in range(NT):
                    c = slice(t * H + 2 * b, t * H + 2 * b + 2)
                    ins = V.tensor_tensor(LT[:, c, :], DT[:, c, :],
                                          bank[4 + b][:, :].rearrange("p (h s) -> p h s", h=2)[:, :, t * P:(t + 1) * P], ALU.mult)
                    if t == NT - 1:
                        ins.then_inc(s["row_done"], 1)
                    else:
                        chain(ins)
            dve.wait_ge(s["row_done"], 8)
            chain(V.tensor_tensor(LT, LT, mask, ALU.mult))
            dve.wait_ge(s["eg_done"], 1)
            chain(V.tensor_tensor(kbs[:, :], egt[:, :], Gtok[:, 1, H:2 * H], ALU.mult))
            dve.wait_ge(s["qd_done"], 4)
            for h0 in (0, 4):
                chain(V.tensor_tensor(qd[:, h0:h0 + 4, :], qd[:, h0:h0 + 4, :], qT[:, h0:h0 + 4, P:S], ALU.mult))
            convolved(24, 1)
            chain.wait()
            for n in range(8):
                g = n % 4
                t, h0 = g // 2, 4 * (g % 2)
                dve.wait_ge(s["tok_ready"], n + 1)
                src = bank[4 + g][:, :].rearrange("p (h c) -> p h c", h=4)
                if n < 4:
                    scale, dst = Gtok[:, t, H + h0:H + h0 + 4], Vb[:, 4 * g:4 * g + 4, :]
                elif t == 0:
                    scale, dst = DT[:, h0:h0 + 4, P - 1], Kd[:, h0:h0 + 4, :]
                else:
                    scale, dst = kbs[:, h0:h0 + 4], Kb[:, h0:h0 + 4, :]
                V.tensor_tensor(dst, src, scale.unsqueeze(2).to_broadcast([P, 4, P]), ALU.mult).then_inc(s["tok_done"], 1)
            dve.wait_ge(s["tok_done"], 6)
            incl = cst[:, C_INCL:C_INCL + P].unsqueeze(1).to_broadcast([P, NT * H, P])
            chain(V.tensor_tensor(DT, DT, incl, ALU.mult))
            chain.wait()
            for n in range(8):
                dve.wait_ge(s["kk_ready"], n + 1)
                g = n % 4
                buf = LT if n < 4 else DT
                V.tensor_tensor(buf[:, 4 * g:4 * g + 4, :], bank[4 + g][:, :].rearrange("p (h c) -> p h c", h=4),
                                buf[:, 4 * g:4 * g + 4, :], ALU.mult).then_inc(s["kk_done"], 1)
            eye = ident.unsqueeze(1).to_broadcast([P, 4, P])
            for lv in range(LEVELS):
                for g in range(4):
                    c = slice(4 * g, 4 * g + 4)
                    src = bank[4 + g][:, :].rearrange("p (h c) -> p h c", h=4)
                    srcT = bank[g][:, :].rearrange("p (h c) -> p h c", h=4)
                    if lv == 0:
                        dve.wait_ge(s["lq_ready"], g + 1)
                        chain(V.tensor_tensor(XT[:, c, :], eye, Loff[:, c, :], ALU.subtract))
                        V.tensor_tensor(X[:, c, :], eye, src, ALU.subtract).then_inc(s["x_done"], 1)
                    else:
                        dve.wait_ge(s["ld_ready"], 4 * (lv - 1) + g + 1)
                        if lv < LEVELS - 1:
                            chain(V.tensor_tensor(X[:, c, :], X[:, c, :], src, ALU.subtract))
                        V.tensor_tensor(XT[:, c, :], XT[:, c, :], srcT, ALU.subtract).then_inc(s["x_done"], 1)
            for g in range(2):
                dve.wait_ge(s["ws_ready"], g + 1)
                dve.wait_ge(s["u_done"], 3 + g)
                c = slice(H + 4 * g, H + 4 * g + 4)
                V.tensor_tensor(u[:, c, :], u[:, c, :], bank[g][:, :].rearrange("p (h c) -> p h c", h=4),
                                ALU.subtract).then_inc(s["vn_done"], 1)
            for p in range(36, 40):
                part = sga[:, 2 * (p - 36):2 * (p - 36) + 2, :]
                V.tensor_tensor(part, pair(p), part, ALU.mult).then_inc(bank_free[p % 4], 1)
            flat, zflat = oT.rearrange("p f s -> p (f s)"), zT.rearrange("p f s -> p (f s)")
            dve.wait_ge(s["o_done"], 4)
            for b in range(4):
                dve.wait_ge(s["osqrt_done"], b + 1)
                c = slice(b * BANK, (b + 1) * BANK)
                chain(V.reciprocal(rn[:, c], rn[:, c]))
                chain.wait()
                chain(V.scalar_tensor_tensor(out=rn[:, c], in0=rn[:, c], scalar=vcol("gdn_norm_g", 0), in1=zflat[:, c],
                                             op0=ALU.mult, op1=ALU.mult))
                chain.wait()
                V.tensor_tensor(flat[:, c], flat[:, c], rn[:, c], ALU.mult).then_inc(s["y_done"], 1)
            for p in range(40, 44):
                c = slice(2 * (p - 40), 2 * (p - 40) + 2)
                V.tensor_tensor(sgb[:, c, :], pair(p), sgb[:, c, :], ALU.mult).then_inc(bank_free[p % 4], 1)
                dve.wait_ge(bank_free[p % 4], p // 4 + 1)
                V.tensor_tensor(sgb[:, c, :], sgb[:, c, :], sga[:, c, :], ALU.add).then_inc(s["mix_done"], 1)

            def add_to_x(ready, counts, done):
                for n in range(2):
                    for t in range(NT):
                        dve.wait_ge(s[ready], counts[2 * n + t])
                        c = slice(n * BANK, (n + 1) * BANK)
                        V.tensor_tensor(x[:, t, c], x[:, t, c], bank[4 + 2 * n + t][:, :], ALU.add).then_inc(s[done], 1)

            add_to_x("wo_ready", (1, 2, 3, 4), "x1_done")
            dve.wait_ge(s["x1_done"], 4)
            norm_rows(1)
            norm_evac(1, lambda k: vcol("norm_ffn_g", k))
            for m in range(UPS):
                for g in range(2):
                    p = up_pair(m, g)
                    src = pair(p)
                    if m >= 2:
                        dve.wait_ge(s["act_done"], m - 1)
                    conv(raw2[:, (2 * m + g) % 4, :, :], src, 3, "ffn_conv_w", (g * FT + 2 * m, g * FT + 2 * m + 1), 2 * FT,
                         bank_free[p % 4])
                for j in ADA_AT.get(m, ()):
                    dve.wait_ge(s["c_done"], 1)
                    dve.wait_ge(s["acc_in"], 16)
                    dve.wait_ge(ada_in[j % 2], 16 * (j // 2 + 1))
                    part = acc[:, j * BANK:(j + 1) * BANK]
                    for k in range(KT):
                        ins = V.scalar_tensor_tensor(out=part, in0=ada[j % 2][:, k, :], scalar=csil[:, k:k + 1], in1=part,
                                                     op0=ALU.mult, op1=ALU.add)
                        if k == KT - 1:
                            ins.then_inc(s["ada_used"], 1)
                        else:
                            chain(ins)
                            chain.wait()
                if m == UPS - 2:
                    dve.wait_ge(s["pair_ready"], MOD0 + 9)
                    src = bank[(MOD0 + 8) % 4]
                    chain(V.tensor_copy(modc[:, 0, :], src[:, 0:KT]))
                    c = VEC["g_mix_2"][0]
                    V.scalar_tensor_tensor(out=modc[:, 1, :], in0=src[:, KT:2 * KT], scalar=1.0, in1=vec[:, c:c + KT],
                                           op0=ALU.add, op1=ALU.mult).then_inc(bank_free[(MOD0 + 8) % 4], 1)
            add_to_x("down_ready", (UPS,) * 4, "x2_done")
            dve.wait_ge(s["x2_done"], 4)
            norm_rows(2)
            dve.wait_ge(s["xn_done"], 6)
            dve.wait_ge(s["row_in"], 16)
            for t in range(NT):
                V.tensor_tensor(x[:, t, :], xn[:, t, :], nfg, ALU.mult).then_inc(s["fin_done"], 1)
            norm_rows(3)
            norm_evac(2, lambda k: modc[:, 1, k:k + 1], lambda k: modc[:, 0, k:k + 1])
            p = PAIR0 + 2
            dve.wait_ge(s["pair_ready"], p + 1)
            V.tensor_scalar(rp[:, :, 0:H, :], bank[p % 4][:, 0:S].rearrange("p (t h n) -> p t h n", t=NT, h=H), 0.125, None,
                            ALU.mult).then_inc(bank_free[p % 4], 1)
            dve.wait_ge(bank_free[p % 4], p // 4 + 1)
            for t in range(NT):
                dve.wait_ge(bank_free[(PAIR0 + t) % 4], (PAIR0 + t) // 4 + 1)
            chain(V.tensor_copy(rp[:, :, H, :], tokp[:, :, P:P + ROPE]))
            dve.wait_ge(s["sin_done"], 1)
            tri = trig[:, 3, :].rearrange("p (t n) -> p t n", t=NT)

            def rotate(buf, half, at):
                x1, x2 = buf[:, :, :, 0:half], buf[:, :, :, half:2 * half]
                shape = [P, NT, H + 1, half]
                sin = tri[:, :, at:at + half].unsqueeze(2).to_broadcast(shape)
                cos = tri[:, :, 12 + at:12 + at + half].unsqueeze(2).to_broadcast(shape)
                tmp = [rtmp[:, m, 0:NT * (H + 1) * half].rearrange("p (t h n) -> p t h n", t=NT, h=H + 1) for m in range(4)]
                chain.wait()
                for m, (a, b) in enumerate(((x1, cos), (x2, sin), (x2, cos), (x1, sin))):
                    chain(V.tensor_tensor(tmp[m], a, b, ALU.mult))
                chain.wait()
                chain(V.tensor_tensor(x1, tmp[0], tmp[1], ALU.subtract))
                V.tensor_tensor(x2, tmp[2], tmp[3], ALU.add).then_inc(s["rope_done"], 1)

            rotate(rp, ROPE // 2, 0)
            dve.wait_ge(s["rope_done"], 1)
            rotate(tokp[:, :, 144:432].rearrange("p t (h n) -> p t h n", n=IDX), IROPE // 2, 8)
            dve.wait_ge(s["rope_done"], 2)
            chain(V.tensor_copy(ikrep.rearrange("p t (r n) -> p t r n", r=4),
                                tokp[:, :, 400:432].unsqueeze(2).to_broadcast([P, NT, 4, IDX])))
            chain(V.tensor_scalar(iws[:, :, :], tokp[:, :, 432:440], H ** -0.5, None, ALU.mult))
            dve.wait_ge(s["lat_rt"], 1)
            chain(V.reciprocal(stat[:, 12:14], stat[:, 10:12]))
            chain.wait()
            for t in range(NT):
                ins = V.tensor_scalar(latn[:, t, :], tokp[:, t, 0:P], stat[:, 12 + t:13 + t], None, ALU.mult)
                if t:
                    ins.then_inc(s["lat_done"], 1)
                else:
                    chain(ins)
            p = PAIR0 + 13
            dve.wait_ge(s["pair_ready"], p + 1)
            V.tensor_scalar(small[:, 0, :], bank[p % 4][0:H, 0:S], gate_par[:, 3:4], -1.0, ALU.add,
                            ALU.mult).then_inc(bank_free[p % 4], 1)
            dve.wait_ge(bank_free[p % 4], p // 4 + 1)
            chain(V.tensor_scalar(small[:, 4, :], small[:, 0, :], -1.0, None, ALU.mult))
            chain.wait()
            V.tensor_tensor(small[:, 1, :], small[:, 0, :], small[:, 4, :], ALU.min).then_inc(s["fb_dve"], 1)
            dve.wait_ge(s["fb_act"], 1)
            chain(V.scalar_tensor_tensor(out=small[:, 5, :], in0=small[:, 0, :], scalar=0.0, in1=small[:, 3, :],
                                         op0=ALU.max, op1=ALU.add))
            chain.wait()
            for t in range(NT):
                ins = V.tensor_tensor_scan(small[:, 6, t * P:(t + 1) * P], ones[0:H, :], small[:, 5, t * P:(t + 1) * P],
                                           0.0 if t == 0 else small[:, 6, P - 1:P], ALU.mult, ALU.add)
                if t:
                    ins.then_inc(s["cum_done"], 1)
                else:
                    chain(ins)
                    chain.wait()
            for n in range(8):
                t, j = divmod(n, 4)
                p = P_SC + n
                dve.wait_ge(bank_free[p % 4], p // 4 + 1)
                part = score[:, t, 0:(t + 1) * P]
                for b in range(2):
                    src = rl[:, n % 4, b, 0:(t + 1) * P]
                    w = iws[:, t, 4 * b + j:4 * b + j + 1]
                    if j == 0 and b == 0:
                        ins = V.tensor_scalar(part, src, w, None, ALU.mult)
                    else:
                        ins = V.scalar_tensor_tensor(out=part, in0=src, scalar=w, in1=part, op0=ALU.mult, op1=ALU.add)
                    if b:
                        ins.then_inc(s["score_used"], 1)
                        dve.wait_ge(s["score_used"], n + 1)
                    else:
                        chain(ins)
                        chain.wait()
            neg = [cst[:, C_NEG + t * S:C_NEG + t * S + (t + 1) * P] for t in range(NT)]
            for t in range(NT):
                chain(V.tensor_tensor(work[:, t, 0:(t + 1) * P], score[:, t, 0:(t + 1) * P], neg[t], ALU.add))
            chain.wait()

            def take_round():
                for t in range(NT):
                    chain(V.max(top8[:, t, :], work[:, t, 0:(t + 1) * P]))
                chain.wait()
                for t in range(NT):
                    part = work[:, t, 0:(t + 1) * P]
                    chain(V.match_replace(part, top8[:, t, :], part, FAR))
                chain.wait()

            U = len(ATT_UNITS)
            for n in range(U):
                br, t, pr = ATT_UNITS[n]
                c = (t + 1) * P
                if n == U // 2:
                    for tt in range(NT):
                        chain(V.tensor_scalar(negA[:, tt, 0:(tt + 1) * P], work[:, tt, 0:(tt + 1) * P], -2e38, BIG,
                                              ALU.is_le, ALU.mult))
                    chain.wait()
                    for tt in range(NT):
                        part = negA[:, tt, 0:(tt + 1) * P]
                        chain(V.scalar_tensor_tensor(out=part, in0=part, scalar=-BIG, in1=neg[tt], op0=ALU.add, op1=ALU.add))
                    chain.wait()
                p = att_pair(0, n)
                dve.wait_ge(s["pair_ready"], p + 1)
                if n >= 4:
                    dve.wait_ge(s["pair_ready"], att_pair(1, n - 4) + 1)
                src = bank[p % 4][:, :].rearrange("p (u s) -> p u s", u=2)[:, :, 0:c]
                dst = lg[:, n % 4, :, 0:c]
                if br:
                    h = att_heads(br, pr)[0]
                    dve.wait_ge(bank_free[(P_ROW + 3) % 4], (P_ROW + 3) // 4 + 1)
                    V.tensor_tensor(dst, src, rows[:, h:h + 3:2, 0:c], ALU.add).then_inc(bank_free[p % 4], 1)
                    dve.wait_ge(bank_free[p % 4], p // 4 + 1)
                    chain(V.tensor_tensor(dst, dst, neg[t].unsqueeze(1).to_broadcast([P, 2, c]), ALU.add))
                else:
                    V.tensor_tensor(dst, src, negA[:, t, 0:c].unsqueeze(1).to_broadcast([P, 2, c]),
                                    ALU.add).then_inc(bank_free[p % 4], 1)
                    dve.wait_ge(bank_free[p % 4], p // 4 + 1)
                chain.wait()
                V.tensor_reduce(amax[:, 2 * n:2 * n + 2], dst, AX.X, ALU.max, negate=True).then_inc(s["lg_done"], 1)
                if n < TAKE // 8:
                    take_round()
            for c in range(4):
                br, t = 1 - c // 2, c % 2
                dve.wait_ge(s["exp_done"], 8 * (c + 1))
                dve.wait_ge(s["pv_ready"], 4 * (c + 1))
                b = 2 * br + t
                chain(V.reciprocal(ssum[:, 32 + b * H:32 + (b + 1) * H], ssum[:, b * H:(b + 1) * H]))
                chain.wait()
                V.tensor_tensor(xn[:, t, br * BANK:(br + 1) * BANK].rearrange("p (h n) -> p h n", h=H),
                                bank[4 + b][:, :].rearrange("p (h n) -> p h n", h=H),
                                ssum[:, 32 + b * H:32 + (b + 1) * H].unsqueeze(2).to_broadcast([P, H, 64]),
                                ALU.mult).then_inc(s["orow_done"], 1)
            dve.wait_ge(s["oss_done"], 1)
            chain(V.reciprocal(stat[:, 24:28], stat[:, 20:24]))
            chain.wait()
            for c in range(4):
                br, t = 1 - c // 2, c % 2
                part = xn[:, t, br * BANK:(br + 1) * BANK]
                V.tensor_scalar(part, part, stat[:, 24 + c:25 + c], None, ALU.mult).then_inc(s["xn_done"], 1)
            norm_evac(3, lambda k: vcol("g_out_a_2" if k < 4 else "g_out_b_2", k % 4))

            def gated_add(ready, counts, gate, done, more=None):
                for n in range(2):
                    for t in range(NT):
                        c = slice(n * BANK, (n + 1) * BANK)
                        tmp = lg[:, 2 * n + t, :, :].rearrange("p u s -> p (u s)")
                        dve.wait_ge(s[ready], counts[2 * n + t])
                        src = bank[4 + 2 * n + t][:, :]
                        if more is not None:
                            chain(V.tensor_tensor(tmp, src, more[:, t, c], ALU.add))
                            chain.wait()
                            src = tmp
                        chain(V.tensor_tensor(tmp, src, modb[:, gate, c], ALU.mult))
                        chain.wait()
                        V.tensor_tensor(x[:, t, c], x[:, t, c], tmp, ALU.add).then_inc(s[done], 1)

            gated_add("wout_ready", (1, 2, 3, 4), 0, "x3_done")
            dve.wait_ge(s["key_ready"], 1)
            V.tensor_copy(keysT[:, :], bank[4][:, 0:P]).then_inc(s["key_done"], 1)
            dve.wait_ge(s["ffg_in"], 48)
            chain(V.scalar_tensor_tensor(out=modb[:, 2, :], in0=modb[:, 2, :], scalar=1.0, in1=ffg, op0=ALU.add, op1=ALU.mult))
            dve.wait_ge(s["x3_done"], 4)
            dve.wait_ge(s["rt_done"], 5)
            chain(V.reciprocal(stat[:, 6:8], stat[:, 4:6]))
            chain.wait()
            for t in range(NT):
                chain(V.scalar_tensor_tensor(out=xn[:, t, :], in0=x[:, t, :], scalar=stat[:, 6 + t:7 + t], in1=modb[:, 2, :],
                                             op0=ALU.mult, op1=ALU.mult))
            chain.wait()
            for t in range(NT):
                V.tensor_tensor(xn[:, t, :], xn[:, t, :], modb[:, 1, :], ALU.add).then_inc(s["xn_done"], 1)
            norm_evac(4, lambda k: 1.0)
            V.memset(dotst[:, :], 0.0).then_inc(s["score_out"], 1)

            def dots_of(part):
                t, q = divmod(part, 2)
                base = part * TURNS
                with dve.Fori(0, TURNS) as it:
                    for c in range(RING):
                        dve.wait_ge(g_in[c], (it + (base + 1)) * 16)
                        if c == 0:
                            dve.wait_ge(s["score_out"], it + (base + 1))
                        V.tensor_tensor_reduce(gring[c], gring[c], xn[:, t, :], 1.0, 0.0, ALU.mult, ALU.add,
                                               dotst[:, c:c + 1]).then_inc(s["slot_free"], 1)
                    dve.wait_ge(s["slot_free"], (it + (base + 2)) * RING)
                    V.tensor_copy(dots[:, t, bass.ds(it * RING + q * P // 2, RING)], dotst[:, :]).then_inc(s["score_out"], 1)

            route(0)
            for part in range(PARTS):
                if part + 1 < PARTS:
                    route(part + 1)
                dots_of(part)
            for t in range(NT):
                dve.wait_ge(s["gelu_done"], t + 1)
                V.tensor_tensor(wgt[:, t, :], wgt[:, t, :], gsoft[:, t, :], ALU.mult).then_inc(s["weight_done"], 1)
            chain(V.memset(vacc[:, 0, :], 0.0))
            V.memset(vacc[:, 1, :], 0.0).then_inc(s["dve_used"], RING // ON_DVE)
            dve.wait_ge(s["weight_done"], NT)
            for t in range(NT):
                with dve.Fori(0, P // RING) as it:
                    for d in range(RING // ON_DVE):
                        c = ON_DVE * d + ON_DVE - 1
                        dve.wait_ge(g_in[c], (it + (NT * P // RING + t * P // RING + 1)) * 16)
                        dve.wait_ge(s["dve_used"], (it + (t * P // RING + 1)) * (RING // ON_DVE) + d)
                        V.scalar_tensor_tensor(out=vacc[:, t, :], in0=gring[c], scalar=wgt[:, t, bass.ds(it * RING + c, 1)],
                                               in1=vacc[:, t, :], op0=ALU.mult, op1=ALU.add).then_inc(s["dve_used"], 1)
            dve.wait_ge(s["dve_used"], (NT * P // RING + 1) * (RING // ON_DVE))
            gated_add("peer_ready", (1, 2, 1, 2), 3, "x_final", vacc)
            dve.wait_ge(s["x_final"], 4)
            dve.wait_ge(s["rt_done"], 6)
            chain(V.reciprocal(stat[:, 6:8], stat[:, 4:6]))
            dve.wait_ge(s["fin_row_in"], 16)
            chain.wait()
            for t in range(NT):
                V.scalar_tensor_tensor(out=x[:, t, :], in0=x[:, t, :], scalar=stat[:, 6 + t:7 + t], in1=ffg,
                                       op0=ALU.mult, op1=ALU.mult).then_inc(s["final_done"], 1)

        @block.gpsimd
        def _(pool):
            G = nc.gpsimd
            G.memset(tick[:, :], 0.0).then_inc(s["pool_chain"], 1)
            pool.wait_ge(s["pool_chain"], 1)
            for n, buf in ((0, qT), (1, kT)):
                pool.wait_ge(s["silu_done"], 4 * (n + 1))
                if n:
                    pool.wait_ge(s["sum_ready"], 4)
                G.tensor_tensor(sq, buf.rearrange("p f s -> p (f s)"), buf.rearrange("p f s -> p (f s)"),
                                ALU.mult).then_inc(s["sq_done"], 1)
            for lv in range(LEVELS):
                off = cst[:, C_OFF + lv * P:C_OFF + (lv + 1) * P].unsqueeze(1).to_broadcast([P, 4, P])
                for g in range(4):
                    if lv == 0:
                        pool.wait_ge(s["kk_done"], g + 1)
                        pool.wait_ge(bank_free[3], 9)
                        pool.wait_ge(bank_free[2], 9)
                    elif lv == 1:
                        pool.wait_ge(s["x_done"], g + 1)
                    else:
                        pool.wait_ge(s["lq_ready"], 4 * (lv - 1) + g + 1)
                    G.tensor_tensor(Loff[:, 4 * g:4 * g + 4, :], LT[:, 4 * g:4 * g + 4, :], off,
                                    ALU.mult).then_inc(s["loff_done"], 1)
            pool.wait_ge(s["mix_done"], 4)
            G.memset(acc, 0.0).then_inc(s["acc_zero"], 1)
            pool.wait_ge(s["acc_zero"], 1)
            pool.dma_start(acc[0:1, :], A["b_ada_2"]).then_inc(s["acc_in"], 16)
            for m in range(UPS):
                p = up_pair(m, 1)
                pool.wait_ge(s["up_silu"], m + 1)
                pool.wait_ge(bank_free[p % 4], p // 4 + 1)
                G.tensor_tensor(act_ffn[:, 2 * m:2 * m + 2, :], sg[:, m % 2, :, :], raw2[:, (2 * m + 1) % 4, :, :],
                                ALU.mult).then_inc(s["act_done"], 1)

            per = RING - RING // ON_DVE
            for phase, name in ((0, "peer_u_2"), (1, "peer_v_2")):
                for part in range(PARTS):
                    t, q = divmod(part, 2)
                    base = part * TURNS
                    pool.wait_ge(s["eid_done"], part + 1)
                    if phase == 1 and part == 0:
                        pool.wait_ge(s["slot_free"], NT * P + RING)
                        G.memset(zero, 0.0).then_inc(s["zero_done"], 1)
                    with pool.Fori(0, TURNS) as it:
                        for d in range(RING // ON_DVE):
                            c0 = d * ON_DVE
                            if phase == 0:
                                pool.wait_ge(s["slot_free"], (it + base) * RING + (c0 + ON_DVE))
                            else:
                                pool.wait_ge(s["dve_used"], (it + base) * (RING // ON_DVE) + (d + 1))
                                pool.wait_ge(s["pe_used"], (it + base) * per + (d + 1) * (ON_DVE - 1))
                            G.tensor_tensor(tick[:, 0:1], tick[:, 2:3], tick[:, 2:3], ALU.add)
                            G.tensor_copy(eidst[:, c0:c0 + ON_DVE],
                                          eid[:, t, bass.ds(it * RING + (q * P // 2 + c0), ON_DVE)]).then_inc(s["ids_ready"], 1)
                            pool.wait_ge(s["ids_ready"], (it + (phase * NT * P // RING + base)) * (RING // ON_DVE) + (d + 1))
                            G.tensor_tensor(tick[:, 1:2], tick[:, 2:3], tick[:, 2:3], ALU.add)
                            for c in range(c0, c0 + ON_DVE):
                                G.indirect_dma_start(gring[c], None, A[name][0],
                                                     bass.IndirectOffsetOnAxis(ap=eidst[:, c:c + 1],
                                                                               axis=0)).then_inc(g_in[c], 16)


def kernel(**inputs):
    import concourse.bacc as bacc
    from concourse.bass_utils import run_bass_kernel_spmd as run

    nc = bacc.Bacc("TRN2", target_bir_lowering=False, num_devices=1)
    arrays, args = {}, {}
    for name in INPUTS:
        a = np.ascontiguousarray(inputs[name])
        arrays[f"in_{name}"] = a
        args[name] = nc.dram_tensor(f"in_{name}", a.shape, mybir.dt.from_np(a.dtype), kind="ExternalInput").ap()
    arrays["consts"] = constant_table()
    args["consts"] = nc.dram_tensor("consts", (P, C_END), F32, kind="ExternalInput").ap()
    out = nc.dram_tensor("out", (1, S, D), F32, kind="ExternalOutput").ap()
    program(nc, args, out)
    return run(nc, [arrays], core_ids=[0]).results[0]["out"]
```

```python
from contextlib import ExitStack

import numpy as np

import concourse.bass as bass
from concourse import mybir

F32 = mybir.dt.float32
U32 = mybir.dt.uint32
I32 = mybir.dt.int32
ALU = mybir.AluOpType
ACT = mybir.ActivationFunctionType
AX = mybir.AxisListType

P = 128
S = 256
NT = S // P
D = 1024
KT = D // P
H = 8
EPS = 1e-6
FAR = -3e38
NOPE, ROPE, IDX, IROPE = 48, 16, 32, 8
TAKE, PK = 64, 16
THETA = 500000.0
TWO_PI = (6.28125, 0.0019350051879882812, 3.019915981956753e-07)
RING, ON_DVE = 16, 4
FF = 2816
FT = FF // P
BANK = 512
LEVELS = 7
BIG = 1e30

C_ID, C_ONE = 0, P
C_OFF = 2 * P
C_STRICT = C_OFF + LEVELS * P
C_INCL = C_STRICT + P
C_CAUS = C_INCL + P
C_NEG = C_CAUS + NT * S
C_SEL = C_NEG + NT * S
C_IOTA = C_SEL + H * P
C_END = C_IOTA + 16


def constant_table():
    j = np.arange(P)[:, None]
    i = np.arange(P)[None, :]
    t = np.zeros((P, C_END), np.float32)
    t[:, C_ID:C_ID + P] = i == j
    t[:, C_ONE:C_ONE + P] = 1.0
    for s in range(LEVELS):
        w = 1 << s
        t[:, C_OFF + s * P:C_OFF + (s + 1) * P] = (j // (2 * w) == i // (2 * w)) & (j // w != i // w)
    t[:, C_STRICT:C_STRICT + P] = i > j
    t[:, C_INCL:C_INCL + P] = i >= j
    key = np.arange(S)[None, :]
    for n in range(NT):
        seen = key <= n * P + j
        t[:, C_CAUS + n * S:C_CAUS + (n + 1) * S] = seen
        t[:, C_NEG + n * S:C_NEG + (n + 1) * S] = np.where(seen, 0.0, -BIG)
    for h in range(H):
        t[h, C_SEL + h * P:C_SEL + (h + 1) * P] = 1.0
    t[:, C_IOTA:C_IOTA + 16] = np.arange(16)
    return t


VEC = {}
_rows = 0
for _name, _n in (("norm_mix_g", 8), ("conv_a_w", 24), ("gdn_conv_w", 96), ("ffn_conv_w", 132), ("norm_ffn_g", 8),
                  ("g_mix_2", 8), ("g_kv_2", 1), ("g_out_a_2", 4), ("g_out_b_2", 4), ("gdn_norm_g", 1), ("c_2", 8)):
    VEC[_name] = (_rows, _n)
    _rows += _n
VROWS = _rows
VT = -(-VROWS // P)
VEC_PIECES = []
for _name, (_row, _n) in VEC.items():
    _done = 0
    while _done < _n:
        _m = min(_n - _done, P - (_row + _done) % P)
        VEC_PIECES.append((_name, _row + _done, _m, _done))
        _done += _m
VEC_DMAS = len(VEC_PIECES) + 4

HP = 4
PER_TILE = H // HP
PARTS = PER_TILE * NT
PC = HP * PK
TURNS = PC // RING
NS = 3
UPS = FT // 2

INPUTS = """x norm_mix_g w_in conv_a_w gdn_conv_w gdn_A_log gdn_dt_bias gdn_norm_g w_a_out w_b_out w_o norm_ffn_g
w_up ffn_conv_w w_down norm_final_g c_2 positions_2 w_ada_2 b_ada_2 g_mix_2 w_in_2 g_kv_2 w_uk_2 w_uv_2 b_forget_2
g_out_a_2 g_out_b_2 w_out_2 g_ffn_2 w_peer_q_2 peer_keys1_2 peer_keys2_2 peer_u_2 peer_v_2 g_final_2""".split()

SEMAPHORES = """const_in vec_in x_in row_in eps_done vt_ready vt_done rt_done xn_done tr_done hTa hTd pair_ready silu_done
ab_ready ab_dve ab_act gates_done gt_ready gt_done sq_done sum_ready sqrt_done qk_done row_ready row_done
qd_done dexp_done eg_done tok_ready tok_done kk_ready kk_done loff_done lq_ready lq_used ld_ready x_done
u_ready u_done w_ready w_done s1_ready s1_done ws_ready vn_done o_ready o_done osq_done osum_ready
osqrt_done y_done mix_done wo_ready x1_done up_silu act_done down_ready x2_done fin_done out_done dve_chain
act_chain pool_chain c_done acc_zero acc_in ada_used small_in ffg_in fin_row_in angle_done sin_done lat_rt
lat_done rope_done score_used fb_dve fb_act cum_done lg_done exp_done pv_ready orow_done oss_done wout_ready
x3_done best_done soft_done eid_done gelu_done weight_done slot_free ids_ready firstT_ready firstT_done
product_ready wuk_zero score_out diag_done pe_used dve_used peer_ready x_final final_done zero_done""".split()


class Chain:

    def __init__(self, eng, sem):
        self.eng, self.sem, self.n = eng, sem, 0

    def __call__(self, ins):
        ins.then_inc(self.sem, 1)
        self.n += 1

    def wait(self):
        self.eng.wait_ge(self.sem, self.n)


NORM_TURNS = 4
XN_PEER = 12

PAIR0 = 75
P_QB = PAIR0 + 4
P_FB = P_QB + 6
P_IDX = P_FB + 1
P_QR = P_IDX + 2
P_KN = P_QR + 2
P_VA = P_KN + 2
P_SC = P_VA + 2
P_ROW = P_SC + 8
P_ATT = P_ROW + 4
ATT_UNITS = [(br, t, pr) for br in (1, 0) for t in range(NT) for pr in range(4)]
ATT_PAIRS = P_ATT + 2 * len(ATT_UNITS) - P_IDX
P_KEY = P_ATT + 2 * len(ATT_UNITS)
P_PQ = P_KEY + 1
P_END = P_PQ + 6 * NT


def att_pair(kind, n):
    if kind == 0:
        return P_ATT + (0 if n == 0 else 2 * n - 1)
    return P_ATT + (2 * n + 2 if n < len(ATT_UNITS) - 1 else 2 * n + 1)


def att_heads(pr):
    return (4 * (pr % 2) + pr // 2, 4 * (pr % 2) + pr // 2 + 2)


MOD0 = 44 + 2 * (UPS - 1)


def up_pair(m, g):
    return 44 + 2 * m + g + (9 if m == UPS - 1 else 0)


ADA_AT = {1: [0], 2: [1, 2], 3: [3], 4: [4, 5], 5: [6], 6: [7, 8], 7: [9], 8: [10, 11]}


def weight_blocks(A):
    w_in = A["w_in"][0].rearrange("(k p) n -> p k n", p=P)
    at = {"bg": 0, "cg": 1024, "xv": 2048, "q": 3072, "k": 4096, "v": 5120, "z": 6144, "ga": 7184, "gb": 8208}
    out = []
    count = {}

    def add(name, src, k, n, signal, by):
        count[signal] = count.get(signal, 0) + by
        out.append((name, src, k, n, signal, count[signal]))

    def inp(name, half):
        c = at[name] + half * BANK
        add(name, w_in[:, :, c:c + BANK], KT, BANK, "pair_ready", 2)

    for name in ("q", "k", "v"):
        inp(name, 0), inp(name, 1)
    add("ab", w_in[:, :, 7168:7184], KT, 16, "ab_ready", 1)
    inp("z", 0), inp("z", 1)
    for half in range(2):
        for name in ("cg", "xv", "bg"):
            inp(name, half)
    for name in ("ga", "gb"):
        inp(name, 0), inp(name, 1)
    for name, w in (("wa", "w_a_out"), ("wb", "w_b_out"), ("wo", "w_o")):
        for half in range(2):
            src = A[w][0].rearrange("(k p) n -> p k n", p=P)[:, :, half * BANK:(half + 1) * BANK]
            add(name, src, KT, BANK, *(("wo_ready", 3 if half == 0 else 1) if name == "wo" else ("pair_ready", 2)))
    up = A["w_up"][0].rearrange("(k p) (g n) -> p k g n", p=P, g=2)
    down = A["w_down"][0].rearrange("(k p) n -> p k n", p=P)
    for m in range(UPS):
        if m == UPS - 1:
            count["pair_ready"] += 9
        add("up", up[:, :, :, 2 * P * m:2 * P * (m + 1)], KT, 4 * P, "pair_ready", 2)
        if m % 2 == 0 and m >= 2:
            add("down", down[:, 2 * m - 4:2 * m, :], 4, D, "down_ready", 2)
    add("down", down[:, FT - 2:FT, :], 2, D, "down_ready", NT)
    w2 = A["w_in_2"][0].rearrange("(k p) n -> p k n", p=P)
    add("tok", w2[:, :, 512:952], KT, 440, "pair_ready", 2)
    add("qa", w2[:, :, 0:512], KT, BANK, "pair_ready", 2)
    add("qb", w2[:, :, 952:1464], KT, BANK, "pair_ready", 2)
    add("kb", w2[:, :, 1464:1976], KT, BANK, "pair_ready", 2)
    add("vb", w2[:, :, 1976:2488], KT, BANK, "pair_ready", 2)
    add("fb", w2[:, :, 2488:2496], KT, H, "pair_ready", 1)
    count["pair_ready"] += ATT_PAIRS
    for name, w in (("wout", "w_out_2"), ("wpq", "w_peer_q_2")):
        for half in range(2):
            src = A[w][0].rearrange("(k p) n -> p k n", p=P)[:, :, half * BANK:(half + 1) * BANK]
            add(name, src, KT, BANK, *(("wout_ready", 3 if half == 0 else 1) if name == "wout" else ("pair_ready", 2)))
    return out


def program(nc, A, out):
    ctx = ExitStack()
    with ctx:
        def sb(name, shape, dt=F32):
            return ctx.enter_context(nc.sbuf_tensor(name, shape, dt))

        def sem(name):
            return ctx.enter_context(nc.semaphore(name))

        cst = sb("cst", [P, C_END])
        vec = sb("vec", [P, VT * P])
        x = sb("x", [P, NT, D])
        xn = sb("xn", [P, NT, D])
        hT = sb("hT", [P, KT, S])
        wr = [sb(f"wr{i}", [P, KT * BANK]) for i in range(NS)]
        small = sb("small", [H, 8, S])
        gate_par = sb("gate_par", [H, 4])
        stat = sb("stat", [P, 48])
        ssum = sb("ssum", [P, 64])
        Gtok = sb("Gtok", [P, NT, 2 * H])
        kbs = sb("kbs", [P, H])
        egt = sb("egt", [P, H])
        eps = sb("eps", [P, 2])
        arena = sb("arena", [P, 110 * 256])
        bank = [ctx.enter_context(nc.psum_tensor(f"bank{i}", [P, BANK], F32)) for i in range(8)]

        ident = cst[:, C_ID:C_ID + P]
        ones = cst[:, C_ONE:C_ONE + P]

        def region(kb, n):
            return arena[:, kb * 256:kb * 256 + n]

        def tiles(kb):
            return region(kb, 2048).rearrange("p (f s) -> p f s", f=KT)

        def heads16(kb):
            return region(kb, 2048).rearrange("p (e c) -> p e c", e=NT * H)

        def heads8(kb):
            return region(kb, 1024).rearrange("p (h c) -> p h c", h=H)

        vrow = region(0, VT * P).rearrange("p (t c) -> p t c", t=VT)
        qT, kT, vT, zT, sga, sgb, ya = (tiles(8 * i) for i in range(7))
        raw = region(56, 1024).rearrange("p (r u s) -> p r u s", r=2, u=2)
        t1 = region(60, 512).rearrange("p (u s) -> p u s", u=2)
        qd = heads8(56)
        DT, LT, X, XT, Vb = (heads16(62 + 8 * i) for i in range(5))
        Kb, Kd = heads8(102), heads8(106)
        sq, rn = region(70, 2048), region(78, 2048)
        Qs = xn[:, :, :].rearrange("p t (h c) -> p (t h) c", c=P)
        Loff = hT[:, :, :].rearrange("p k (a c) -> p (k a) c", a=2)
        u = heads16(0)
        wT, S1 = heads8(8), heads8(12)
        oT = vT
        act_ffn = region(0, FT * S).rearrange("p (f s) -> p f s", f=FT)
        raw2 = region(22, 2048).rearrange("p (r u s) -> p r u s", r=4, u=2)
        sg = region(30, 1024).rearrange("p (r u s) -> p r u s", r=2, u=2)
        nfg = region(90, D)
        ada = [region(34 + 16 * i, 4096).rearrange("p (k n) -> p k n", k=KT) for i in range(2)]
        acc = region(66, 6 * D)
        csil = sb("csil", [P, KT])
        modc = sb("modc", [P, 2, KT])
        modb = region(34, 4 * D).rearrange("p (m n) -> p m n", m=4)
        qa = region(0, 4 * S).rearrange("p (f s) -> p f s", f=4)
        qtok = region(4, NT * BANK).rearrange("p (t n) -> p t n", t=NT)
        ka = region(8, 4 * S).rearrange("p (f s) -> p f s", f=4)
        tokp = region(25, NT * 440).rearrange("p (t n) -> p t n", t=NT)
        krp = region(29, NT * P).rearrange("p (t f n) -> p t f n", t=NT, f=2)
        rtmp = region(31, 4 * 144).rearrange("p (m n) -> p m n", m=4)
        iqT = region(50, 2 * S).rearrange("p (b s) -> p b s", b=2)
        ikT, latT = region(52, S), region(53, S)
        va = region(54, NT * BANK).rearrange("p (t n) -> p t n", t=NT)
        qb = region(58, 4 * S).rearrange("p (f s) -> p f s", f=4)
        kb = region(62, 4 * S).rearrange("p (f s) -> p f s", f=4)
        lg = region(66, 4 * BANK).rearrange("p (r u s) -> p r u s", r=4, u=2)
        pT = region(74, 4 * BANK).rearrange("p (r c) -> p r c", r=4)
        rl = region(82, 4 * BANK).rearrange("p (r u s) -> p r u s", r=4, u=2)
        latn = region(90, NT * P).rearrange("p (t c) -> p t c", t=NT)
        ikrep = region(91, NT * P).rearrange("p (t c) -> p t c", t=NT)
        work = region(92, NT * S).rearrange("p (t s) -> p t s", t=NT)
        vb = region(94, NT * BANK).rearrange("p (t n) -> p t n", t=NT)
        score = region(98, NT * S).rearrange("p (t s) -> p t s", t=NT)
        negA = region(100, NT * S).rearrange("p (t s) -> p t s", t=NT)
        wuk, wuv = region(106, H * 64).rearrange("p (h n) -> p h n", h=H), region(108, BANK)
        rows = xn[:, :, :].rearrange("p t (h s) -> p (t h) s", s=S)
        posi = sb("posi", [P, NT], I32)
        trig = sb("trig", [P, 4, NT * 24])
        amax = sb("amax", [P, 32])
        iws = sb("iws", [P, NT, H])
        top8 = sb("top8", [P, NT, 8])
        qpT = tiles(0)
        scr = region(8, NT * 2 * H * P).rearrange("p (t g c) -> p t g c", t=NT, g=2 * H)
        cand = region(24, H * S).rearrange("p (h c) -> p h c", h=H)
        hot = region(66, 8 * S)
        keys = region(106, P)
        keysT = sb("keysT", [P, P])
        top = region(74, NT * 256).rearrange("p (t g c) -> p t g c", t=NT, g=2 * H)
        topi = arena[:, 76 * 256:76 * 256 + NT * 256].bitcast(U32).rearrange("p (t g c) -> p t g c", t=NT, g=2 * H)
        topf = region(78, NT * 256).rearrange("p (t g c) -> p t g c", t=NT, g=2 * H)
        best = region(80, NT * P).rearrange("p (t c) -> p t c", t=NT)
        bpos = arena[:, 81 * 256:82 * 256].bitcast(U32).rearrange("p (t c) -> p t c", t=NT)
        babu = arena[:, 82 * 256:84 * 256].bitcast(U32).rearrange("p (m t c) -> p m t c", m=2, t=NT)
        babf = region(84, 512).rearrange("p (m t c) -> p m t c", m=2, t=NT)
        pick = region(86, 512).rearrange("p (m t c) -> p m t c", m=2, t=NT)
        eid = arena[:, 88 * 256:89 * 256].bitcast(U32).rearrange("p (t c) -> p t c", t=NT)
        gsoft = region(89, NT * P).rearrange("p (t c) -> p t c", t=NT)
        dots = region(98, NT * P).rearrange("p (t c) -> p t c", t=NT)
        wgt = region(99, NT * P).rearrange("p (t c) -> p t c", t=NT)
        diag = region(16, 12 * P).rearrange("p (r c) -> p r c", r=12)
        zero = region(107, P)
        firstT = region(94, D).rearrange("p (k c) -> p k c", k=KT)
        vacc = region(0, NT * D).rearrange("p (t n) -> p t n", t=NT)
        dotst = sb("dotst", [P, RING])
        tick = sb("tick", [P, 4])
        eidst = sb("eidst", [P, RING], U32)
        gring = [wr[i // 4][:, (i % 4) * D:(i % 4 + 1) * D] for i in range(12)] + [region(50 + 4 * i, D) for i in range(4)]
        ffg = region(90, D)
        junk = region(102, D)

        s = {n: sem(n) for n in SEMAPHORES}
        ada_in = [sem(f"ada_in{i}") for i in range(2)]
        w_in = [sem(f"w_in{i}") for i in range(NS)]
        g_in = [sem(f"g_in{i}") for i in range(RING)]
        bank_free = [sem(f"bank_free{i}") for i in range(4)]
        blocks = weight_blocks(A)
        landed = [16 * sum(2 if b[0] == "up" else 1 for b in blocks[i % NS:i + 1:NS]) for i in range(len(blocks))]

        def slot(i):
            k, n = blocks[i][2:4]
            return wr[i % NS][:, 0:k * n].rearrange("p (k n) -> p k n", k=k)

        def vcol(name, i):
            c = VEC[name][0] + i
            return vec[:, c:c + 1]

        block = ctx.enter_context(nc.Block())

        @block.sync
        def _(sp):
            sp.dma_start(x[:, :, :], A["x"][0].rearrange("(t p) d -> p t d", p=P)).then_inc(s["x_in"], 16)
            sp.dma_start(cst[:, :], A["consts"][:, :]).then_inc(s["const_in"], 16)
            for name, row, m, r0 in VEC_PIECES:
                flat = A[name]
                while len(flat.shape) > 2:
                    flat = flat.rearrange("a b c -> (a b) c")
                if len(flat.shape) == 1:
                    flat = flat.unsqueeze(0)
                src = flat.rearrange("a (r c) -> (a r) c", c=P)
                t, r = divmod(row, P)
                sp.dma_start(vrow[r:r + m, t, :], src[r0:r0 + m, :]).then_inc(s["vec_in"], 16)
            for i, name in enumerate(("gdn_A_log", "gdn_dt_bias")):
                sp.dma_start(gate_par[:, i:i + 1], A[name].rearrange("a h -> h a")).then_inc(s["vec_in"], 16)
            sp.dma_start(gate_par[:, 3:4], A["b_forget_2"].rearrange("a h -> h a")).then_inc(s["vec_in"], 16)
            sp.dma_start(posi[:, :], A["positions_2"][0].rearrange("(t p) -> p t", p=P),
                         allow_slow_non_contiguous=True).then_inc(s["vec_in"], 16)
            ups = 0
            w_ada = A["w_ada_2"][0].rearrange("(k p) n -> p k n", p=P)
            for i, (name, src, k, cols, _, _) in enumerate(blocks):
                if i >= NS:
                    sp.wait_ge(s[blocks[i - NS][4]], blocks[i - NS][5])
                if name == "up":
                    for g in range(2):
                        half = slot(i)[:, :, g * 2 * P:(g + 1) * 2 * P]
                        sp.dma_start(half, src[:, :, g, :]).then_inc(w_in[i % NS], 16)
                else:
                    sp.dma_start(slot(i), src).then_inc(w_in[i % NS], 16)
                if name == "up":
                    ups += 1
                    for j in ADA_AT.get(ups - 2, ()):
                        if j >= 2:
                            sp.wait_ge(s["ada_used"], j - 1)
                        sp.dma_start(ada[j % 2], w_ada[:, :, j * BANK:(j + 1) * BANK]).then_inc(ada_in[j % 2], 16)
                if name == "fb":
                    sp.wait_ge(s["wuk_zero"], 1)
                    sp.dma_start(wuk[:, :, ROPE:], A["w_uk_2"][0]).then_inc(s["small_in"], 16)
                    sp.dma_start(wuv, A["w_uv_2"][0].rearrange("r h n -> r (h n)")).then_inc(s["small_in"], 16)
                if name == "wpq" and blocks[i - 1][0] != "wpq":
                    sp.wait_ge(s["lg_done"], len(ATT_UNITS))
                    sp.dma_start(ffg, A["g_ffn_2"][0].partition_broadcast(P)).then_inc(s["ffg_in"], 16)
                    for n, key in enumerate(("peer_keys1_2", "peer_keys2_2")):
                        sp.dma_start(keys[:, n * 64:(n + 1) * 64], A[key][0]).then_inc(s["ffg_in"], 16)
                if name == "wo" and blocks[i - 1][0] == "wo":
                    sp.wait_ge(s["mix_done"], 4)
                    sp.dma_start(nfg, A["norm_final_g"].partition_broadcast(P)).then_inc(s["row_in"], 16)
            sp.wait_ge(s["xn_done"], XN_PEER)
            sp.dma_start(ffg, A["g_final_2"].partition_broadcast(P)).then_inc(s["fin_row_in"], 16)
            for t in range(NT):
                sp.wait_ge(s["final_done"], t + 1)
                sp.dma_start(out[0, t * P:(t + 1) * P, :], x[:, t, :]).then_inc(s["out_done"], 16)
            sp.wait_ge(s["out_done"], 16 * NT)

        @block.tensor
        def _(pe):
            pairs = [0]

            def weights(i):
                pe.wait_ge(w_in[i % NS], landed[i])

            def wide(i, act):
                weights(i)
                for half in range(2):
                    p = pairs[0]
                    if p >= 4:
                        pe.wait_ge(bank_free[p % 4], p // 4)
                    for f in range(2):
                        for k in range(KT):
                            c = (2 * half + f) * P
                            mm = nc.tensor.matmul(bank[p % 4][:, f * S:(f + 1) * S], slot(i)[:, k, c:c + P],
                                                  act[:, k, :], start=k == 0, stop=k == KT - 1)
                    mm.then_inc(s["pair_ready"], 1)
                    pairs[0] += 1

            def claim():
                p = pairs[0]
                if p >= 4:
                    pe.wait_ge(bank_free[p % 4], p // 4)
                pairs[0] += 1
                return p

            def modulation():
                for r in range(8):
                    p = claim()
                    c = 2 * D + r * BANK
                    nc.tensor.matmul(bank[p % 4][:, :], ones, acc[:, c:c + BANK], start=True,
                                     stop=True).then_inc(s["pair_ready"], 1)
                p = claim()
                for f in range(2 * KT):
                    mm = nc.tensor.matmul(bank[p % 4][:, f:f + 1], acc[:, f * P:(f + 1) * P], ones[:, 0:1],
                                          start=True, stop=True)
                mm.then_inc(s["pair_ready"], 1)

            def norm_turn(n):
                pe.wait_ge(s["xn_done"], (2, 4, 6, 10)[n])
                for b in range(4):
                    for i in range(4):
                        k, t = 2 * b + i // 2, i % 2
                        mm = nc.tensor.transpose(bank[4 + b][:, i * P:(i + 1) * P], xn[:, t, k * P:(k + 1) * P], ident)
                    mm.then_inc(s["tr_done"], 1)
                pe.wait_ge(s["hTa"], 4 * (n + 1))
                pe.wait_ge(s["hTd"], 4 * (n + 1))

            pe.wait_ge(s["const_in"], 16)
            pe.wait_ge(s["vec_in"], 16 * VEC_DMAS)
            for t in range(VT):
                r = min(P, VROWS - t * P)
                mm = nc.tensor.transpose(bank[0][:, t * P:t * P + r], vrow[0:r, t, :], cst[0:r, C_ID:C_ID + r])
            mm.then_inc(s["vt_ready"], 1)
            pe.wait_ge(s["vt_done"], 1)
            norm_turn(0)
            for i in range(6):
                wide(i, hT)
            weights(6)
            for g in range(2):
                for k in range(KT):
                    mm = nc.tensor.matmul(bank[4][0:H, g * S:(g + 1) * S], slot(6)[:, k, g * H:(g + 1) * H], hT[:, k, :],
                                          start=k == 0, stop=k == KT - 1)
            mm.then_inc(s["ab_ready"], 1)
            wide(7, hT)
            pe.wait_ge(s["gates_done"], 1)
            for g in range(2):
                for t in range(NT):
                    mm = nc.tensor.transpose(bank[4][:, t * 16 + g * H:t * 16 + (g + 1) * H],
                                             small[:, 6 + g, t * P:(t + 1) * P], cst[0:H, C_ID:C_ID + H])
            mm.then_inc(s["gt_ready"], 1)
            pe.wait_ge(s["gt_done"], 1)
            for n in range(2):
                pe.wait_ge(s["sq_done"], n + 1)
                for b in range(4):
                    if n:
                        pe.wait_ge(s["sqrt_done"], b + 1)
                    nc.tensor.matmul(bank[4 + b][:, :], ones, sq[:, b * BANK:(b + 1) * BANK],
                                     start=True, stop=True).then_inc(s["sum_ready"], 1)
                if n == 0:
                    wide(8, hT)
            for i in range(9, 12):
                wide(i, hT)
            for g in range(2):
                for b in range(4):
                    pe.wait_ge(s["sqrt_done"], 5 + b)
                    if g:
                        pe.wait_ge(s["row_done"], b + 1)
                        pe.wait_ge(s["qd_done"], b + 1)
                    for f in range(2):
                        h = 2 * b + f
                        mm = nc.tensor.matmul(bank[4 + b][:, f * S:(f + 1) * S],
                                              cst[0:H, C_SEL + h * P:C_SEL + (h + 1) * P], small[:, 6 + g, :],
                                              start=True, stop=True)
                    mm.then_inc(s["row_ready"], 1)
            for i in range(12, 19):
                wide(i, hT)
            pe.wait_ge(s["row_done"], 8)
            pe.wait_ge(s["qk_done"], 8)
            for n in range(8):
                src, g = (vT, n) if n < 4 else (kT, n - 4)
                t, h0 = g // 2, 4 * (g % 2)
                if n >= 4:
                    pe.wait_ge(s["tok_done"], n - 3)
                for j in range(4):
                    mm = nc.tensor.transpose(bank[4 + g][:, j * P:(j + 1) * P], src[:, h0 + j, t * P:(t + 1) * P], ident)
                mm.then_inc(s["tok_ready"], 1)
            for n in range(8):
                g = n % 4
                t, h0 = g // 2, 4 * (g % 2)
                if n < 4:
                    pe.wait_ge(s["tok_done"], 5 + g)
                else:
                    pe.wait_ge(s["kk_done"], n - 3)
                other = kT if n < 4 else qT
                for j in range(4):
                    mm = nc.tensor.matmul(bank[4 + g][:, j * P:(j + 1) * P], kT[:, h0 + j, t * P:(t + 1) * P],
                                          other[:, h0 + j, t * P:(t + 1) * P], start=True, stop=True)
                mm.then_inc(s["kk_ready"], 1)
            for b in range(4):
                pe.wait_ge(bank_free[b], 9)
            for lv in range(LEVELS):
                for g in range(4):
                    pe.wait_ge(s["loff_done"], 4 * lv + g + 1)
                    if lv == 0:
                        pe.wait_ge(s["kk_done"], 5 + g)
                    else:
                        pe.wait_ge(s["x_done"], 4 * (lv - 1) + g + 1)
                    for e in range(4 * g, 4 * g + 4):
                        o = bank[4 + g][:, (e % 4) * P:(e % 4 + 1) * P]
                        if lv == 0:
                            mm = nc.tensor.transpose(o, Loff[:, e, :], ident)
                        else:
                            mm = nc.tensor.matmul(o, Loff[:, e, :], X[:, e, :], start=True, stop=True)
                    mm.then_inc(s["lq_ready"], 1)
                if lv == 0:
                    continue
                for g in range(4):
                    pe.wait_ge(s["lq_used"], 4 * (lv - 1) + g + 1)
                    for e in range(4 * g, 4 * g + 4):
                        if lv < LEVELS - 1:
                            nc.tensor.matmul(bank[4 + g][:, (e % 4) * P:(e % 4 + 1) * P], XT[:, e, :], Qs[:, e, :],
                                             start=True, stop=True)
                        mm = nc.tensor.matmul(bank[g][:, (e % 4) * P:(e % 4 + 1) * P], Qs[:, e, :], XT[:, e, :],
                                              start=True, stop=True)
                    mm.then_inc(s["ld_ready"], 1)
            for g in range(4):
                pe.wait_ge(s["x_done"], 4 * (LEVELS - 1) + g + 1)
                for e in range(4 * g, 4 * g + 4):
                    mm = nc.tensor.matmul(bank[4 + g][:, (e % 4) * P:(e % 4 + 1) * P], XT[:, e, :], Vb[:, e, :],
                                          start=True, stop=True)
                mm.then_inc(s["u_ready"], 1)

            def by_head(b, lhs, rhs, g):
                for h in range(4 * g, 4 * g + 4):
                    mm = nc.tensor.matmul(bank[b][:, (h % 4) * P:(h % 4 + 1) * P], lhs[:, h, :], rhs[:, h, :],
                                          start=True, stop=True)
                return mm

            for g in range(2):
                by_head(g, Kb, XT[:, H:, :], g).then_inc(s["w_ready"], 1)
            for g in range(2):
                pe.wait_ge(s["u_done"], g + 1)
                by_head(2 + g, Kd, u, g).then_inc(s["s1_ready"], 1)
            for g in range(2):
                by_head(4 + g, u, DT, g).then_inc(s["o_ready"], 1)
            for g in range(2):
                pe.wait_ge(s["s1_done"], g + 1)
                pe.wait_ge(s["w_done"], g + 1)
                by_head(g, wT, S1, g).then_inc(s["ws_ready"], 1)
            for g in range(2):
                pe.wait_ge(s["vn_done"], g + 1)
                for h in range(4 * g, 4 * g + 4):
                    o = bank[6 + g][:, (h % 4) * P:(h % 4 + 1) * P]
                    nc.tensor.matmul(o, S1[:, h, :], qd[:, h, :], start=True, stop=False)
                    mm = nc.tensor.matmul(o, u[:, H + h, :], DT[:, H + h, :], start=False, stop=True)
                mm.then_inc(s["o_ready"], 1)
            pe.wait_ge(s["osq_done"], 4)
            for b in range(4):
                nc.tensor.matmul(bank[4 + b][:, :], ones, sq[:, b * BANK:(b + 1) * BANK],
                                 start=True, stop=True).then_inc(s["osum_ready"], 1)
            wide(19, ya)
            wide(20, ya)
            pe.wait_ge(s["y_done"], 4)
            wide(21, oT)
            wide(22, oT)
            pe.wait_ge(s["mix_done"], 4)
            for t in range(NT):
                for n in range(2):
                    weights(23 + n)
                    for k in range(KT):
                        mm = nc.tensor.matmul(bank[4 + 2 * n + t][:, :], sgb[:, k, t * P:(t + 1) * P],
                                              slot(23 + n)[:, k, :], start=k == 0, stop=k == KT - 1)
                    mm.then_inc(s["wo_ready"], 1)
            norm_turn(1)
            i = 25
            for m in range(UPS):
                assert blocks[i][0] == "up"
                wide(i, hT)
                i += 1
                downs = [m - 2, m - 1] if m % 2 == 0 and m >= 2 else []
                for step in downs + ([m] if m == UPS - 1 else []):
                    if step != m - 1:
                        weights(i)
                    pe.wait_ge(s["act_done"], step + 1)
                    for t in range(NT):
                        for r in range(2):
                            f = 2 * step + r
                            for n in range(2):
                                row = 2 * (step % 2) + r
                                mm = nc.tensor.matmul(bank[4 + 2 * n + t][:, :], act_ffn[:, f, t * P:(t + 1) * P],
                                                      slot(i)[:, row, n * BANK:(n + 1) * BANK],
                                                      start=f == 0, stop=f == FT - 1)
                        if t == NT - 1 or step == UPS - 1:
                            mm.then_inc(s["down_ready"], 1)
                    if step != m - 2:
                        i += 1
                if m == UPS - 2:
                    pe.wait_ge(s["ada_used"], 12)
                    modulation()
            norm_turn(2)

            def by_token(i, cols):
                weights(i)
                for t in range(NT):
                    p = claim()
                    for k in range(KT):
                        mm = nc.tensor.matmul(bank[p % 4][:, 0:cols], hT[:, k, t * P:(t + 1) * P], slot(i)[:, k, :],
                                              start=k == 0, stop=k == KT - 1)
                    mm.then_inc(s["pair_ready"], 1)

            assert blocks[i][0] == "tok" and pairs[0] == PAIR0
            by_token(i, 440)
            i += 1
            by_token(i, BANK)
            wide(i + 1, hT)
            wide(i + 2, hT)
            by_token(i + 3, BANK)
            i += 4
            weights(i)
            p = claim()
            for k in range(KT):
                mm = nc.tensor.matmul(bank[p % 4][0:H, 0:S], slot(i)[:, k, :], hT[:, k, :], start=k == 0, stop=k == KT - 1)
            mm.then_inc(s["pair_ready"], 1)
            i += 1
            assert pairs[0] == P_IDX
            pe.wait_ge(s["rope_done"], 1)
            p = claim()
            for b in range(2):
                for t in range(NT):
                    mm = nc.tensor.transpose(bank[p % 4][:, b * S + t * P:b * S + (t + 1) * P],
                                             tokp[:, t, 144 + b * P:144 + (b + 1) * P], ident)
            mm.then_inc(s["pair_ready"], 1)
            p = claim()
            pe.wait_ge(s["lat_done"], 1)
            for b, src in enumerate((ikrep, latn)):
                for t in range(NT):
                    mm = nc.tensor.transpose(bank[p % 4][:, b * S + t * P:b * S + (t + 1) * P], src[:, t, :], ident)
            mm.then_inc(s["pair_ready"], 1)
            pe.wait_ge(s["rope_done"], 3)
            for b in range(2):
                p = claim()
                for f in range(2):
                    for t in range(NT):
                        c = (2 * b + f) * P
                        mm = nc.tensor.transpose(bank[p % 4][:, f * S + t * P:f * S + (t + 1) * P], qtok[:, t, c:c + P], ident)
                mm.then_inc(s["pair_ready"], 1)
            pe.wait_ge(s["small_in"], 32)
            pe.wait_ge(bank_free[(P_IDX + 1) % 4], (P_IDX + 1) // 4 + 1)
            for b in range(2):
                p = claim()
                for f in range(2):
                    h = 4 * b + 2 * f
                    nc.tensor.matmul(bank[p % 4][:, f * S:(f + 1) * S], wuk[:, h:h + 2, :], latT, start=True, stop=False,
                                     skip_group_check=True)
                    for t in range(NT):
                        mm = nc.tensor.matmul(bank[p % 4][:, f * S + t * P:f * S + (t + 1) * P], krp[:, t, :, :], ident,
                                              start=False, stop=t == NT - 1, skip_group_check=True)
                mm.then_inc(s["pair_ready"], 1)
            for t in range(NT):
                p = claim()
                nc.tensor.matmul(bank[p % 4][:, :], latT[:, t * P:(t + 1) * P], wuv, start=True,
                                 stop=True).then_inc(s["pair_ready"], 1)
            for t in range(NT):
                for j in range(4):
                    p = claim()
                    n = (t + 1) * P
                    for b in range(2):
                        mm = nc.tensor.matmul(bank[p % 4][:, b * S:b * S + n], iqT[IDX * j:IDX * (j + 1), b, t * P:(t + 1) * P],
                                              ikT[IDX * j:IDX * (j + 1), 0:n], start=True, stop=True)
                    mm.then_inc(s["pair_ready"], 1)
            pe.wait_ge(s["cum_done"], 1)
            for pr in range(4):
                p = claim()
                for f in range(2):
                    h = 2 * pr + f
                    mm = nc.tensor.matmul(bank[p % 4][:, f * S:(f + 1) * S], cst[0:H, C_SEL + h * P:C_SEL + (h + 1) * P],
                                          small[:, 6, :], start=True, stop=True)
                mm.then_inc(s["pair_ready"], 1)
            assert pairs[0] == P_ATT
            pe.wait_ge(bank_free[(P_VA + 1) % 4], (P_VA + 1) // 4 + 1)
            U = len(ATT_UNITS)
            for step in range(U + 2):
                if step < U:
                    br, t, pr = ATT_UNITS[step]
                    p = claim()
                    assert p == att_pair(0, step)
                    n = (t + 1) * P
                    for f, h in enumerate(att_heads(pr)):
                        o = bank[p % 4][:, f * S:f * S + n]
                        q, k = (qb, kb) if br else (qa, ka)
                        r = 64 * (h % 2)
                        mm = nc.tensor.matmul(o, q[r:r + 64, h // 2, t * P:(t + 1) * P], k[r:r + 64, h // 2, 0:n],
                                              start=True, stop=True)
                    mm.then_inc(s["pair_ready"], 1)
                if 1 <= step <= U:
                    br, t, pr = ATT_UNITS[step - 1]
                    p = claim()
                    pe.wait_ge(s["exp_done"], 2 * step)
                    assert p == att_pair(1, step - 1)
                    for f in range(2):
                        for b in range(t + 1):
                            mm = nc.tensor.transpose(bank[p % 4][:, (f * 2 + b) * P:(f * 2 + b + 1) * P],
                                                     lg[:, (step - 1) % 4, f, b * P:(b + 1) * P], ident)
                    mm.then_inc(s["pair_ready"], 1)
                if step >= 2:
                    br, t, pr = ATT_UNITS[step - 2]
                    turned = att_pair(1, step - 2)
                    pe.wait_ge(bank_free[turned % 4], turned // 4 + 1)
                    src = vb if br else va
                    for f, h in enumerate(att_heads(pr)):
                        for b in range(t + 1):
                            mm = nc.tensor.matmul(bank[4 + 2 * br + t][:, h * 64:(h + 1) * 64],
                                                  pT[:, (step - 2) % 4, (f * 2 + b) * P:(f * 2 + b + 1) * P],
                                                  src[:, b, h * 64:(h + 1) * 64], start=b == 0, stop=b == t)
                    mm.then_inc(s["pv_ready"], 1)
            norm_turn(3)
            for t in range(NT):
                for n in range(2):
                    weights(i + n)
                    for k in range(KT):
                        mm = nc.tensor.matmul(bank[4 + 2 * n + t][:, :], hT[:, k, t * P:(t + 1) * P], slot(i + n)[:, k, :],
                                              start=k == 0, stop=k == KT - 1)
                    mm.then_inc(s["wout_ready"], 1)
            pe.wait_ge(s["ffg_in"], 48)
            p = claim()
            nc.tensor.transpose(bank[p % 4][:, 0:P], keys, ident).then_inc(s["pair_ready"], 1)

            def tile_turn(t):
                pe.wait_ge(s["xn_done"], XN_PEER - NT + t + 1)
                for b in range(2):
                    for j in range(4):
                        k = 4 * b + j
                        mm = nc.tensor.transpose(bank[4 + 2 * b + t][:, j * P:(j + 1) * P], xn[:, t, k * P:(k + 1) * P], ident)
                    mm.then_inc(s["tr_done"], 1)
                pe.wait_ge(s["hTa"], 4 * NORM_TURNS + t + 1)
                pe.wait_ge(s["hTd"], 4 * NORM_TURNS + t + 1)

            def queries(t):
                for q in range(2):
                    weights(i + 2 + q)
                    p = claim()
                    for j in range(4):
                        for k in range(KT):
                            mm = nc.tensor.matmul(bank[p % 4][:, j * P:(j + 1) * P], slot(i + 2 + q)[:, k, j * P:(j + 1) * P],
                                                  hT[:, k, t * P:(t + 1) * P], start=k == 0, stop=k == KT - 1)
                    mm.then_inc(s["pair_ready"], 1)

            def key_scores(t):
                for q in range(2):
                    done = P_PQ + 6 * t + q
                    pe.wait_ge(bank_free[done % 4], done // 4 + 1)
                    for half in range(2):
                        p = claim()
                        r = slice(64 * half, 64 * half + 64)
                        for h in range(4 * q, 4 * q + 4):
                            mm = nc.tensor.matmul(bank[p % 4][:, (h % 4) * P:(h % 4 + 1) * P], qpT[r, h, t * P:(t + 1) * P],
                                                  keysT[r, :], start=True, stop=True)
                        mm.then_inc(s["pair_ready"], 1)

            tile_turn(0)
            queries(0)
            tile_turn(1)
            pe.wait_ge(bank_free[P_KEY % 4], P_KEY // 4 + 1)
            key_scores(0)
            queries(1)
            key_scores(1)
            assert pairs[0] == P_END and i + 4 == len(blocks)
            for t in range(NT):
                with pe.Fori(0, P // RING) as it:
                    for c in range(0, RING, ON_DVE):
                        turn = t * P // RING
                        pe.wait_ge(g_in[c], (it + (turn + 1)) * 16)
                        for b in range(2):
                            for j in range(4):
                                k = 4 * b + j
                                mm = nc.tensor.transpose(bank[4 + b][:, j * P:(j + 1) * P], gring[c][:, k * P:(k + 1) * P], ident)
                            mm.then_inc(s["firstT_ready"], 1)
                        pe.wait_ge(s["firstT_done"], (it + turn) * (2 * RING // ON_DVE) + 2 * (c // ON_DVE + 1))
                        pe.wait_ge(s["slot_free"], (it + (turn + 1)) * RING + c)
                        for k in range(KT):
                            mm = nc.tensor.matmul(bank[7][:, 0:P], firstT[:, k, :], hT[:, k, t * P:(t + 1) * P],
                                                  start=k == 0, stop=k == KT - 1)
                        mm.then_inc(s["product_ready"], 1)
            pe.wait_ge(s["zero_done"], 1)
            per = RING - RING // ON_DVE
            for t in range(NT):
                for n in range(2):
                    mm = nc.tensor.matmul(bank[4 + 2 * n + t][:, :], zero, xn[:, 0, 0:BANK], start=True, stop=False,
                                          skip_group_check=True)
                if t == 0:
                    mm.then_inc(s["pe_used"], per)
                with pe.Fori(0, P // RING) as it:
                    for c in range(RING):
                        if c % ON_DVE == ON_DVE - 1:
                            continue
                        q = c - c // ON_DVE
                        pe.wait_ge(g_in[c], (it + (NT * P // RING + t * P // RING + 1)) * 16)
                        pe.wait_ge(s["diag_done"], it * per + (t * P // RING * per + q + 1))
                        for n in range(2):
                            mm = nc.tensor.matmul(bank[4 + 2 * n + t][:, :], diag[:, q, :], gring[c][:, n * BANK:(n + 1) * BANK],
                                                  start=False, stop=False, skip_group_check=True)
                        mm.then_inc(s["pe_used"], 1)
                for n in range(2):
                    mm = nc.tensor.matmul(bank[4 + 2 * n + t][:, :], zero, xn[:, 0, 0:BANK], start=False, stop=True,
                                          skip_group_check=True)
                mm.then_inc(s["peer_ready"], 1)

        @block.scalar
        def _(act):
            chain = Chain(act, s["act_chain"])
            A_ = nc.scalar.activation

            def norm_stats(n, ready, count):
                act.wait_ge(s[ready], count)
                for t in range(NT):
                    if t:
                        chain.wait()
                    chain(A_(junk[:, :], x[:, t, :], ACT.Square, accum_out=stat[:, t:t + 1]))
                chain.wait()
                A_(stat[:, 4:6], stat[:, 0:2], ACT.Sqrt, scale=1.0 / D, bias=eps[:, 0:1]).then_inc(s["rt_done"], 1)

            def tile_stats(t, ready, each=2):
                act.wait_ge(s[ready], each * (t + 1))
                chain(A_(junk[:, :], x[:, t, :], ACT.Square, accum_out=stat[:, t:t + 1]))
                chain.wait()
                A_(stat[:, 4 + t:5 + t], stat[:, t:t + 1], ACT.Sqrt, scale=1.0 / D, bias=eps[:, 0:1]).then_inc(s["rt_done"], 1)

            def norm_evac(n, scale, bias=None):
                for b in range(2):
                    act.wait_ge(s["tr_done"], 4 * n + b + 1)
                    for f in range(2):
                        k = 2 * b + f
                        src = bank[4 + b][:, f * S:(f + 1) * S]
                        if bias is None:
                            A_(hT[:, k, :], src, ACT.Copy, scale=scale(k)).then_inc(s["hTa"], 1)
                        else:
                            A_(hT[:, k, :], src, ACT.Identity, scale=scale(k), bias=bias(k)).then_inc(s["hTa"], 1)

            act.wait_ge(s["eps_done"], 1)
            norm_stats(0, "x_in", 16)
            act.wait_ge(s["vt_done"], 1)
            norm_evac(0, lambda k: vcol("norm_mix_g", k))
            act.wait_ge(s["angle_done"], 1)
            A_(trig[:, 3, :], trig[:, 0, :], ACT.Sin).then_inc(s["sin_done"], 1)
            for p in range(12):
                act.wait_ge(bank_free[p % 4], p // 4 + 1)
                dst = (qT, kT, vT)[p // 4]
                f = 2 * (p % 4)
                A_(dst[:, f:f + 2, :], raw[:, p % 2, :, :], ACT.Silu).then_inc(s["silu_done"], 1)

            def pair(p):
                act.wait_ge(s["pair_ready"], p + 1)
                return bank[p % 4][:, :].rearrange("p (u s) -> p u s", u=2)

            def evac(p, dst, f, func):
                A_(dst[:, f:f + 2, :], pair(p), func).then_inc(bank_free[p % 4], 1)

            act.wait_ge(s["ab_dve"], 1)
            chain(A_(gate_par[:, 2:3], gate_par[:, 0:1], ACT.Exp))
            chain(A_(small[:, 7, :], bank[4][0:H, S:2 * S], ACT.Exp, scale=-1.0))
            chain(A_(small[:, 2, :], small[:, 1, :], ACT.Exp))
            chain.wait()
            A_(small[:, 3, :], small[:, 2, :], ACT.Ln, bias=1.0).then_inc(s["ab_act"], 1)
            for n in range(2):
                for p in range(12 + 2 * n, 14 + 2 * n):
                    evac(p, zT, 2 * (p - 12), ACT.Silu)
                if n == 0:
                    act.wait_ge(s["gt_done"], 1)
                    A_(egt[:, :], Gtok[:, 1, 0:H], ACT.Exp).then_inc(s["eg_done"], 1)
                for b in range(4):
                    act.wait_ge(s["sum_ready"], 4 * n + b + 1)
                    if n:
                        act.wait_ge(s["qk_done"], b + 1)
                    A_(rn[:, b * BANK:(b + 1) * BANK], bank[4 + b][:, :], ACT.Sqrt, scale=float(P) if n == 0 else 1.0,
                       bias=eps[:, 1:2] if n == 0 else eps[:, 0:1]).then_inc(s["sqrt_done"], 1)
            for p in range(16, 18):
                evac(p, ya, 2 * (p - 16), ACT.Copy)
            for b in range(4):
                act.wait_ge(s["row_ready"], b + 1)
                src = bank[4 + b][:, :].rearrange("p (h s) -> p h s", h=2)[:, :, P:S]
                A_(qd[:, 2 * b:2 * b + 2, :], src, ACT.Exp).then_inc(s["qd_done"], 1)
            for b in range(4):
                act.wait_ge(s["row_done"], b + 1)
                part = DT.rearrange("p (t h) c -> p t h c", t=NT)[:, :, 2 * b:2 * b + 2, :]
                A_(part, part, ACT.Exp).then_inc(s["dexp_done"], 1)
            for p in range(22, 24):
                evac(p, ya, 4 + 2 * (p - 22), ACT.Copy)
            for p in range(28, 36):
                evac(p, sga if p < 32 else sgb, 2 * ((p - 28) % 4), ACT.Sigmoid)
            for lv in range(1, LEVELS):
                for g in range(4):
                    act.wait_ge(s["lq_ready"], 4 * lv + g + 1)
                    A_(Qs[:, 4 * g:4 * g + 4, :], bank[4 + g][:, :], ACT.Copy).then_inc(s["lq_used"], 1)
            for g in range(4):
                act.wait_ge(s["u_ready"], g + 1)
                A_(u[:, 4 * g:4 * g + 4, :], bank[4 + g][:, :], ACT.Copy).then_inc(s["u_done"], 1)
            for g in range(2):
                act.wait_ge(s["w_ready"], g + 1)
                A_(wT[:, 4 * g:4 * g + 4, :], bank[g][:, :], ACT.Copy).then_inc(s["w_done"], 1)
            for g in range(2):
                act.wait_ge(s["s1_ready"], g + 1)
                A_(S1[:, 4 * g:4 * g + 4, :], bank[2 + g][:, :], ACT.Copy).then_inc(s["s1_done"], 1)
            for n in range(4):
                t, g = divmod(n, 2)
                act.wait_ge(s["o_ready"], n + 1)
                src = bank[4 + n][:, :].rearrange("p (h c) -> p h c", h=4)
                A_(oT[:, 4 * g:4 * g + 4, t * P:(t + 1) * P], src, ACT.Copy).then_inc(s["o_done"], 1)
                A_(sq.rearrange("p (h s) -> p h s", h=H)[:, 4 * g:4 * g + 4, t * P:(t + 1) * P], src,
                   ACT.Square).then_inc(s["osq_done"], 1)
            for b in range(4):
                act.wait_ge(s["osum_ready"], b + 1)
                A_(rn[:, b * BANK:(b + 1) * BANK], bank[4 + b][:, :], ACT.Sqrt, scale=1.0 / P,
                   bias=eps[:, 0:1]).then_inc(s["osqrt_done"], 1)
            for t in range(NT):
                tile_stats(t, "x1_done")
            norm_evac(1, lambda k: vcol("norm_ffn_g", k))
            A_(csil[:, :], vec[:, VEC["c_2"][0]:VEC["c_2"][0] + KT], ACT.Silu).then_inc(s["c_done"], 1)
            for m in range(UPS):
                if m == UPS - 1:
                    for r in range(8):
                        src = bank[(MOD0 + r) % 4][:, :]
                        act.wait_ge(s["pair_ready"], MOD0 + r + 1)
                        A_(modb[:, r // 2, (r % 2) * BANK:(r % 2 + 1) * BANK], src, ACT.Copy).then_inc(bank_free[(MOD0 + r) % 4], 1)
                act.wait_ge(bank_free[up_pair(m, 0) % 4], up_pair(m, 0) // 4 + 1)
                if m >= 2:
                    act.wait_ge(s["act_done"], m - 1)
                A_(sg[:, m % 2, :, :], raw2[:, (2 * m) % 4, :, :], ACT.Silu).then_inc(s["up_silu"], 1)
            for t in range(NT):
                tile_stats(t, "x2_done")
            for t in range(NT):
                tile_stats(t, "fin_done", 1)
            norm_evac(2, lambda k: modc[:, 1, k:k + 1], lambda k: modc[:, 0, k:k + 1])

            def copy_bank(p, dst, src, scale=1.0, func=ACT.Copy, free=True):
                act.wait_ge(s["pair_ready"], p + 1)
                ins = A_(dst, src, func, scale=scale)
                if free:
                    ins.then_inc(bank_free[p % 4], 1)
                else:
                    chain(ins)

            def by_head_pair(b, rows, width=S):
                return bank[b % 4][0:rows, :].rearrange("p (u s) -> p u s", u=2)

            for t in range(NT):
                copy_bank(PAIR0 + t, tokp[:, t, :], bank[(PAIR0 + t) % 4][:, 0:440])
            for t in range(NT):
                act.wait_ge(bank_free[(PAIR0 + t) % 4], (PAIR0 + t) // 4 + 1)
                chain.wait()
                chain(A_(junk[:, 0:P], tokp[:, t, 0:P], ACT.Square, accum_out=stat[:, 8 + t:9 + t]))
            chain.wait()
            A_(stat[:, 10:12], stat[:, 8:10], ACT.Sqrt, scale=1.0 / P, bias=eps[:, 0:1]).then_inc(s["lat_rt"], 1)
            for t in range(NT):
                p = PAIR0 + 2 + t
                copy_bank(p, qtok[:, t, :], bank[p % 4][:, :], scale=0.125)
            for pr in range(4):
                p = P_QB + pr
                copy_bank(p, (qb, kb)[pr // 2][:, 2 * (pr % 2):2 * (pr % 2) + 2, :], by_head_pair(p, P),
                          scale=0.125 if pr < 2 else 1.0)
            for t in range(NT):
                p = P_QB + 4 + t
                copy_bank(p, vb[:, t, :], bank[p % 4][:, :])
            act.wait_ge(s["fb_dve"], 1)
            chain(A_(small[:, 2, :], small[:, 1, :], ACT.Exp))
            chain.wait()
            A_(small[:, 3, :], small[:, 2, :], ACT.Ln, bias=1.0).then_inc(s["fb_act"], 1)
            copy_bank(P_IDX, iqT, bank[P_IDX % 4][:, :].rearrange("p (b s) -> p b s", b=2))
            p = P_IDX + 1
            copy_bank(p, ikT, bank[p % 4][:, 0:S], free=False)
            copy_bank(p, latT, bank[p % 4][:, S:2 * S], scale=vcol("g_kv_2", 0))
            for b in range(2):
                copy_bank(P_QR + b, qa[:, 2 * b:2 * b + 2, :], by_head_pair(P_QR + b, P))
            for b in range(2):
                copy_bank(P_KN + b, ka[:, 2 * b:2 * b + 2, :], by_head_pair(P_KN + b, P))
            for t in range(NT):
                copy_bank(P_VA + t, va[:, t, :], bank[(P_VA + t) % 4][:, :])
            for n in range(8):
                if n >= 4:
                    act.wait_ge(s["score_used"], n - 3)
                c = (n // 4 + 1) * P
                copy_bank(P_SC + n, rl[:, n % 4, :, 0:c], by_head_pair(P_SC + n, P)[:, :, 0:c], scale=IDX ** -0.5, func=ACT.Relu)
            for pr in range(4):
                copy_bank(P_ROW + pr, rows[:, 2 * pr:2 * pr + 2, :], by_head_pair(P_ROW + pr, P))
            for step in range(len(ATT_UNITS) + 1):
                if step < len(ATT_UNITS):
                    br, t, pr = ATT_UNITS[step]
                    act.wait_ge(s["lg_done"], step + 1)
                    for f, h in enumerate(att_heads(pr)):
                        part = lg[:, step % 4, f, 0:(t + 1) * P]
                        c = (2 * br + t) * H + h
                        A_(part, part, ACT.Exp, bias=amax[:, 2 * step + f:2 * step + f + 1],
                           accum_out=ssum[:, c:c + 1]).then_inc(s["exp_done"], 1)
                if step >= 1:
                    br, t, pr = ATT_UNITS[step - 1]
                    p = att_pair(1, step - 1)
                    act.wait_ge(s["pair_ready"], p + 1)
                    if step - 1 >= 4:
                        act.wait_ge(s["pv_ready"], step - 4)
                    src = bank[p % 4][:, :].rearrange("p (f b c) -> p f b c", f=2, b=2)[:, :, 0:t + 1, :]
                    dst = pT[:, (step - 1) % 4, :].rearrange("p (f b c) -> p f b c", f=2, b=2)[:, :, 0:t + 1, :]
                    A_(dst, src, ACT.Copy).then_inc(bank_free[p % 4], 1)
            for c in range(4):
                br, t = 1 - c // 2, c % 2
                act.wait_ge(s["orow_done"], c + 1)
                chain.wait()
                chain(A_(junk[:, 0:BANK], xn[:, t, br * BANK:(br + 1) * BANK], ACT.Square, accum_out=stat[:, 16 + c:17 + c]))
            chain.wait()
            A_(stat[:, 20:24], stat[:, 16:20], ACT.Sqrt, scale=1.0 / BANK, bias=eps[:, 0:1]).then_inc(s["oss_done"], 1)
            norm_evac(3, lambda k: vcol("g_out_a_2" if k < 4 else "g_out_b_2", k % 4))

            def tile_evac(t):
                act.wait_ge(s["tr_done"], 4 * NORM_TURNS + 2 * t + 1)
                A_(hT[:, 0:4, t * P:(t + 1) * P], bank[4 + t][:, :].rearrange("p (k c) -> p k c", k=4),
                   ACT.Copy).then_inc(s["hTa"], 1)

            def copy_queries(t):
                for q in range(2):
                    p = P_PQ + 6 * t + q
                    copy_bank(p, qpT[:, 4 * q:4 * q + 4, t * P:(t + 1) * P], bank[p % 4][:, :].rearrange("p (h c) -> p h c", h=4))

            def copy_scores(t):
                for n in range(4):
                    q, half = divmod(n, 2)
                    g, p = half * H + 4 * q, P_PQ + 6 * t + 2 + n
                    copy_bank(p, scr[:, t, g:g + 4, :], bank[p % 4][:, :].rearrange("p (h c) -> p h c", h=4))

            tile_stats(0, "x3_done")
            tile_evac(0)
            tile_stats(1, "x3_done")
            copy_queries(0)
            tile_evac(1)
            copy_scores(0)
            copy_queries(1)
            copy_scores(1)
            def soften(part):
                t, q = divmod(part, PER_TILE)
                mine = gsoft[:, t, q * PC:(q + 1) * PC]
                act.wait_ge(s["best_done"], part + 1)
                A_(mine, mine, ACT.Exp).then_inc(s["soft_done"], 1)

            soften(0)
            for part in range(PARTS):
                for half in range(2):
                    turn = part * TURNS + half * TURNS // 2
                    with act.Fori(0, TURNS // 2) as it:
                        for n in range(2 * RING // ON_DVE):
                            act.wait_ge(s["firstT_ready"], (it + turn) * (2 * RING // ON_DVE) + (n + 1))
                            b = n % 2
                            A_(firstT[:, 4 * b:4 * b + 4, :], bank[4 + b][:, :].rearrange("p (k c) -> p k c", k=4),
                               ACT.Copy).then_inc(s["firstT_done"], 1)
                    if half == 0 and part + 1 < PARTS:
                        soften(part + 1)
                if part % PER_TILE == PER_TILE - 1:
                    t = part // PER_TILE
                    act.wait_ge(s["score_out"], 1 + (t + 1) * P // RING)
                    A_(wgt[:, t, :], dots[:, t, :], ACT.Gelu).then_inc(s["gelu_done"], 1)
            per = RING - RING // ON_DVE
            for t in range(NT):
                act.wait_ge(s["weight_done"], t + 1)
                with act.Fori(0, P // RING) as it:
                    for c in range(RING):
                        if c % ON_DVE == ON_DVE - 1:
                            continue
                        q = c - c // ON_DVE
                        act.wait_ge(s["pe_used"], it * per + (t * P // RING * per + q + 1))
                        A_(diag[:, q, :], ident, ACT.Copy,
                           scale=wgt[:, t, bass.ds(it * RING + c, 1)]).then_inc(s["diag_done"], 1)
                tile_stats(t, "x_final")

        @block.vector
        def _(dve):
            chain = Chain(dve, s["dve_chain"])
            V = nc.vector

            def norm_rows(n):
                dve.wait_ge(s["rt_done"], n + 1)
                chain(V.reciprocal(stat[:, 6:8], stat[:, 4:6]))
                chain.wait()
                for t in range(NT):
                    V.tensor_scalar(xn[:, t, :], x[:, t, :], stat[:, 6 + t:7 + t], None, ALU.mult).then_inc(s["xn_done"], 1)

            def norm_evac(n, scale, bias=None):
                for b in range(2, 4):
                    dve.wait_ge(s["tr_done"], 4 * n + b + 1)
                    for f in range(2):
                        k = 2 * b + f
                        V.tensor_scalar(hT[:, k, :], bank[4 + b][:, f * S:(f + 1) * S], scale(k),
                                        bias(k) if bias else None, ALU.mult,
                                        ALU.add if bias else ALU.bypass).then_inc(s["hTd"], 1)

            def conv(dst, src, taps, name, f0, tiles, done):
                for j in range(taps - 1, -1, -1):
                    back = taps - 1 - j
                    if back:
                        chain.wait()
                    for n in range(2):
                        w = vcol(name, j * tiles + f0[n])
                        if back == 0:
                            ins = V.tensor_scalar(dst[:, n, :], src[:, n, :], w, None, ALU.mult)
                        else:
                            ins = V.scalar_tensor_tensor(out=dst[:, n, back:S], in0=src[:, n, 0:S - back], scalar=w,
                                                         in1=dst[:, n, back:S], op0=ALU.mult, op1=ALU.add)
                        if back == taps - 1 and n == 1 and done is not None:
                            ins.then_inc(done, 1)
                        else:
                            chain(ins)

            def pair(p):
                dve.wait_ge(s["pair_ready"], p + 1)
                return bank[p % 4][:, :].rearrange("p (u s) -> p u s", u=2)

            def sixteen(rows_of, top_v, top_i, each):
                for at in range(2):
                    for g in each:
                        chain(V.max(top_v(g)[:, 8 * at:8 * at + 8], rows_of(g)))
                    chain.wait()
                    for g in each:
                        chain(V.max_index(top_i(g)[:, 8 * at:8 * at + 8], top_v(g)[:, 8 * at:8 * at + 8], rows_of(g)))
                    if at == 0:
                        chain.wait()
                        for g in each:
                            chain(V.match_replace(rows_of(g), top_v(g)[:, 0:8], rows_of(g), FAR))
                    chain.wait()

            def route_halves(part):
                t, q = divmod(part, PER_TILE)
                h0 = HP * q
                groups = [half * H + h0 + i for half in range(2) for i in range(HP)]
                for half in range(2):
                    p = P_PQ + 6 * t + 2 + 2 * (h0 // 4) + half
                    dve.wait_ge(bank_free[p % 4], p // 4 + 1)
                sixteen(lambda g: scr[:, t, g, :], lambda g: top[:, t, g, :], lambda g: topi[:, t, g, :], groups)
                for half in range(2):
                    g = half * H + h0
                    chain(V.tensor_copy(topf[:, t, g:g + HP, :], topi[:, t, g:g + HP, :]))

            def route_sums(part):
                t, q = divmod(part, PER_TILE)
                h0 = HP * q
                cols = slice(q * PC, (q + 1) * PC)
                sums = cand[:, h0:h0 + HP, :].rearrange("p h (a b) -> p h a b", a=PK)
                chain(V.tensor_tensor(sums, top[:, t, h0:h0 + HP, :].unsqueeze(3).to_broadcast([P, HP, PK, PK]),
                                      top[:, t, H + h0:H + h0 + HP, :].unsqueeze(2).to_broadcast([P, HP, PK, PK]), ALU.add))
                chain.wait()
                b3 = best[:, t, :].rearrange("p (h k) -> p h k", h=H)
                p3 = bpos[:, t, :].rearrange("p (h k) -> p h k", h=H)
                sixteen(lambda h: cand[:, h, :], lambda h: b3[:, h, :], lambda h: p3[:, h, :], range(h0, h0 + HP))
                g3 = gsoft[:, t, cols].rearrange("p (h k) -> p h k", h=HP)
                b4 = best[:, t, cols].rearrange("p (h k) -> p h k", h=HP)
                V.tensor_tensor(g3, b4, b4[:, :, 0:1].to_broadcast([P, HP, PK]), ALU.subtract).then_inc(s["best_done"], 1)
                chain(V.tensor_scalar(babu[:, 0, t, cols], bpos[:, t, cols], 4, None, ALU.logical_shift_right))
                chain(V.tensor_scalar(babu[:, 1, t, cols], bpos[:, t, cols], 15, None, ALU.bitwise_and))
                chain.wait()
                chain(V.tensor_copy(babf[:, :, t, cols], babu[:, :, t, cols]))
                chain.wait()
                iota = cst[:, C_IOTA:C_IOTA + PK]
                flats = [hot[:, half * PC * PK:(half + 1) * PC * PK] for half in range(2)]
                for half in range(2):
                    chain(V.tensor_tensor(flats[half].rearrange("p (j a) -> p j a", a=PK),
                                          babf[:, half, t, cols].unsqueeze(2).to_broadcast([P, PC, PK]),
                                          iota.unsqueeze(1).to_broadcast([P, PC, PK]), ALU.is_equal))
                chain.wait()
                for half in range(2):
                    four = flats[half].rearrange("p (h k a) -> p h k a", h=HP, k=PK)
                    g = half * H + h0
                    chain(V.tensor_tensor(four, four, topf[:, t, g:g + HP, :].unsqueeze(2)
                                          .to_broadcast([P, HP, PK, PK]), ALU.mult))
                chain.wait()
                for half in range(2):
                    chain(V.tensor_reduce(pick[:, half, t, cols], flats[half].rearrange("p (j a) -> p j a", a=PK), AX.X, ALU.add))
                chain.wait()
                chain(V.scalar_tensor_tensor(out=pick[:, 0, t, cols], in0=pick[:, 0, t, cols], scalar=float(P),
                                             in1=pick[:, 1, t, cols], op0=ALU.mult, op1=ALU.add))
                chain.wait()
                V.tensor_copy(eid[:, t, cols], pick[:, 0, t, cols]).then_inc(s["eid_done"], 1)
                dve.wait_ge(s["soft_done"], part + 1)
                chain(V.tensor_reduce(stat[:, 32:32 + HP], g3, AX.X, ALU.add))
                chain.wait()
                chain(V.reciprocal(stat[:, 40:40 + HP], stat[:, 32:32 + HP]))
                chain.wait()
                ins = V.tensor_tensor(g3, g3, stat[:, 40:40 + HP].unsqueeze(2).to_broadcast([P, HP, PK]), ALU.mult)
                if part == 0:
                    ins.then_inc(s["slot_free"], RING)
                else:
                    chain(ins)
                    chain.wait()

            V.memset(eps[:, 0:1], EPS).then_inc(s["dve_chain"], 1)
            chain.n += 1
            V.memset(eps[:, 1:2], EPS * P).then_inc(s["eps_done"], 1)
            ang, turns = trig[:, 0, :].rearrange("p (t n) -> p t n", t=NT), trig[:, 1, :].rearrange("p (t n) -> p t n", t=NT)
            dve.wait_ge(s["vec_in"], 16 * VEC_DMAS)
            chain(V.tensor_copy(trig[:, 2, 0:NT], posi[:, :]))
            chain.wait()
            for n in range(12):
                width, i = (ROPE, n) if n < 8 else (IROPE, n - 8)
                inv = float(np.float32(THETA) ** np.float32(-2.0 * i / width))
                chain(V.tensor_scalar(ang[:, :, n], trig[:, 2, 0:NT], inv, None, ALU.mult))
            chain.wait()
            magic = 1.5 * 2.0 ** 23
            first, last = slice(0, 12), slice(12, 24)
            chain(V.tensor_scalar(turns[:, :, first], ang[:, :, first], 1.0 / sum(TWO_PI), magic, ALU.mult, ALU.add))
            chain.wait()
            chain(V.tensor_scalar(turns[:, :, first], turns[:, :, first], magic, None, ALU.subtract))
            chain.wait()
            for part in TWO_PI:
                chain(V.scalar_tensor_tensor(out=ang[:, :, first], in0=turns[:, :, first], scalar=-part, in1=ang[:, :, first],
                                             op0=ALU.mult, op1=ALU.add))
                chain.wait()
            chain(V.tensor_scalar(ang[:, :, last], ang[:, :, first], np.pi / 2, None, ALU.add))
            chain.wait()
            chain(V.tensor_scalar(turns[:, :, first], ang[:, :, last], np.pi, -2 * np.pi, ALU.is_gt, ALU.mult))
            chain.wait()
            chain(V.tensor_tensor(ang[:, :, last], ang[:, :, last], turns[:, :, first], ALU.add))
            chain.wait()
            V.tensor_scalar(trig[:, 0, :], trig[:, 0, :], 3.1415925, -3.1415925, ALU.min, ALU.max).then_inc(s["angle_done"], 1)
            norm_rows(0)
            dve.wait_ge(s["vt_ready"], 1)
            V.tensor_copy(vec[:, 0:VROWS], bank[0][:, 0:VROWS]).then_inc(s["vt_done"], 1)
            dve.wait_ge(s["vt_done"], 1)
            norm_evac(0, lambda k: vcol("norm_mix_g", k))
            for p in range(12):
                src = pair(p)
                if p >= 2:
                    dve.wait_ge(s["silu_done"], p - 1)
                conv(raw[:, p % 2, :, :], src, 4, "gdn_conv_w", (2 * p, 2 * p + 1), 24, bank_free[p % 4])
            dve.wait_ge(s["ab_ready"], 1)
            chain(V.tensor_scalar(small[:, 0, :], bank[4][0:H, 0:S], gate_par[:, 1:2], None, ALU.add))
            chain.wait()
            chain(V.tensor_scalar(small[:, 4, :], small[:, 0, :], -1.0, None, ALU.mult))
            chain.wait()
            V.tensor_tensor(small[:, 1, :], small[:, 0, :], small[:, 4, :], ALU.min).then_inc(s["ab_dve"], 1)
            dve.wait_ge(s["ab_act"], 1)
            chain(V.scalar_tensor_tensor(out=small[:, 5, :], in0=small[:, 0, :], scalar=0.0, in1=small[:, 3, :],
                                         op0=ALU.max, op1=ALU.add))
            chain(V.tensor_scalar(small[:, 7, :], small[:, 7, :], 1.0, None, ALU.add))
            chain.wait()
            chain(V.tensor_scalar(small[:, 5, :], small[:, 5, :], gate_par[:, 2:3], -1.0, ALU.mult, ALU.mult))
            chain(V.reciprocal(small[:, 7, :], small[:, 7, :]))
            chain.wait()
            for t in range(NT):
                ins = V.tensor_tensor_scan(small[:, 6, t * P:(t + 1) * P], ones[0:H, :], small[:, 5, t * P:(t + 1) * P],
                                           0.0, ALU.mult, ALU.add)
                if t == NT - 1:
                    ins.then_inc(s["gates_done"], 1)
                else:
                    chain(ins)
            dve.wait_ge(s["gt_ready"], 1)
            V.tensor_copy(Gtok[:, :, :], bank[4][:, 0:32].rearrange("p (t c) -> p t c", t=NT)).then_inc(s["gt_done"], 1)
            for n, buf in ((0, qT), (1, kT)):
                flat = buf.rearrange("p f s -> p (f s)")
                for b in range(4):
                    dve.wait_ge(s["sqrt_done"], 4 * n + b + 1)
                    c = slice(b * BANK, (b + 1) * BANK)
                    chain(V.reciprocal(rn[:, c], rn[:, c]))
                    chain.wait()
                    V.tensor_tensor(flat[:, c], flat[:, c], rn[:, c], ALU.mult).then_inc(s["qk_done"], 1)

            def convolved(p, half):
                for i in range(2):
                    src = pair(p + i)
                    part = ya[:, 4 * half + 2 * i:4 * half + 2 * i + 2, :]
                    dve.wait_ge(bank_free[(p + i - 2) % 4], (p + i - 2) // 4 + 1)
                    chain.wait()
                    V.tensor_tensor(t1, src, part, ALU.mult).then_inc(bank_free[(p + i) % 4], 1)
                    dve.wait_ge(bank_free[(p + i) % 4], (p + i) // 4 + 1)
                    f = 4 * half + 2 * i
                    conv(part, t1, 3, "conv_a_w", (f, f + 1), 8, None)
                chain.wait()
                for i in range(2):
                    src = pair(p + 2 + i)
                    part = ya[:, 4 * half + 2 * i:4 * half + 2 * i + 2, :]
                    V.tensor_tensor(part, src, part, ALU.mult).then_inc(bank_free[(p + 2 + i) % 4], 1)

            convolved(18, 0)
            for b in range(4):
                dve.wait_ge(s["qd_done"], b + 1)
                for f in range(2):
                    for t in range(NT):
                        ins = V.tensor_scalar(DT[:, t * H + 2 * b + f, :], bank[4 + b][:, f * S + t * P:f * S + (t + 1) * P],
                                              Gtok[:, t, 2 * b + f:2 * b + f + 1], 0.0, ALU.subtract, ALU.min)
                        if f == 1 and t == NT - 1:
                            ins.then_inc(s["row_done"], 1)
                        else:
                            chain(ins)
            mask = cst[:, C_STRICT:C_STRICT + P].unsqueeze(1).to_broadcast([P, NT * H, P])
            for b in range(4):
                dve.wait_ge(s["dexp_done"], b + 1)
                dve.wait_ge(s["row_ready"], 4 + b + 1)
                for t in range(NT):
                    c = slice(t * H + 2 * b, t * H + 2 * b + 2)
                    ins = V.tensor_tensor(LT[:, c, :], DT[:, c, :],
                                          bank[4 + b][:, :].rearrange("p (h s) -> p h s", h=2)[:, :, t * P:(t + 1) * P], ALU.mult)
                    if t == NT - 1:
                        ins.then_inc(s["row_done"], 1)
                    else:
                        chain(ins)
            dve.wait_ge(s["row_done"], 8)
            chain(V.tensor_tensor(LT, LT, mask, ALU.mult))
            dve.wait_ge(s["eg_done"], 1)
            chain(V.tensor_tensor(kbs[:, :], egt[:, :], Gtok[:, 1, H:2 * H], ALU.mult))
            dve.wait_ge(s["qd_done"], 4)
            for h0 in (0, 4):
                chain(V.tensor_tensor(qd[:, h0:h0 + 4, :], qd[:, h0:h0 + 4, :], qT[:, h0:h0 + 4, P:S], ALU.mult))
            convolved(24, 1)
            chain.wait()
            for n in range(8):
                g = n % 4
                t, h0 = g // 2, 4 * (g % 2)
                dve.wait_ge(s["tok_ready"], n + 1)
                src = bank[4 + g][:, :].rearrange("p (h c) -> p h c", h=4)
                if n < 4:
                    scale, dst = Gtok[:, t, H + h0:H + h0 + 4], Vb[:, 4 * g:4 * g + 4, :]
                elif t == 0:
                    scale, dst = DT[:, h0:h0 + 4, P - 1], Kd[:, h0:h0 + 4, :]
                else:
                    scale, dst = kbs[:, h0:h0 + 4], Kb[:, h0:h0 + 4, :]
                V.tensor_tensor(dst, src, scale.unsqueeze(2).to_broadcast([P, 4, P]), ALU.mult).then_inc(s["tok_done"], 1)
            dve.wait_ge(s["tok_done"], 6)
            incl = cst[:, C_INCL:C_INCL + P].unsqueeze(1).to_broadcast([P, NT * H, P])
            chain(V.tensor_tensor(DT, DT, incl, ALU.mult))
            chain.wait()
            for n in range(8):
                dve.wait_ge(s["kk_ready"], n + 1)
                g = n % 4
                buf = LT if n < 4 else DT
                V.tensor_tensor(buf[:, 4 * g:4 * g + 4, :], bank[4 + g][:, :].rearrange("p (h c) -> p h c", h=4),
                                buf[:, 4 * g:4 * g + 4, :], ALU.mult).then_inc(s["kk_done"], 1)
            eye = ident.unsqueeze(1).to_broadcast([P, 4, P])
            for lv in range(LEVELS):
                for g in range(4):
                    c = slice(4 * g, 4 * g + 4)
                    src = bank[4 + g][:, :].rearrange("p (h c) -> p h c", h=4)
                    srcT = bank[g][:, :].rearrange("p (h c) -> p h c", h=4)
                    if lv == 0:
                        dve.wait_ge(s["lq_ready"], g + 1)
                        chain(V.tensor_tensor(XT[:, c, :], eye, Loff[:, c, :], ALU.subtract))
                        V.tensor_tensor(X[:, c, :], eye, src, ALU.subtract).then_inc(s["x_done"], 1)
                    else:
                        dve.wait_ge(s["ld_ready"], 4 * (lv - 1) + g + 1)
                        if lv < LEVELS - 1:
                            chain(V.tensor_tensor(X[:, c, :], X[:, c, :], src, ALU.subtract))
                        V.tensor_tensor(XT[:, c, :], XT[:, c, :], srcT, ALU.subtract).then_inc(s["x_done"], 1)
            for g in range(2):
                dve.wait_ge(s["ws_ready"], g + 1)
                dve.wait_ge(s["u_done"], 3 + g)
                c = slice(H + 4 * g, H + 4 * g + 4)
                V.tensor_tensor(u[:, c, :], u[:, c, :], bank[g][:, :].rearrange("p (h c) -> p h c", h=4),
                                ALU.subtract).then_inc(s["vn_done"], 1)
            flat, zflat = oT.rearrange("p f s -> p (f s)"), zT.rearrange("p f s -> p (f s)")
            dve.wait_ge(s["o_done"], 4)
            for b in range(4):
                dve.wait_ge(s["osqrt_done"], b + 1)
                c = slice(b * BANK, (b + 1) * BANK)
                chain(V.reciprocal(rn[:, c], rn[:, c]))
                chain.wait()
                chain(V.scalar_tensor_tensor(out=rn[:, c], in0=rn[:, c], scalar=vcol("gdn_norm_g", 0), in1=zflat[:, c],
                                             op0=ALU.mult, op1=ALU.mult))
                chain.wait()
                V.tensor_tensor(flat[:, c], flat[:, c], rn[:, c], ALU.mult).then_inc(s["y_done"], 1)
            for p in range(36, 40):
                part = sga[:, 2 * (p - 36):2 * (p - 36) + 2, :]
                V.tensor_tensor(part, pair(p), part, ALU.mult).then_inc(bank_free[p % 4], 1)
            for p in range(40, 44):
                c = slice(2 * (p - 40), 2 * (p - 40) + 2)
                V.tensor_tensor(sgb[:, c, :], pair(p), sgb[:, c, :], ALU.mult).then_inc(bank_free[p % 4], 1)
                dve.wait_ge(bank_free[p % 4], p // 4 + 1)
                V.tensor_tensor(sgb[:, c, :], sgb[:, c, :], sga[:, c, :], ALU.add).then_inc(s["mix_done"], 1)

            def inverse_root(t, n):
                dve.wait_ge(s["rt_done"], n)
                chain(V.reciprocal(stat[:, 6 + t:7 + t], stat[:, 4 + t:5 + t]))
                chain.wait()

            def add_to_x(t, ready, count, done):
                for n in range(2):
                    dve.wait_ge(s[ready], count(n))
                    c = slice(n * BANK, (n + 1) * BANK)
                    V.tensor_tensor(x[:, t, c], x[:, t, c], bank[4 + 2 * n + t][:, :], ALU.add).then_inc(s[done], 1)

            for t in range(NT):
                add_to_x(t, "wo_ready", lambda n: 2 * t + n + 1, "x1_done")
            dve.wait_ge(s["x1_done"], 4)
            for t in range(NT):
                inverse_root(t, 2 + t)
                V.tensor_scalar(xn[:, t, :], x[:, t, :], stat[:, 6 + t:7 + t], None, ALU.mult).then_inc(s["xn_done"], 1)
            norm_evac(1, lambda k: vcol("norm_ffn_g", k))
            for m in range(UPS):
                for g in range(2):
                    p = up_pair(m, g)
                    src = pair(p)
                    if m >= 2:
                        dve.wait_ge(s["act_done"], m - 1)
                    conv(raw2[:, (2 * m + g) % 4, :, :], src, 3, "ffn_conv_w", (g * FT + 2 * m, g * FT + 2 * m + 1), 2 * FT,
                         bank_free[p % 4])
                for j in ADA_AT.get(m, ()):
                    dve.wait_ge(s["c_done"], 1)
                    dve.wait_ge(s["acc_in"], 16)
                    dve.wait_ge(ada_in[j % 2], 16 * (j // 2 + 1))
                    part = acc[:, j * BANK:(j + 1) * BANK]
                    for k in range(KT):
                        ins = V.scalar_tensor_tensor(out=part, in0=ada[j % 2][:, k, :], scalar=csil[:, k:k + 1], in1=part,
                                                     op0=ALU.mult, op1=ALU.add)
                        if k == KT - 1:
                            ins.then_inc(s["ada_used"], 1)
                        else:
                            chain(ins)
                            chain.wait()
                if m == UPS - 2:
                    dve.wait_ge(s["pair_ready"], MOD0 + 9)
                    src = bank[(MOD0 + 8) % 4]
                    chain(V.tensor_copy(modc[:, 0, :], src[:, 0:KT]))
                    c = VEC["g_mix_2"][0]
                    V.scalar_tensor_tensor(out=modc[:, 1, :], in0=src[:, KT:2 * KT], scalar=1.0, in1=vec[:, c:c + KT],
                                           op0=ALU.add, op1=ALU.mult).then_inc(bank_free[(MOD0 + 8) % 4], 1)
            for t in range(NT):
                add_to_x(t, "down_ready", lambda n: UPS + t, "x2_done")
            dve.wait_ge(s["x2_done"], 4)
            dve.wait_ge(s["row_in"], 16)
            for t in range(NT):
                inverse_root(t, 4 + t)
                V.scalar_tensor_tensor(out=x[:, t, :], in0=x[:, t, :], scalar=stat[:, 6 + t:7 + t], in1=nfg,
                                       op0=ALU.mult, op1=ALU.mult).then_inc(s["fin_done"], 1)
            dve.wait_ge(s["fin_done"], NT)
            for t in range(NT):
                inverse_root(t, 6 + t)
                V.tensor_scalar(xn[:, t, :], x[:, t, :], stat[:, 6 + t:7 + t], None, ALU.mult).then_inc(s["xn_done"], 1)
            norm_evac(2, lambda k: modc[:, 1, k:k + 1], lambda k: modc[:, 0, k:k + 1])
            dve.wait_ge(s["act_done"], UPS)
            chain(V.memset(region(29, NT * P), 0.0))
            for t in range(NT):
                dve.wait_ge(bank_free[(PAIR0 + t) % 4], (PAIR0 + t) // 4 + 1)
            dve.wait_ge(s["sin_done"], 1)
            tri = trig[:, 3, :].rearrange("p (t n) -> p t n", t=NT)

            def rotate(buf, heads, half, at):
                x1, x2 = buf[:, :, :, 0:half], buf[:, :, :, half:2 * half]
                shape = [P, NT, heads, half]
                sin = tri[:, :, at:at + half].unsqueeze(2).to_broadcast(shape)
                cos = tri[:, :, 12 + at:12 + at + half].unsqueeze(2).to_broadcast(shape)
                tmp = [rtmp[:, m, 0:NT * heads * half].rearrange("p (t h n) -> p t h n", t=NT, h=heads) for m in range(4)]
                chain.wait()
                for m, (a, b) in enumerate(((x1, cos), (x2, sin), (x2, cos), (x1, sin))):
                    chain(V.tensor_tensor(tmp[m], a, b, ALU.mult))
                chain.wait()
                chain(V.tensor_tensor(x1, tmp[0], tmp[1], ALU.subtract))
                V.tensor_tensor(x2, tmp[2], tmp[3], ALU.add).then_inc(s["rope_done"], 1)

            rotate(tokp[:, :, 144:432].rearrange("p t (h n) -> p t h n", n=IDX), H + 1, IROPE // 2, 8)
            dve.wait_ge(s["rope_done"], 1)
            rotate(tokp[:, :, P:P + ROPE].unsqueeze(2), 1, ROPE // 2, 0)
            dve.wait_ge(s["rope_done"], 2)
            chain(V.tensor_copy(krp[:, :, :, 0:ROPE], tokp[:, :, P:P + ROPE].unsqueeze(2).to_broadcast([P, NT, 2, ROPE])))
            chain(V.tensor_copy(ikrep.rearrange("p t (r n) -> p t r n", r=4),
                                tokp[:, :, 400:432].unsqueeze(2).to_broadcast([P, NT, 4, IDX])))
            chain(V.tensor_scalar(iws[:, :, :], tokp[:, :, 432:440], H ** -0.5, None, ALU.mult))
            dve.wait_ge(s["lat_rt"], 1)
            chain(V.reciprocal(stat[:, 12:14], stat[:, 10:12]))
            chain.wait()
            for t in range(NT):
                ins = V.tensor_scalar(latn[:, t, :], tokp[:, t, 0:P], stat[:, 12 + t:13 + t], None, ALU.mult)
                if t:
                    ins.then_inc(s["lat_done"], 1)
                else:
                    chain(ins)
            for t in range(NT):
                dve.wait_ge(bank_free[(PAIR0 + 2 + t) % 4], (PAIR0 + 2 + t) // 4 + 1)
            rotate(qtok.rearrange("p t (h n) -> p t h n", h=H), H, ROPE // 2, 0)
            p = P_FB
            dve.wait_ge(s["pair_ready"], p + 1)
            V.tensor_scalar(small[:, 0, :], bank[p % 4][0:H, 0:S], gate_par[:, 3:4], -1.0, ALU.add,
                            ALU.mult).then_inc(bank_free[p % 4], 1)
            dve.wait_ge(bank_free[p % 4], p // 4 + 1)
            chain(V.tensor_scalar(small[:, 4, :], small[:, 0, :], -1.0, None, ALU.mult))
            chain.wait()
            V.tensor_tensor(small[:, 1, :], small[:, 0, :], small[:, 4, :], ALU.min).then_inc(s["fb_dve"], 1)
            dve.wait_ge(s["fb_act"], 1)
            chain(V.scalar_tensor_tensor(out=small[:, 5, :], in0=small[:, 0, :], scalar=0.0, in1=small[:, 3, :],
                                         op0=ALU.max, op1=ALU.add))
            chain.wait()
            for t in range(NT):
                ins = V.tensor_tensor_scan(small[:, 6, t * P:(t + 1) * P], ones[0:H, :], small[:, 5, t * P:(t + 1) * P],
                                           0.0 if t == 0 else small[:, 6, P - 1:P], ALU.mult, ALU.add)
                if t:
                    ins.then_inc(s["cum_done"], 1)
                else:
                    chain(ins)
                    chain.wait()
            for n in range(8):
                t, j = divmod(n, 4)
                p = P_SC + n
                dve.wait_ge(bank_free[p % 4], p // 4 + 1)
                part = score[:, t, 0:(t + 1) * P]
                for b in range(2):
                    src = rl[:, n % 4, b, 0:(t + 1) * P]
                    w = iws[:, t, 4 * b + j:4 * b + j + 1]
                    if j == 0 and b == 0:
                        ins = V.tensor_scalar(part, src, w, None, ALU.mult)
                    else:
                        ins = V.scalar_tensor_tensor(out=part, in0=src, scalar=w, in1=part, op0=ALU.mult, op1=ALU.add)
                    if b:
                        ins.then_inc(s["score_used"], 1)
                        dve.wait_ge(s["score_used"], n + 1)
                    else:
                        chain(ins)
                        chain.wait()
            neg = [cst[:, C_NEG + t * S:C_NEG + t * S + (t + 1) * P] for t in range(NT)]
            for t in range(NT):
                chain(V.tensor_tensor(work[:, t, 0:(t + 1) * P], score[:, t, 0:(t + 1) * P], neg[t], ALU.add))
            chain.wait()

            def take_round():
                for t in range(NT):
                    chain(V.max(top8[:, t, :], work[:, t, 0:(t + 1) * P]))
                chain.wait()
                for t in range(NT):
                    part = work[:, t, 0:(t + 1) * P]
                    chain(V.match_replace(part, top8[:, t, :], part, FAR))
                chain.wait()

            U = len(ATT_UNITS)
            for n in range(U):
                br, t, pr = ATT_UNITS[n]
                c = (t + 1) * P
                if n == U // 2:
                    for tt in range(NT):
                        chain(V.tensor_scalar(negA[:, tt, 0:(tt + 1) * P], work[:, tt, 0:(tt + 1) * P], -2e38, BIG,
                                              ALU.is_le, ALU.mult))
                    chain.wait()
                    for tt in range(NT):
                        part = negA[:, tt, 0:(tt + 1) * P]
                        chain(V.scalar_tensor_tensor(out=part, in0=part, scalar=-BIG, in1=neg[tt], op0=ALU.add, op1=ALU.add))
                    chain.wait()
                p = att_pair(0, n)
                dve.wait_ge(s["pair_ready"], p + 1)
                if n >= 4:
                    dve.wait_ge(s["pair_ready"], att_pair(1, n - 4) + 1)
                src = bank[p % 4][:, :].rearrange("p (u s) -> p u s", u=2)[:, :, 0:c]
                dst = lg[:, n % 4, :, 0:c]
                if br:
                    h = att_heads(pr)[0]
                    dve.wait_ge(bank_free[(P_ROW + 3) % 4], (P_ROW + 3) // 4 + 1)
                    V.tensor_tensor(dst, src, rows[:, h:h + 3:2, 0:c], ALU.add).then_inc(bank_free[p % 4], 1)
                    dve.wait_ge(bank_free[p % 4], p // 4 + 1)
                    chain(V.tensor_tensor(dst, dst, neg[t].unsqueeze(1).to_broadcast([P, 2, c]), ALU.add))
                else:
                    V.tensor_tensor(dst, src, negA[:, t, 0:c].unsqueeze(1).to_broadcast([P, 2, c]),
                                    ALU.add).then_inc(bank_free[p % 4], 1)
                    dve.wait_ge(bank_free[p % 4], p // 4 + 1)
                chain.wait()
                V.tensor_reduce(amax[:, 2 * n:2 * n + 2], dst, AX.X, ALU.max, negate=True).then_inc(s["lg_done"], 1)
                if n < TAKE // 8:
                    take_round()
            for c in range(4):
                br, t = 1 - c // 2, c % 2
                dve.wait_ge(s["exp_done"], 8 * (c + 1))
                dve.wait_ge(s["pv_ready"], 4 * (c + 1))
                b = 2 * br + t
                chain(V.reciprocal(ssum[:, 32 + b * H:32 + (b + 1) * H], ssum[:, b * H:(b + 1) * H]))
                chain.wait()
                V.tensor_tensor(xn[:, t, br * BANK:(br + 1) * BANK].rearrange("p (h n) -> p h n", h=H),
                                bank[4 + b][:, :].rearrange("p (h n) -> p h n", h=H),
                                ssum[:, 32 + b * H:32 + (b + 1) * H].unsqueeze(2).to_broadcast([P, H, 64]),
                                ALU.mult).then_inc(s["orow_done"], 1)
            dve.wait_ge(s["oss_done"], 1)
            chain(V.reciprocal(stat[:, 24:28], stat[:, 20:24]))
            chain.wait()
            for c in range(4):
                br, t = 1 - c // 2, c % 2
                part = xn[:, t, br * BANK:(br + 1) * BANK]
                V.tensor_scalar(part, part, stat[:, 24 + c:25 + c], None, ALU.mult).then_inc(s["xn_done"], 1)
            norm_evac(3, lambda k: vcol("g_out_a_2" if k < 4 else "g_out_b_2", k % 4))

            def gated_add(t, ready, counts, gate, done, more=None):
                for n in range(2):
                    c = slice(n * BANK, (n + 1) * BANK)
                    tmp = lg[:, 2 * n + t, :, :].rearrange("p u s -> p (u s)")
                    dve.wait_ge(s[ready], counts[n])
                    src = bank[4 + 2 * n + t][:, :]
                    if more is not None:
                        chain(V.tensor_tensor(tmp, src, more[:, t, c], ALU.add))
                        chain.wait()
                        src = tmp
                    chain(V.tensor_tensor(tmp, src, modb[:, gate, c], ALU.mult))
                    chain.wait()
                    V.tensor_tensor(x[:, t, c], x[:, t, c], tmp, ALU.add).then_inc(s[done], 1)

            dve.wait_ge(s["ffg_in"], 48)
            chain(V.scalar_tensor_tensor(out=modb[:, 2, :], in0=modb[:, 2, :], scalar=1.0, in1=ffg, op0=ALU.add, op1=ALU.mult))
            for t in range(NT):
                gated_add(t, "wout_ready", (2 * t + 1, 2 * t + 2), 0, "x3_done")
                dve.wait_ge(s["x3_done"], 2 * t + 2)
                inverse_root(t, 8 + t)
                for n in range(2):
                    c = slice(n * BANK, (n + 1) * BANK)
                    chain(V.scalar_tensor_tensor(out=xn[:, t, c], in0=x[:, t, c], scalar=stat[:, 6 + t:7 + t],
                                                 in1=modb[:, 2, c], op0=ALU.mult, op1=ALU.mult))
                chain.wait()
                V.tensor_tensor(xn[:, t, :], xn[:, t, :], modb[:, 1, :], ALU.add).then_inc(s["xn_done"], 1)
                if t == 0:
                    dve.wait_ge(s["pair_ready"], P_KEY + 1)
                    V.tensor_copy(keysT[:, :], bank[P_KEY % 4][:, 0:P]).then_inc(bank_free[P_KEY % 4], 1)
                dve.wait_ge(s["tr_done"], 4 * NORM_TURNS + 2 * t + 2)
                V.tensor_copy(hT[:, 4:8, t * P:(t + 1) * P],
                              bank[6 + t][:, :].rearrange("p (k c) -> p k c", k=4)).then_inc(s["hTd"], 1)
            V.memset(dotst[:, :], 0.0).then_inc(s["score_out"], 1)

            def dots_of(part, half):
                t, q = divmod(part, PER_TILE)
                first = part * TURNS + half * TURNS // 2
                at = first % (PER_TILE * TURNS) * RING
                with dve.Fori(0, TURNS // 2) as it:
                    for c in (c0 + n for c0 in range(0, RING, ON_DVE) for n in (1, 2, 3, 0)):
                        if c == 1:
                            dve.wait_ge(s["score_out"], it + (first + 1))
                        if c % ON_DVE:
                            dve.wait_ge(g_in[c], (it + (first + 1)) * 16)
                            V.tensor_tensor_reduce(gring[c], gring[c], xn[:, t, :], 1.0, 0.0, ALU.mult, ALU.add,
                                                   dotst[:, c:c + 1]).then_inc(s["slot_free"], 1)
                        else:
                            dve.wait_ge(s["product_ready"], (it + first) * (RING // ON_DVE) + (c // ON_DVE + 1))
                            V.tensor_tensor_reduce(gring[c][:, 0:P], bank[7][:, 0:P], ident, 1.0, 0.0, ALU.mult, ALU.add,
                                                   dotst[:, c:c + 1]).then_inc(s["slot_free"], 1)
                    dve.wait_ge(s["slot_free"], (it + (first + 2)) * RING)
                    V.tensor_copy(dots[:, t, bass.ds(it * RING + at, RING)], dotst[:, :]).then_inc(s["score_out"], 1)

            def expert_weights(t):
                dve.wait_ge(s["gelu_done"], t + 1)
                V.tensor_tensor(wgt[:, t, :], wgt[:, t, :], gsoft[:, t, :], ALU.mult).then_inc(s["weight_done"], 1)

            route_halves(0)
            route_sums(0)
            for part in range(PARTS):
                if part + 1 < PARTS:
                    route_halves(part + 1)
                else:
                    expert_weights(0)
                    chain(V.memset(vacc[:, 0, :], 0.0))
                    V.memset(vacc[:, 1, :], 0.0).then_inc(s["dve_used"], RING // ON_DVE)
                dots_of(part, 0)
                if part + 1 < PARTS:
                    route_sums(part + 1)
                dots_of(part, 1)
            expert_weights(1)
            for t in range(NT):
                dve.wait_ge(s["weight_done"], t + 1)
                with dve.Fori(0, P // RING) as it:
                    for d in range(RING // ON_DVE):
                        c = ON_DVE * d + ON_DVE - 1
                        dve.wait_ge(g_in[c], (it + (NT * P // RING + t * P // RING + 1)) * 16)
                        dve.wait_ge(s["dve_used"], (it + (t * P // RING + 1)) * (RING // ON_DVE) + d)
                        V.scalar_tensor_tensor(out=vacc[:, t, :], in0=gring[c], scalar=wgt[:, t, bass.ds(it * RING + c, 1)],
                                               in1=vacc[:, t, :], op0=ALU.mult, op1=ALU.add).then_inc(s["dve_used"], 1)
                dve.wait_ge(s["dve_used"], ((t + 1) * P // RING + 1) * (RING // ON_DVE))
                gated_add(t, "peer_ready", (t + 1, t + 1), 3, "x_final", vacc)
                dve.wait_ge(s["x_final"], 2 * t + 2)
                inverse_root(t, 10 + t)
                dve.wait_ge(s["fin_row_in"], 16)
                V.scalar_tensor_tensor(out=x[:, t, :], in0=x[:, t, :], scalar=stat[:, 6 + t:7 + t], in1=ffg,
                                       op0=ALU.mult, op1=ALU.mult).then_inc(s["final_done"], 1)

        @block.gpsimd
        def _(pool):
            G = nc.gpsimd
            G.memset(tick[:, :], 0.0).then_inc(s["pool_chain"], 1)
            pool.wait_ge(s["pool_chain"], 1)
            for n, buf in ((0, qT), (1, kT)):
                pool.wait_ge(s["silu_done"], 4 * (n + 1))
                if n:
                    pool.wait_ge(s["sum_ready"], 4)
                G.tensor_tensor(sq, buf.rearrange("p f s -> p (f s)"), buf.rearrange("p f s -> p (f s)"),
                                ALU.mult).then_inc(s["sq_done"], 1)
            for lv in range(LEVELS):
                off = cst[:, C_OFF + lv * P:C_OFF + (lv + 1) * P].unsqueeze(1).to_broadcast([P, 4, P])
                for g in range(4):
                    if lv == 0:
                        pool.wait_ge(s["kk_done"], g + 1)
                        pool.wait_ge(bank_free[3], 9)
                        pool.wait_ge(bank_free[2], 9)
                    elif lv == 1:
                        pool.wait_ge(s["x_done"], g + 1)
                    else:
                        pool.wait_ge(s["lq_ready"], 4 * (lv - 1) + g + 1)
                    G.tensor_tensor(Loff[:, 4 * g:4 * g + 4, :], LT[:, 4 * g:4 * g + 4, :], off,
                                    ALU.mult).then_inc(s["loff_done"], 1)
            pool.wait_ge(s["mix_done"], 4)
            G.memset(region(106, H * 64), 0.0).then_inc(s["wuk_zero"], 1)
            G.memset(acc, 0.0).then_inc(s["acc_zero"], 1)
            pool.wait_ge(s["acc_zero"], 1)
            pool.dma_start(acc[0:1, :], A["b_ada_2"]).then_inc(s["acc_in"], 16)
            for m in range(UPS):
                p = up_pair(m, 1)
                pool.wait_ge(s["up_silu"], m + 1)
                pool.wait_ge(bank_free[p % 4], p // 4 + 1)
                G.tensor_tensor(act_ffn[:, 2 * m:2 * m + 2, :], sg[:, m % 2, :, :], raw2[:, (2 * m + 1) % 4, :, :],
                                ALU.mult).then_inc(s["act_done"], 1)

            per = RING - RING // ON_DVE
            for phase, name in ((0, "peer_u_2"), (1, "peer_v_2")):
                for part in range(PARTS):
                    t, q = divmod(part, PER_TILE)
                    base = part * TURNS
                    pool.wait_ge(s["eid_done"], part + 1)
                    if phase == 0 and part == 0:
                        pool.wait_ge(s["pair_ready"], P_PQ + 6 + 2)
                        G.memset(zero, 0.0).then_inc(s["zero_done"], 1)
                    with pool.Fori(0, TURNS) as it:
                        for d in range(RING // ON_DVE):
                            c0 = d * ON_DVE
                            if phase == 0:
                                pool.wait_ge(s["slot_free"], (it + base) * RING + (c0 + ON_DVE))
                            else:
                                pool.wait_ge(s["slot_free"], NT * P + c0 + ON_DVE)
                                pool.wait_ge(s["dve_used"], (it + base) * (RING // ON_DVE) + (d + 1))
                                pool.wait_ge(s["pe_used"], (it + base) * per + (d + 1) * (ON_DVE - 1))
                            G.tensor_tensor(tick[:, 0:1], tick[:, 2:3], tick[:, 2:3], ALU.add)
                            G.tensor_copy(eidst[:, c0:c0 + ON_DVE],
                                          eid[:, t, bass.ds(it * RING + (q * PC + c0), ON_DVE)]).then_inc(s["ids_ready"], 1)
                            pool.wait_ge(s["ids_ready"], (it + (phase * NT * P // RING + base)) * (RING // ON_DVE) + (d + 1))
                            G.tensor_tensor(tick[:, 1:2], tick[:, 2:3], tick[:, 2:3], ALU.add)
                            for c in range(c0, c0 + ON_DVE):
                                G.indirect_dma_start(gring[c], None, A[name][0],
                                                     bass.IndirectOffsetOnAxis(ap=eidst[:, c:c + 1],
                                                                               axis=0)).then_inc(g_in[c], 16)


def kernel(**inputs):
    import concourse.bacc as bacc
    from concourse.bass_utils import run_bass_kernel_spmd as run

    nc = bacc.Bacc("TRN2", target_bir_lowering=False, num_devices=1)
    arrays, args = {}, {}
    for name in INPUTS:
        a = np.ascontiguousarray(inputs[name])
        arrays[f"in_{name}"] = a
        args[name] = nc.dram_tensor(f"in_{name}", a.shape, mybir.dt.from_np(a.dtype), kind="ExternalInput").ap()
    arrays["consts"] = constant_table()
    args["consts"] = nc.dram_tensor("consts", (P, C_END), F32, kind="ExternalInput").ap()
    out = nc.dram_tensor("out", (1, S, D), F32, kind="ExternalOutput").ap()
    program(nc, args, out)
    return run(nc, [arrays], core_ids=[0]).results[0]["out"]
```
